# Optimizing a Trainium2 kernel written in Bass

```python
import math
import jax, jax.numpy as jnp
from jax import lax
import numpy as np

D_MODEL = 1024
BATCH = 1
SEQ = 512
DEPTH = 2
DEC_BATCH = 1
DEC_SEQ = 64
PAST_LEN = 512

CHUNK = 64
N_A_LAYERS = DEPTH // 2
N_B_LAYERS = DEPTH - N_A_LAYERS
MLSTM_HEADS = 8
MLSTM_QK_DIM = D_MODEL // (2 * MLSTM_HEADS)
MLSTM_V_DIM = D_MODEL // MLSTM_HEADS
MLSTM_IN_WIDTH = 2 * MLSTM_HEADS * MLSTM_QK_DIM + MLSTM_HEADS * MLSTM_V_DIM + D_MODEL + 2 * MLSTM_HEADS
GATE_SOFTCAP = 15.0
SB_HEADS = 8
SB_HEAD_DIM = D_MODEL // SB_HEADS
SB_QUERY_BLOCK = 128
D_FF = 2816
CONV_WIDTH = 3
NORM_EPS = 1e-6
NEG_BIG = -1e30

kernel_name = "yoco_mlstm_stickbreaking_convffn_step"

def rmsnorm(x, g):
    x32 = x.astype(jnp.float32)
    y = x32 * lax.rsqrt(jnp.mean(x32 * x32, axis=-1, keepdims=True) + NORM_EPS)
    return (y * g.astype(jnp.float32)).astype(x.dtype)

def softcap(x, cap):
    return cap * jnp.tanh(x / cap)

def mlstm_scan(q, k, v, li, lf, c0, n0, m0):
    B, H, T, DK = q.shape
    DV = v.shape[-1]
    L = min(CHUNK, T)
    NC = T // L

    def to_chunks(a):
        return jnp.moveaxis(a.reshape(a.shape[:2] + (NC, L) + a.shape[3:]), 2, 0)

    xs = tuple(to_chunks(a.astype(jnp.float32)) for a in (q, k, v, li, lf))
    causal = jnp.tril(jnp.ones((L, L), dtype=bool))

    def step(carry, chunk):
        c, n, m = carry
        qc, kc, vc, lic, lfc = chunk
        b = jnp.cumsum(lfc, axis=-1)
        log_d = jnp.where(causal, b[..., :, None] - b[..., None, :] + lic[..., None, :], -jnp.inf)
        m_inter = b + m[..., None]
        m_t = jnp.maximum(m_inter, jnp.max(log_d, axis=-1))
        w_inter = jnp.exp(m_inter - m_t)
        s = jnp.einsum('bhtd,bhsd->bhts', qc, kc) * jnp.exp(log_d - m_t[..., None])
        num = jnp.einsum('bhts,bhsv->bhtv', s, vc) + w_inter[..., None] * jnp.einsum('bhtd,bhdv->bhtv', qc, c)
        den = jnp.sum(s, axis=-1) + w_inter * jnp.einsum('bhtd,bhd->bht', qc, n)
        h = num / jnp.maximum(jnp.abs(den), jnp.exp(-m_t))[..., None]
        m_new = m_t[..., -1]
        decay = jnp.exp(b[..., -1] + m - m_new)
        w_in = jnp.exp(b[..., -1:] - b + lic - m_new[..., None])
        c_new = decay[..., None, None] * c + jnp.einsum('bhsd,bhsv->bhdv', kc * w_in[..., None], vc)
        n_new = decay[..., None] * n + jnp.einsum('bhsd,bhs->bhd', kc, w_in)
        return (c_new, n_new, m_new), h

    carry0 = (c0.astype(jnp.float32), n0.astype(jnp.float32), m0.astype(jnp.float32))
    (c, n, m), h = lax.scan(step, carry0, xs)
    h = jnp.moveaxis(h, 0, 2).reshape(B, H, T, DV)
    return h, c, n, m

def mlstm_layer(x, g_norm, w_in, b_gates, g_out, w_out, c0, n0, m0):
    B, T, _ = x.shape
    H, DK, DV = MLSTM_HEADS, MLSTM_QK_DIM, MLSTM_V_DIM
    proj = rmsnorm(x, g_norm) @ w_in
    s1 = H * DK
    s2 = 2 * H * DK
    s3 = s2 + H * DV
    s4 = s3 + D_MODEL
    q = proj[..., :s1].reshape(B, T, H, DK).transpose(0, 2, 1, 3) * (DK ** -0.5)
    k = proj[..., s1:s2].reshape(B, T, H, DK).transpose(0, 2, 1, 3)
    v = proj[..., s2:s3].reshape(B, T, H, DV).transpose(0, 2, 1, 3)
    o = proj[..., s3:s4]
    gates = softcap(proj[..., s4:].astype(jnp.float32) + b_gates.astype(jnp.float32), GATE_SOFTCAP)
    li = gates[..., :H].transpose(0, 2, 1)
    lf = jax.nn.log_sigmoid(gates[..., H:]).transpose(0, 2, 1)
    h, c, n, m = mlstm_scan(q, k, v, li, lf, c0, n0, m0)
    h = h.transpose(0, 2, 1, 3)
    h = h * lax.rsqrt(jnp.mean(h * h, axis=-1, keepdims=True) + NORM_EPS)
    h = h.reshape(B, T, D_MODEL) * g_out.astype(jnp.float32) * jax.nn.sigmoid(o.astype(jnp.float32))
    out = h.astype(x.dtype) @ w_out
    return out, c.astype(x.dtype), n.astype(x.dtype), m.astype(x.dtype)

def stick_breaking_attention(q, k, v):
    B, Tq, H, DH = q.shape
    Tk = k.shape[1]
    QB = min(SB_QUERY_BLOCK, Tq)
    NB = Tq // QB
    q_blocks = jnp.moveaxis(q.astype(jnp.float32).reshape(B, NB, QB, H, DH), 1, 0)
    k32 = k.astype(jnp.float32)
    v32 = v.astype(jnp.float32)
    k_pos = jnp.arange(Tk)
    scale = DH ** -0.5

    def block(args):
        q_blk, i = args
        q_pos = (Tk - Tq) + i * QB + jnp.arange(QB)
        z = jnp.einsum('bqhd,bkhd->bhqk', q_blk, k32) * scale
        earlier = k_pos[None, :] < q_pos[:, None]
        log_beta = jnp.where(earlier, jax.nn.log_sigmoid(z), -jnp.inf)
        log_keep = jnp.where(earlier, jax.nn.log_sigmoid(-z), 0.0)
        log_keep_after = lax.cumsum(log_keep, axis=3, reverse=True) - log_keep
        a = jnp.exp(log_beta + log_keep_after)
        return jnp.einsum('bhqk,bkhd->bqhd', a, v32)

    out = lax.map(block, (q_blocks, jnp.arange(NB)))
    return jnp.moveaxis(out, 0, 1).reshape(B, Tq, H, DH)

def conv_ffn(x, g_norm, w_up, w_conv, b_conv, w_down, prev):
    T = x.shape[1]
    u = rmsnorm(x, g_norm) @ w_up
    a = u[..., :D_FF]
    val = u[..., D_FF:]
    ext = jnp.concatenate([prev.astype(a.dtype), a], axis=1)
    acc = b_conv
    for i in range(CONV_WIDTH):
        acc = acc + w_conv[i] * ext[:, i:i + T]
    h = jax.nn.gelu(acc.astype(jnp.float32)) * val.astype(jnp.float32)
    return h.astype(x.dtype) @ w_down, ext[:, -(CONV_WIDTH - 1):]

def trunk(x, c0, n0, m0, conv0, k_past, v_past,
          g_mix_norm, w_mlstm_in, b_mlstm_gates, g_mlstm_out, w_mlstm_out,
          g_kv_norm, w_kv, w_sb_q, w_sb_o,
          g_ffn_norm, w_ffn_up, w_ffn_conv, b_ffn_conv, w_ffn_down, g_final):
    B, T, _ = x.shape
    new_c, new_n, new_m, new_conv = [], [], [], []
    k_all = v_all = k_new = v_new = None
    for l in range(DEPTH):
        if l < N_A_LAYERS:
            a, c, n, m = mlstm_layer(x, g_mix_norm[l], w_mlstm_in[l], b_mlstm_gates[l], g_mlstm_out[l],
                                     w_mlstm_out[l], c0[l], n0[l], m0[l])
            x = x + a
            new_c.append(c)
            new_n.append(n)
            new_m.append(m)
        else:
            j = l - N_A_LAYERS
            q = (rmsnorm(x, g_mix_norm[l]) @ w_sb_q[j]).reshape(B, T, SB_HEADS, SB_HEAD_DIM)
            att = stick_breaking_attention(q, k_all, v_all).reshape(B, T, D_MODEL).astype(x.dtype)
            x = x + att @ w_sb_o[j]
        f, conv_rows = conv_ffn(x, g_ffn_norm[l], w_ffn_up[l], w_ffn_conv[l], b_ffn_conv[l], w_ffn_down[l], conv0[l])
        x = x + f
        new_conv.append(conv_rows)
        if l == N_A_LAYERS - 1:
            kv = rmsnorm(x, g_kv_norm) @ w_kv
            k_new = kv[..., :D_MODEL].reshape(B, T, SB_HEADS, SB_HEAD_DIM)
            v_new = kv[..., D_MODEL:].reshape(B, T, SB_HEADS, SB_HEAD_DIM)
            k_all = jnp.concatenate([k_past.astype(x.dtype), k_new], axis=1)
            v_all = jnp.concatenate([v_past.astype(x.dtype), v_new], axis=1)
    y = rmsnorm(x, g_final)
    return y, jnp.stack(new_c), jnp.stack(new_n), jnp.stack(new_m), jnp.stack(new_conv), k_new, v_new

def setup_inputs(seed: int = 0) -> dict:
    key = jax.random.key(seed)
    ks = jax.random.split(key, 24)
    f32 = jnp.float32
    D = D_MODEL

    def nrm(k, shape, scale):
        return jax.random.normal(k, shape, f32) * scale

    b_gates = jnp.concatenate([nrm(ks[10], (N_A_LAYERS, MLSTM_HEADS), 0.1),
                               3.0 + nrm(ks[11], (N_A_LAYERS, MLSTM_HEADS), 0.1)], axis=-1)
    return {
        'x_prompt': nrm(ks[0], (BATCH, SEQ, D), 1.0),
        'x_sample': nrm(ks[1], (DEC_BATCH, DEC_SEQ, D), 1.0),
        'cache_k': nrm(ks[2], (DEC_BATCH, PAST_LEN, SB_HEADS, SB_HEAD_DIM), 1.0),
        'cache_v': nrm(ks[3], (DEC_BATCH, PAST_LEN, SB_HEADS, SB_HEAD_DIM), 1.0),
        'state_mlstm_c': nrm(ks[4], (N_A_LAYERS, DEC_BATCH, MLSTM_HEADS, MLSTM_QK_DIM, MLSTM_V_DIM), 0.1),
        'state_mlstm_n': nrm(ks[5], (N_A_LAYERS, DEC_BATCH, MLSTM_HEADS, MLSTM_QK_DIM), 0.1),
        'state_mlstm_m': nrm(ks[6], (N_A_LAYERS, DEC_BATCH, MLSTM_HEADS), 0.5),
        'state_ffn_conv': nrm(ks[7], (DEPTH, DEC_BATCH, CONV_WIDTH - 1, D_FF), 1.0),
        'g_mix_norm': 1.0 + nrm(ks[8], (DEPTH, D), 0.02),
        'w_mlstm_in': nrm(ks[9], (N_A_LAYERS, D, MLSTM_IN_WIDTH), D ** -0.5),
        'b_mlstm_gates': b_gates,
        'g_mlstm_out': 1.0 + nrm(ks[12], (N_A_LAYERS, D), 0.02),
        'w_mlstm_out': nrm(ks[13], (N_A_LAYERS, D, D), D ** -0.5),
        'g_kv_norm': 1.0 + nrm(ks[14], (D,), 0.02),
        'w_kv': nrm(ks[15], (D, 2 * D), D ** -0.5),
        'w_sb_q': nrm(ks[16], (N_B_LAYERS, D, D), D ** -0.5),
        'w_sb_o': nrm(ks[17], (N_B_LAYERS, D, D), D ** -0.5),
        'g_ffn_norm': 1.0 + nrm(ks[18], (DEPTH, D), 0.02),
        'w_ffn_up': nrm(ks[19], (DEPTH, D, 2 * D_FF), D ** -0.5),
        'w_ffn_conv': nrm(ks[20], (DEPTH, CONV_WIDTH, D_FF), CONV_WIDTH ** -0.5),
        'b_ffn_conv': nrm(ks[21], (DEPTH, D_FF), 0.02),
        'w_ffn_down': nrm(ks[22], (DEPTH, D_FF, D), D_FF ** -0.5),
        'g_final': 1.0 + nrm(ks[23], (D,), 0.02),
    }

def reference(x_prompt, x_sample, cache_k, cache_v, state_mlstm_c, state_mlstm_n, state_mlstm_m, state_ffn_conv,
              g_mix_norm, w_mlstm_in, b_mlstm_gates, g_mlstm_out, w_mlstm_out,
              g_kv_norm, w_kv, w_sb_q, w_sb_o,
              g_ffn_norm, w_ffn_up, w_ffn_conv, b_ffn_conv, w_ffn_down, g_final):
    weights = (g_mix_norm, w_mlstm_in, b_mlstm_gates, g_mlstm_out, w_mlstm_out,
               g_kv_norm, w_kv, w_sb_q, w_sb_o,
               g_ffn_norm, w_ffn_up, w_ffn_conv, b_ffn_conv, w_ffn_down, g_final)
    bp = x_prompt.shape[0]
    dt = x_prompt.dtype
    p_c0 = jnp.zeros((N_A_LAYERS, bp, MLSTM_HEADS, MLSTM_QK_DIM, MLSTM_V_DIM), dt)
    p_n0 = jnp.zeros((N_A_LAYERS, bp, MLSTM_HEADS, MLSTM_QK_DIM), dt)
    p_m0 = jnp.full((N_A_LAYERS, bp, MLSTM_HEADS), NEG_BIG, jnp.float32)
    p_conv0 = jnp.zeros((DEPTH, bp, CONV_WIDTH - 1, D_FF), dt)
    p_kv0 = jnp.zeros((bp, 0, SB_HEADS, SB_HEAD_DIM), dt)
    y_prompt, p_mlstm_c, p_mlstm_n, p_mlstm_m, p_ffn_conv, p_k, p_v = trunk(
        x_prompt, p_c0, p_n0, p_m0, p_conv0, p_kv0, p_kv0, *weights)
    y_sample, s_mlstm_c, s_mlstm_n, s_mlstm_m, s_ffn_conv, s_k, s_v = trunk(
        x_sample, state_mlstm_c, state_mlstm_n, state_mlstm_m, state_ffn_conv, cache_k, cache_v, *weights)
    return (y_prompt, y_sample,
            p_mlstm_c, p_mlstm_n, p_mlstm_m, p_ffn_conv, p_k, p_v,
            s_mlstm_c, s_mlstm_n, s_mlstm_m, s_ffn_conv, s_k, s_v)


_drawn_inputs = setup_inputs


def setup_inputs(seed=0):
    import zlib

    import numpy as np

    out = dict(_drawn_inputs(seed))
    spreads = {}
    factors = {'state_mlstm_n': 64.0,
     'state_mlstm_m': 3.321,
     'g_mlstm_out': 4.769,
     'g_kv_norm': 8.239,
     'b_ffn_conv': 4.036,
     'g_final': 24.25,
     'cache_k': 10.779,
     'g_ffn_norm': 2.749}
    for name, (base, spread) in spreads.items():
        noise = np.random.default_rng([zlib.crc32(name.encode()), seed]).standard_normal(out[name].shape)
        drawn = base * np.exp(spread * noise) if base else spread * noise
        out[name] = __import__('jax').numpy.asarray(drawn.astype(out[name].dtype))
    for name, factor in factors.items():
        out[name] = (out[name] * factor).astype(out[name].dtype)
    return out
```

```python
import concourse.bass as bass
from concourse import mybir
from contextlib import ExitStack

P = 128
D = 1024
TP, TS = 512, 64
T = TP + TS
HALF = T // 2
BANK = 512
KT = D // P
H = 8
DK, DV = D // (2 * H), D // H
DH = D // H
PAST = 512
FF = 2816
FT = FF // P
THIRDS = (8, 8, 6)
EPS = 1e-6
CAP = 15.0
NEG_BIG = -1e30
PAIRS = H // 2
IN_BLOCKS, IN_USES = 6, 16
G_LI, G_LF, G_ROWS = 0, 32, 40

C_MIX, C_OUT, C_KV, C_FFN, C_FIN, C_N0 = 0, 16, 24, 32, 48, 56
C_CONV, CONV_ROWS = 60, 88
C_PREV = C_CONV + 2 * CONV_ROWS
C_ALL = C_PREV + 2 * 44

ACT = mybir.ActivationFunctionType
ALU = mybir.AluOpType
F32 = mybir.dt.float32
F32R = mybir.dt.float32r


class Pos:

    def __init__(self, const, i=None, stride=0):
        self.const, self.i, self.stride = const, i, stride

    def at(self, k=0, times=1):
        n = (self.const + k) * times
        return n if self.i is None else self.i * (self.stride * times) + n

    def plus(self, k):
        return Pos(self.const + k, self.i, self.stride)

    @property
    def slot(self):
        return self.const % 2

    def turn(self, k=0, times=1):
        n = (self.const // 2 + k) * times
        return n if self.i is None else self.i * (self.stride // 2 * times) + n


class Chain:

    def __init__(self, eng, sem):
        self.eng, self.sem, self.n, self.i, self.k = eng, sem, 0, None, 0

    def link(self, ins):
        ins.then_inc(self.sem, 1)
        self.n += 1
        self.eng.wait_ge(self.sem, self.n if self.i is None else self.i * self.k + self.n)

    def enter(self, i, k):
        self.i, self.k, self.start = i, k, self.n

    def leave(self, turns):
        assert self.n - self.start == self.k, (self.n - self.start, self.k)
        self.i, self.n = None, self.start + self.k * turns


def plan():
    b, u = 0, 1 + KT + 1
    at = {"in": (b, u)}
    b, u = b + IN_BLOCKS * PAIRS, u + IN_USES * PAIRS
    at["out"] = (b, u)
    b, u = b + KT, u + KT
    for layer in range(2):
        for t, n in enumerate(THIRDS):
            at["up", layer, t] = (b, u)
            b, u = b + 2 * n, u + 2 * n
            at["down", layer, t] = (b, u)
            b, u = b + KT, u + KT
        if layer == 0:
            at["kvq"] = (b, u)
            b, u = b + 3 * H, u + 7 * H
            at["o"] = (b, u)
            b, u = b + KT, u + KT
    at["end"] = (b, u)
    return at


AT = plan()
LAST_BLOCK = AT["end"][0]


def trunk_kernel(nc, A, O):
    ctx = ExitStack()
    with ctx:
        def sb(name, shape, dt=F32, scope=ctx):
            return scope.enter_context(nc.sbuf_tensor(name, shape, dt))

        def sem(name):
            return ctx.enter_context(nc.semaphore(name))

        def fb(x):
            return x.bitcast(F32)

        x = sb("x", [P, KT, T])
        xh, xl = sb("xh", [P, KT, T], F32R), sb("xl", [P, KT, T], F32R)
        hh, hl = sb("hh", [P, KT, T], F32R), sb("hl", [P, KT, T], F32R)
        wraw = sb("wraw", [P, 2, KT, P])
        whi, wlo = sb("whi", [P, 2, KT, P], F32R), sb("wlo", [P, 2, KT, P], F32R)
        ident, ones = sb("ident", [P, P]), sb("ones", [P, P])
        mean_d, mean_v = sb("mean_d", [P, P]), sb("mean_v", [P, P])
        neg_tri, neg_one = sb("neg_tri", [P, P]), sb("neg_one", [P, P])
        eps = sb("eps", [P, 1])
        par = sb("par", [P, C_ALL])
        out_half = sb("out_half", [P, KT])
        rstd, rstd_q = sb("rstd", [P, T]), sb("rstd_q", [P, T])
        nr = sb("nr", [P, T])
        ssq, sq = sb("ssq", [P, T]), sb("sq", [P, 2, T])
        conv_rows = sb("conv_rows", [P, 2, 2, 2, FT])
        tails = sb("tails", [88, 3, P])
        gm = sb("gm", [H, 2])
        nall = sb("nall", [P, 2, PAIRS])

        setup = ExitStack()
        xtok = sb("xtok", [P, 5, D], scope=setup)
        prow = sb("prow", [P, 4, P], scope=setup)
        graw = sb("graw", [P, KT, G_ROWS], scope=setup)
        ghi, glo = sb("ghi", [P, KT, G_ROWS], F32R, setup), sb("glo", [P, KT, G_ROWS], F32R, setup)
        setup.close()

        ml = ExitStack()
        ga, gwin = sb("ga", [H, T], scope=ml), sb("gwin", [H, T], scope=ml)
        gates = ExitStack()
        gth = sb("gth", [G_ROWS, T], scope=gates)
        nlf, ones8 = sb("nlf", [H, T], scope=gates), sb("ones8", [H, T], scope=gates)
        nb, gg = sb("nb", [H, T], scope=gates), sb("gg", [H, T], scope=gates)
        gneg, gem = sb("gneg", [H, T], scope=gates), sb("gem", [H, T], scope=gates)
        gates.close()
        dec, sdec = sb("dec", [P, 4, BANK], scope=ml), sb("sdec", [P, 4, BANK], scope=ml)
        num, nsq = sb("num", [P, T], scope=ml), sb("nsq", [P, T], scope=ml)
        dn, inv = sb("dn", [P, T], scope=ml), sb("inv", [P, T], scope=ml)
        hm = sb("hm", [P, T], scope=ml)
        gwint, gbias = sb("gwint", [H, TS], scope=ml), sb("gbias", [G_ROWS, 1], scope=ml)
        gm0 = sb("gm0", [H, 1], scope=ml)
        kf, qf = sb("kf", [P, 5 * P], scope=ml), sb("qf", [P, T], scope=ml)
        vf = sb("vf", [P, 2, T], scope=ml)
        qw = sb("qw", [P, TS], scope=ml)
        vtok = sb("vtok", [P, 5, 2 * DV + 1], scope=ml)
        kw = sb("kw", [P, 5, P], scope=ml)
        acol, wcol = sb("acol", [P, 5, 2], scope=ml), sb("wcol", [P, 5, 2], scope=ml)
        gb, eb = sb("gb", [P, 2, T], scope=ml), sb("eb", [P, 2, T], scope=ml)
        wint = sb("wint", [P, TS], scope=ml)
        c0s, n0b = sb("c0s", [P, DV], scope=ml), sb("n0b", [P, P], scope=ml)
        tg = sb("tg", [P, 2, T], scope=ml)
        cst = sb("cst", [P, 2, DV], scope=ml)
        ml.close()

        late = ExitStack()
        ext = sb("ext", [P, T + 4], scope=late)
        ffn = ExitStack()
        acc, gel = sb("acc", [P, T + 2], scope=ffn), sb("gel", [P, T], scope=ffn)
        val, hid = sb("val", [P, T], scope=ffn), sb("hid", [P, T], scope=ffn)
        ffn.close()
        att = ExitStack()
        za, sp = sb("za", [P, 4, BANK], scope=att), sb("sp", [P, 4, BANK], scope=att)
        prob = sb("prob", [P, 4, BANK], scope=att)
        kfa, qfa = sb("kfa", [P, 2, 5 * P], scope=att), sb("qfa", [P, 2, T], scope=att)
        vfa = sb("vfa", [P, T], scope=att)
        ktok, vta = sb("ktok", [P, 5, P], scope=att), sb("vta", [P, 2, 5, P], scope=att)
        ck, cv = sb("ck", [P, 2, 4, P], scope=att), sb("cv", [P, 2, 4, P], scope=att)
        ckT = sb("ckT", [P, 2, PAST], scope=att)
        att.close()
        yT = sb("yT", [P, KT, T], scope=late)
        ytok = sb("ytok", [P, 2, D], scope=late)
        late.close()

        slots = [ctx.enter_context(nc.psum_tensor(f"slot{s}", [P, 2 * BANK], F32)) for s in range(2)]
        Z = ctx.enter_context(nc.psum_tensor("Z", [P, 4 * BANK], F32))
        Zb = Z[:, :].rearrange("p (b n) -> p b n", b=4)
        rows_d = nc.dram_tensor("gate_rows", (2 * H, T), F32).ap()
        wint_d = nc.dram_tensor("gate_winter", (H, TS), F32).ap()

        w_loaded = [sem("w_loaded0"), sem("w_loaded1")]
        w_gained, w_high = sem("w_gained"), sem("w_high")
        w_split = sem("w_split")
        out_full = sem("out_full")
        out_free = [sem("out_free0"), sem("out_free1")]
        chain_dve, chain_act, chain_pool = sem("chain_dve"), sem("chain_act"), sem("chain_pool")
        passed = sem("passed")
        consts_ready, pads_ready = sem("consts_ready"), sem("pads_ready")
        prow_loaded, x_loaded, g_loaded = sem("prow_loaded"), sem("x_loaded"), sem("g_loaded")
        gbias_loaded = sem("gbias_loaded")
        g_high, g_split = sem("g_high"), sem("g_split")
        x_high, x_split = sem("x_high"), sem("x_split")
        x_square, x_summed = sem("x_square"), sem("x_summed")
        ms_full, rstd_raw, rstd_ready = sem("ms_full"), sem("rstd_raw"), sem("rstd_ready")
        h_high, h_split = sem("h_high"), sem("h_split")
        gate_dve, gate_act = sem("gate_dve"), sem("gate_act")
        rows_stored, pair_loaded = sem("rows_stored"), sem("pair_loaded")
        gT_full, cols_ready, qw_ready = sem("gT_full"), sem("cols_ready"), sem("qw_ready")
        dec_exp, dec_ready = sem("dec_exp"), sem("dec_ready")
        s_full, sdec_ready = sem("s_full"), sem("sdec_ready")
        num_squared, den_ready, den_squared = sem("num_squared"), sem("den_ready"), sem("den_squared")
        inv_ready, tanh_ready, hm_ready = sem("inv_ready"), sem("tanh_ready"), sem("hm_ready")
        state_stored = sem("state_stored")
        prev_ready, conv_ready = sem("prev_ready"), sem("conv_ready")
        gelu_ready, hid_ready, rows_taken = sem("gelu_ready"), sem("hid_ready"), sem("rows_taken")
        ck_loaded = [sem("ck_loaded0"), sem("ck_loaded1")]
        cv_loaded = [sem("cv_loaded0"), sem("cv_loaded1")]
        z_full, z_log, z_kept = sem("z_full"), sem("z_log"), sem("z_kept")
        sp_raw, sp_ready = sem("sp_raw"), sem("sp_ready")
        log_full, log_ready = sem("log_full"), sem("log_ready")
        prob_raw, prob_ready = sem("prob_raw"), sem("prob_ready")
        k_stored = sem("k_stored")
        v_stored = [sem("v_stored0"), sem("v_stored1")]
        y_ready, y_stored, tail_stored = sem("y_ready"), [sem("y_stored0"), sem("y_stored1")], sem("tail_stored")

        def by_rows(w):
            return w.rearrange("(k p) n -> p k n", p=P)

        w_in, w_out = by_rows(A["w_mlstm_in"][0]), by_rows(A["w_mlstm_out"][0])
        w_kv, w_q, w_o = by_rows(A["w_kv"]), by_rows(A["w_sb_q"][0]), by_rows(A["w_sb_o"][0])
        w_up = [by_rows(A["w_ffn_up"][l]) for l in range(2)]
        w_down = [by_rows(A["w_ffn_down"][l]) for l in range(2)]
        K_COL, V_COL = H * DK, 2 * H * DK
        O_COL = V_COL + H * DV
        G_COL = O_COL + D

        def ds(start, size=1):
            return slice(start, start + size) if isinstance(start, int) else bass.ds(start, size)

        def fb(ap):
            return ap.bitcast(F32)

        def tile_of(buf, m):
            return buf[:, ds(m), :].rearrange("p a n -> p (a n)")

        def slot(u):
            return slots[u.slot]

        def halves(u):
            return slot(u)[:, :].rearrange("p (b n) -> p b n", b=2)[:, :, 0:HALF]

        def two(ap):
            return ap.rearrange("p (b n) -> p b n", b=2)

        def apart(eng):
            eng.sem_inc(passed, 1)

        def full(eng, u):
            eng.wait_ge(out_full, u.at(1))

        def copied(eng, u):
            eng.wait_ge(out_free[u.slot], u.turn(2))

        def stepwise(eng, n, body, peel=0):
            turns = n // 2 - peel
            with eng.Fori(0, turns) as i:
                for e in range(2):
                    body(Pos(e, i, 2))
            for s in range(2 * turns, n):
                body(Pos(s))

        def counted(chain, eng, n, body, per_step, peel=0):
            turns = n // 2 - peel
            with eng.Fori(0, turns) as i:
                chain.enter(i, 2 * per_step)
                for e in range(2):
                    body(Pos(e, i, 2))
            chain.leave(turns)
            for s in range(2 * turns, n):
                body(Pos(s))

        def scaled(phase, which, s, per=1, k=0):
            return Pos(AT[phase][which] + s.const * per + k, s.i, s.stride * per)

        def B(phase, s, per=1, k=0):
            return scaled(phase, 0, s, per, k)

        def U(phase, s, per=1, k=0):
            return scaled(phase, 1, s, per, k)

        def in_pos(i):
            return Pos(AT["in"][0], i, IN_BLOCKS), Pos(AT["in"][1], i, IN_USES)

        (U_K, U_V0, U_V1, U_Q, U_KT, U_V0T, U_V1T, U_O0, U_NUM0, U_DEN0, U_O1, U_SSQ0, U_NUM1, U_DEN1, U_STATE,
         U_SSQ1) = range(IN_USES)
        U_O, U_NUM, U_DEN, U_SSQ = (U_O0, U_O1), (U_NUM0, U_NUM1), (U_DEN0, U_DEN1), (U_SSQ0, U_SSQ1)

        S_K, S_V, S_KT, S_Q, S_VT, S_AV = range(6)

        def att_use(s, which):
            return Pos(AT["kvq"][1] - (1 if s.const else 0) + 7 * s.const + which, s.i, 7 * s.stride)

        def s_ckT(s):
            return att_use(s, 6 if s.const else 5)

        def s_av(c):
            if c.i is None and c.const == H - 1:
                return Pos(AT["o"][1] - 1)
            return att_use(c.plus(1), S_AV)

        def att_steps(eng, body):
            body(Pos(0), None)
            with eng.Fori(0, PAIRS - 1) as i:
                body(Pos(1, i, 2), Pos(0, i, 2))
                body(Pos(2, i, 2), Pos(1, i, 2))
            body(Pos(H - 1), Pos(H - 2))
            body(None, Pos(H - 1))

        block = ctx.enter_context(nc.Block())

        @block.sync
        def _(dma):
            def load_block(b, src, nk=KT):
                dma.wait_ge(w_split, b.at(1))
                apart(dma)
                dma.dma_start(wraw[:, b.slot, 0:nk, :], src).then_inc(w_loaded[b.slot], 16)

            for at, name, dims, n in ((C_MIX, "g_mix_norm", "l (t p) -> (l t) p", 16),
                                      (C_OUT, "g_mlstm_out", "l (t p) -> (l t) p", 8),
                                      (C_KV, "g_kv_norm", "(t p) -> t p", 8),
                                      (C_FFN, "g_ffn_norm", "l (t p) -> (l t) p", 16),
                                      (C_FIN, "g_final", "(t p) -> t p", 8)):
                dma.dma_start(prow[at:at + n, 0, :], A[name].rearrange(dims, p=P)).then_inc(prow_loaded, 16)
            dma.dma_start(prow[C_N0:C_N0 + PAIRS, 0, :],
                          A["state_mlstm_n"].rearrange("l b (i e) k -> (l b i) (e k)", e=2)).then_inc(prow_loaded, 16)
            for l in range(2):
                dma.dma_start(prow[0:3 * FT, 1 + l, :],
                              A["w_ffn_conv"][l].rearrange("i (t p) -> (i t) p", p=P)).then_inc(prow_loaded, 16)
                dma.dma_start(prow[3 * FT:4 * FT, 1 + l, :],
                              A["b_ffn_conv"][l].rearrange("(t p) -> t p", p=P)).then_inc(prow_loaded, 16)
            dma.dma_start(prow[0:4 * FT, 3, :],
                          A["state_ffn_conv"].rearrange("l b r (t p) -> (l b r t) p", p=P)).then_inc(prow_loaded, 16)
            dma.dma_start(xtok[:, 0:4, :], A["x_prompt"][0].rearrange("(t p) d -> p t d", p=P)).then_inc(x_loaded, 16)
            dma.dma_start(xtok[0:TS, 4, :], A["x_sample"][0]).then_inc(x_loaded, 16)
            for at, src, n in ((0, G_COL, 2 * H), (2 * H, G_COL, 2 * H), (G_LF, G_COL + H, H)):
                dma.dma_start(graw[:, :, at:at + n], w_in[:, :, src:src + n]).then_inc(g_loaded, 16)
            dma.wait_ge(pads_ready, 1)
            for at, src in ((G_LI, 0), (G_LF, H)):
                dma.dma_start(gbias[at:at + H, :],
                              A["b_mlstm_gates"][0, src:src + H].unsqueeze(1)).then_inc(gbias_loaded, 16)
            dma.dma_start(gm0[:, :], A["state_mlstm_m"][0, 0].unsqueeze(1)).then_inc(gbias_loaded, 16)

            with dma.Fori(0, PAIRS) as i:
                b, _ = in_pos(i)
                load_block(b.plus(0), w_in[:, :, ds(i * P + K_COL, P)])
                load_block(b.plus(1), w_in[:, :, ds(i * (2 * P) + V_COL, P)])
                load_block(b.plus(2), w_in[:, :, ds(i * (2 * P) + (V_COL + P), P)])
                load_block(b.plus(3), w_in[:, :, ds(i * P, P)])
                dma.wait_ge(h_split, i * 2 + 1)
                dma.wait_ge(rows_stored, 48)
                for e in range(2):
                    dma.dma_start(gb[:, e, :], rows_d[ds(i * 2 + e), :].broadcast_to([P, T])).then_inc(pair_loaded, 16)
                    dma.dma_start(eb[:, e, :], rows_d[ds(i * 2 + (e + H)), :].broadcast_to([P, T])).then_inc(pair_loaded, 16)
                    dma.dma_start(wint[e * DK:(e + 1) * DK, :],
                                  wint_d[ds(i * 2 + e), :].broadcast_to([DK, TS])).then_inc(pair_loaded, 16)
                dma.dma_start(c0s[:, :], A["state_mlstm_c"].rearrange("l b h k v -> (l b h k) v")[ds(i * P, P), :]
                              ).then_inc(pair_loaded, 16)
                load_block(b.plus(4), w_in[:, :, ds(i * (2 * P) + O_COL, P)])
                load_block(b.plus(5), w_in[:, :, ds(i * (2 * P) + (O_COL + P), P)])

            def load_square(phase, w):
                stepwise(dma, KT, lambda s: load_block(B(phase, s), w[:, :, ds(s.at(0, P), P)]))

            def load_ffn(layer):
                done = 0
                for t, n in enumerate(THIRDS):
                    up, down = ("up", layer, t), ("down", layer, t)

                    def load_up(s):
                        load_block(B(up, s, 2, 0), w_up[layer][:, :, ds(s.at(done, P), P)])
                        load_block(B(up, s, 2, 1), w_up[layer][:, :, ds(s.at(done + FT, P), P)])

                    stepwise(dma, n, load_up)
                    stepwise(dma, KT, lambda s: load_block(
                        B(down, s), w_down[layer][:, done:done + n, ds(s.at(0, P), P)], n))
                    done += n

            load_square("out", w_out)
            load_ffn(0)

            def load_head(s, c):
                if s is None:
                    return
                e = s.const % 2
                load_block(B("kvq", s, 3, 0), w_kv[:, :, ds(s.at(0, P), P)])
                load_block(B("kvq", s, 3, 1), w_kv[:, :, ds(s.at(KT, P), P)])
                dma.wait_ge(out_full, Pos(AT["kvq"][1] + 7 * s.const - 2, s.i, 7 * s.stride).at(0))
                for dst, name, loaded in ((ck, "cache_k", ck_loaded), (cv, "cache_v", cv_loaded)):
                    src = A[name][0].rearrange("(t p) h d -> p t (h d)", p=P)
                    dma.dma_start(dst[:, e, :, :], src[:, :, ds(s.at(0, P), P)]).then_inc(loaded[e], 16)
                load_block(B("kvq", s, 3, 2), w_q[:, :, ds(s.at(0, P), P)])

            att_steps(dma, load_head)
            load_square("o", w_o)
            load_ffn(1)

        @block.tensor
        def _(pe):
            mm = nc.tensor.matmul

            def take(u):
                pe.wait_ge(out_free[u.slot], u.turn(1))

            def product(b, u, rh, rl, tiles=None, nk=KT, lh=whi, ll=wlo, rows=P):
                take(u)
                if b is not None:
                    pe.wait_ge(w_split, b.at(3))
                for k in range(nk):
                    if tiles is not None:
                        tiles(k)
                    hi = lh[:, b.slot, k, :] if b is not None else lh[:, k, :]
                    lo = ll[:, b.slot, k, :] if b is not None else ll[:, k, :]
                    for half in range(2):
                        out = slot(u)[0:rows, half * BANK:half * BANK + HALF]
                        cols = slice(half * HALF, (half + 1) * HALF)
                        mm(out, hi, rh[:, k, cols], start=(k == 0), stop=False)
                        mm(out, hi, rl[:, k, cols], start=False, stop=False)
                        last = mm(out, lo, rh[:, k, cols], start=False, stop=(k == nk - 1))
                return last

            def weights_product(b, u, rh, rl, tiles=None, nk=KT):
                product(b, u, rh, rl, tiles, nk).then_inc(out_full, 1)

            def norm_stats(n):
                pe.wait_ge(x_summed, 9 * n + 10)
                mm(Z[:, 0:TP], mean_d[:, :], ssq[:, 0:TP], start=True, stop=True)
                mm(Z[:, TP:T], mean_d[:, :], ssq[:, TP:T], start=True, stop=True).then_inc(ms_full, 1)

            def x_tiles(n):
                return lambda k: pe.wait_ge(x_split, KT * n + k + 1)

            pe.wait_ge(consts_ready, 1)
            pe.wait_ge(prow_loaded, 11 * 16)
            u = Pos(0)
            take(u)
            at = 0
            for tile, n in enumerate((C_CONV, CONV_ROWS, CONV_ROWS, 88)):
                last = nc.tensor.transpose(slot(u)[:, at:at + n], prow[0:n, tile, :], ident[0:n, 0:n])
                at += n
            last.then_inc(out_full, 1)
            pe.wait_ge(x_loaded, 32)
            for m in range(KT):
                u = Pos(1 + m)
                take(u)
                for t in range(5):
                    n = P if t < 4 else TS
                    last = nc.tensor.transpose(slot(u)[:, t * P:t * P + n], xtok[0:n, t, m * P:(m + 1) * P],
                                               ident[0:n, 0:n])
                last.then_inc(out_full, 1)
            pe.wait_ge(g_split, 1)
            product(None, Pos(1 + KT), xh, xl, x_tiles(0), lh=ghi, ll=glo, rows=G_ROWS).then_inc(out_full, 1)
            norm_stats(0)

            with pe.Fori(0, PAIRS) as i:
                b, u = in_pos(i)
                for k in (U_K, U_V0, U_V1, U_Q):
                    weights_product(b.plus(k), u.plus(k), xh, xl)
                pe.wait_ge(sdec_ready, i * 2 + 1)
                pe.wait_ge(gate_act, 5)
                apart(pe)
                for g, src in enumerate((ga, gwin)):
                    for t in range(5):
                        n = P if t < 4 else TS
                        last = nc.tensor.transpose(Z[0:n, (g * 5 + t) * H:(g * 5 + t + 1) * H],
                                                   src[:, t * P:t * P + n], ident[0:H, 0:H])
                last.then_inc(gT_full, 1)
                for src, which, of in ((kf[:, :], U_KT, U_K), (vf[:, 0, :], U_V0T, U_V0), (vf[:, 1, :], U_V1T, U_V1)):
                    to = u.plus(which)
                    take(to)
                    copied(pe, u.plus(of))
                    for t in range(5):
                        n = P if t < 4 else TS
                        last = nc.tensor.transpose(slot(to)[0:n, t * P:(t + 1) * P], src[:, t * P:t * P + n],
                                                   ident[:, :])
                    last.then_inc(out_full, 1)
                for e in range(2):
                    rows = slice(e * DK, (e + 1) * DK)
                    pe.wait_ge(sdec_ready, i * 2 + (e + 1))
                    pe.wait_ge(cols_ready, i + 1)
                    pe.wait_ge(pads_ready, 2)
                    copied(pe, u.plus(U_Q))
                    for j in range(4):
                        mm(Zb[:, j, 0:TP - P * j], kf[rows, j * P:(j + 1) * P], qf[rows, j * P:TP],
                           start=True, stop=(j < 3))
                    mm(Zb[:, 3, P:P + TS], kf[rows, TP:TP + P], qf[rows, TP:T], start=False,
                       stop=True).then_inc(s_full, 1)
                    weights_product(b.plus(4 + e), u.plus(U_O[e]), xh, xl)
                    if e == 1:
                        to = u.plus(U_SSQ[0])
                        take(to)
                        pe.wait_ge(num_squared, i * 2 + 1)
                        mm(slot(to)[:, 0:TP], mean_v[:, :], nsq[:, 0:TP], start=True, stop=True)
                        mm(slot(to)[:, TP:T], mean_v[:, :], nsq[:, TP:T], start=True, stop=True).then_inc(out_full, 1)
                    pe.wait_ge(sdec_ready, i * 2 + (e + 2))
                    copied(pe, u.plus(U_V1T if e else U_V0T))
                    pe.wait_ge(qw_ready, i + 1)
                    for which in (U_NUM[e], U_DEN[e]):
                        to = u.plus(which)
                        take(to)
                        values = which == U_NUM[e]
                        for j in range(4):
                            mm(slot(to)[:, j * P:TP], vtok[:, j, e * DV:(e + 1) * DV] if values else ones[:, :],
                               sdec[:, j, 0:TP - P * j], start=(j == 0), stop=(j == 3))
                        mm(slot(to)[:, TP:T], vtok[:, 4, e * DV:(e + 1) * DV] if values else ones[:, :],
                           sdec[:, 3, P:P + TS], start=True, stop=False)
                        mm(slot(to)[:, TP:T], c0s[rows, :] if values else n0b[rows, :], qw[rows, :],
                           start=False, stop=True).then_inc(out_full, 1)
                to = u.plus(U_STATE)
                take(to)
                copied(pe, u.plus(U_KT))
                for j in range(4):
                    mm(slot(to)[:, 0:2 * DV + 1], kw[:, j, :], vtok[:, j, :], start=(j == 0), stop=(j == 3))
                mm(slot(to)[:, BANK:BANK + 2 * DV + 1], kw[0:TS, 4, :], vtok[0:TS, 4, :], start=True,
                   stop=True).then_inc(out_full, 1)
                to = u.plus(U_SSQ[1])
                take(to)
                pe.wait_ge(num_squared, i * 2 + 2)
                mm(slot(to)[:, 0:TP], mean_v[:, :], nsq[:, 0:TP], start=True, stop=True)
                mm(slot(to)[:, TP:T], mean_v[:, :], nsq[:, TP:T], start=True, stop=True).then_inc(out_full, 1)

            def square(phase, tiles):
                stepwise(pe, KT, lambda s: weights_product(B(phase, s), U(phase, s), hh, hl,
                                                           tiles if s.const == 0 else None))

            def h_tiles(base):
                return lambda k: pe.wait_ge(h_split, 1 + base + k + 1)

            def ffn_products(layer, n, hbase):
                norm_stats(n)
                done = 0
                for t, nt in enumerate(THIRDS):
                    up, down = ("up", layer, t), ("down", layer, t)

                    def up_pair(s):
                        first = t == 0 and s.const == 0
                        weights_product(B(up, s, 2, 0), U(up, s, 2, 0), xh, xl, x_tiles(n) if first else None)
                        weights_product(B(up, s, 2, 1), U(up, s, 2, 1), xh, xl)

                    stepwise(pe, nt, up_pair)
                    stepwise(pe, KT, lambda s: weights_product(
                        B(down, s), U(down, s), hh, hl, h_tiles(hbase + done) if s.const == 0 else None, nt))
                    done += nt

            square("out", h_tiles(0))
            ffn_products(0, 1, H)
            norm_stats(2)

            def attend(c, stage):
                e = c.const % 2
                if stage == 0:
                    pe.wait_ge(prob_raw, c.at(1))
                    copied(pe, att_use(c, S_K))
                    copied(pe, att_use(c, S_Q))
                    copied(pe, s_ckT(c))
                    for j in range(4):
                        mm(Zb[:, j, 0:TP - P * j], kfa[:, e, j * P:(j + 1) * P], qfa[:, e, j * P:TP],
                           start=True, stop=(j < 3))
                    for j in range(4):
                        mm(Zb[:, 3, P + j * TS:P + (j + 1) * TS], ckT[:, e, j * P:(j + 1) * P], qfa[:, e, TP:T],
                           start=False, stop=False)
                    mm(Zb[:, 3, P + 4 * TS:P + 5 * TS], kfa[:, e, TP:TP + P], qfa[:, e, TP:T], start=False,
                       stop=True).then_inc(z_full, 1)
                elif stage == 1:
                    pe.wait_ge(z_kept, c.at(1))
                    pe.wait_ge(sp_ready, c.at(1))
                    for j in range(4):
                        for jp in range(j, 4):
                            mm(Zb[:, j, (jp - j) * P:TP - P * j], (neg_tri if jp == j else neg_one)[:, :],
                               sp[:, jp, 0:TP - P * jp], start=(jp == j), stop=(j < 3 and jp == 3))
                    late_keys = sp[:, 3, P:P + 5 * TS].rearrange("p (j n) -> p j n", j=5)
                    target = Zb[:, 3, P:P + 5 * TS].rearrange("p (j n) -> p j n", j=5)
                    mm(target, neg_tri[:, :], late_keys, start=False, stop=False)
                    for jp in range(1, 5):
                        last = mm(target[:, 0:jp, :], neg_one[:, :],
                                  late_keys[:, jp:jp + 1, :].broadcast_to([P, jp, TS]), start=False, stop=(jp == 4))
                    last.then_inc(log_full, 1)
                else:
                    u = s_av(c)
                    take(u)
                    pe.wait_ge(prob_ready, c.at(1))
                    copied(pe, att_use(c, S_VT))
                    pe.wait_ge(cv_loaded[e], c.turn(1, 16))
                    for j in range(4):
                        mm(slot(u)[:, j * P:TP], vta[:, e, j, :], prob[:, j, 0:TP - P * j], start=(j == 0), stop=(j == 3))
                    for j in range(4):
                        mm(slot(u)[:, TP:T], cv[:, e, j, :], prob[:, 3, P + j * TS:P + (j + 1) * TS],
                           start=(j == 0), stop=False)
                    mm(slot(u)[:, TP:T], vta[:, e, 4, :], prob[:, 3, P + 4 * TS:P + 5 * TS], start=False,
                       stop=True).then_inc(out_full, 1)

            def by_tokens(to, src, n):
                take(to)
                for t in range(n):
                    w = P if t < 4 else TS
                    last = nc.tensor.transpose(slot(to)[0:w, t * P:(t + 1) * P], src[:, t * P:t * P + w], ident[:, :])
                last.then_inc(out_full, 1)

            def att_step(s, c):
                if s is None:
                    for stage in range(3):
                        attend(c, stage)
                    return
                e = s.const % 2
                weights_product(B("kvq", s, 3, 0), att_use(s, S_K), xh, xl, x_tiles(2) if c is None else None)
                if c is not None:
                    attend(c, 0)
                weights_product(B("kvq", s, 3, 1), att_use(s, S_V), xh, xl)
                copied(pe, att_use(s, S_K))
                by_tokens(att_use(s, S_KT), kfa[:, e, :], 5)
                if c is not None:
                    attend(c, 1)
                weights_product(B("kvq", s, 3, 2), att_use(s, S_Q), xh, xl)
                copied(pe, att_use(s, S_V))
                by_tokens(att_use(s, S_VT), vfa[:, :], 5)
                if c is not None:
                    attend(c, 2)
                to = s_ckT(s)
                take(to)
                pe.wait_ge(ck_loaded[e], s.turn(1, 16))
                for t in range(4):
                    last = nc.tensor.transpose(slot(to)[:, t * P:(t + 1) * P], ck[:, e, t, :], ident[:, :])
                last.then_inc(out_full, 1)

            att_steps(pe, att_step)
            last_av = s_av(Pos(H - 1))
            square("o", lambda k: copied(pe, last_av) if k == H - 1 else None)
            ffn_products(1, 3, H + FT)
            norm_stats(4)

            pe.wait_ge(y_ready, KT)
            for t in range(5):
                w = P if t < 4 else TS
                u = Pos(AT["end"][1] + t)
                take(u)
                for m in range(KT):
                    last = nc.tensor.transpose(slot(u)[0:w, m * P:(m + 1) * P], yT[:, m, t * P:t * P + w], ident[:, :])
                last.then_inc(out_full, 1)
            u = Pos(AT["end"][1] + 5)
            take(u)
            pe.wait_ge(rows_taken, 2 * FT + 1)
            for l in range(2):
                nc.tensor.transpose(slot(u)[0:88, l * P:(l + 1) * P],
                                    conv_rows[:, l, :, :, :].rearrange("p g r t -> p (g r t)"), ident[:, :])
            nc.tensor.transpose(slot(u)[0:8, 2 * P:3 * P], nall[:, :, :].rearrange("p g i -> p (g i)"),
                                ident[:, :]).then_inc(out_full, 1)

        @block.vector
        def _(dve):
            v = nc.vector
            chain = Chain(dve, chain_dve)
            dve.sem_inc(w_split, 2)
            dve.sem_inc(sdec_ready, 1)
            dve.sem_inc(h_split, 1)
            dve.sem_inc(conv_ready, 1)
            for s in range(2):
                dve.sem_inc(out_free[s], 1)

            def split(b, gain=None):
                if b.i is None and b.const >= LAST_BLOCK:
                    return
                raw = wraw[:, b.slot, :, :]
                dve.wait_ge(w_loaded[b.slot], b.turn(1, 16))
                if gain is not None:
                    v.tensor_tensor(raw, raw, par[:, gain:gain + KT].unsqueeze(2).broadcast_to([P, KT, P]),
                                    ALU.mult).then_inc(w_gained, 1)
                    dve.wait_ge(w_gained, Pos(b.const - AT["kvq"][0], b.i, b.stride).at(1))
                v.tensor_copy(whi[:, b.slot, :, :], raw).then_inc(w_high, 1)
                dve.wait_ge(w_high, b.at(1))
                v.tensor_tensor(wlo[:, b.slot, :, :], raw, fb(whi[:, b.slot, :, :]), ALU.subtract).then_inc(w_split, 1)

            def block_out(b, u, gain=None):
                full(dve, u)
                split(b.plus(2), gain)

            def norm_split(ev, m, gain):
                dve.wait_ge(x_high, ev.at(1))
                lo, xm, hi = tile_of(xl, m), tile_of(x, m), fb(tile_of(xh, m))
                if gain is None:
                    ins = v.tensor_tensor(lo, xm, hi, ALU.subtract)
                else:
                    ins = v.scalar_tensor_tensor(out=lo, in0=xm, scalar=gain, in1=hi,
                                                 op0=ALU.mult, op1=ALU.subtract)
                ins.then_inc(x_split, 1)

            def norm_factor(n, query_scale=None):
                dve.wait_ge(rstd_raw, n + 1)
                chain.link(v.tensor_tensor(rstd_q[:, :], nr[:, :], nr[:, :], ALU.mult))
                chain.link(v.scalar_tensor_tensor(out=rstd_q[:, :], in0=Z[:, 0:T], scalar=EPS, in1=rstd_q[:, :],
                                                  op0=ALU.add, op1=ALU.mult))
                chain.link(v.tensor_scalar(rstd_q[:, :], rstd_q[:, :], -0.5, 1.5, ALU.mult, ALU.add))
                chain.link(v.tensor_tensor(rstd[:, :], nr[:, :], rstd_q[:, :], ALU.mult))
                if query_scale is not None:
                    chain.link(v.tensor_scalar(rstd_q[:, :], rstd[:, :], query_scale, None, ALU.mult))

            def factored(u, out, factor=rstd):
                v.tensor_tensor(two(out), halves(u), two(factor[:, :]), ALU.mult).then_inc(out_free[u.slot], 1)

            v.memset(Z[:, :], 0.0)
            split(Pos(0))
            split(Pos(1))
            full(dve, Pos(0))
            v.tensor_copy(par[:, :], slots[0][:, 0:C_ALL]).then_inc(out_free[0], 1)
            copied(dve, Pos(0))
            chain.link(v.tensor_scalar(out_half[:, :], par[:, C_OUT:C_OUT + KT], 0.5, None, ALU.mult))
            dve.wait_ge(g_loaded, 48)
            v.tensor_copy(ghi[:, :, :], graw[:, :, :]).then_inc(g_high, 1)
            dve.wait_ge(g_high, 1)
            v.tensor_tensor(glo[:, :, :], graw[:, :, :], fb(ghi[:, :, :]), ALU.subtract).then_inc(g_split, 1)
            for m in range(KT):
                u = Pos(1 + m)
                full(dve, u)
                v.tensor_copy(x[:, m, :], slot(u)[:, 0:T]).then_inc(out_free[u.slot], 1)
                norm_split(Pos(m), m, par[:, C_MIX + m:C_MIX + m + 1])
            norm_factor(0, DK ** -0.5)

            u = Pos(1 + KT)
            gstep = [0]

            def gate(ins):
                gstep[0] += 1
                ins.then_inc(gate_dve, 1)
                dve.wait_ge(gate_dve, gstep[0])

            full(dve, u)
            v.tensor_tensor(two(gth[:, :]), halves(u)[0:G_ROWS], two(rstd[0:G_ROWS, :]),
                            ALU.mult).then_inc(out_free[u.slot], 1)
            dve.wait_ge(gbias_loaded, 48)
            gate(v.tensor_scalar(gbias[:, :], gbias[:, :], 1.0 / CAP, None, ALU.mult))
            gate(v.memset(ones8[:, :], 1.0))
            dve.wait_ge(gate_act, 2)
            groups = ((0, TP), (TP, T))
            for a, z in groups:
                gate(v.tensor_tensor_scan(nb[:, a:z], ones8[:, a:z], nlf[:, a:z], 0.0, ALU.mult, ALU.add))
            gate(v.scalar_tensor_tensor(out=ga[:, :], in0=gth[G_LI:G_LI + H, :], scalar=CAP, in1=nb[:, :],
                                        op0=ALU.mult, op1=ALU.add))
            for (a, z), m0 in zip(groups, (NEG_BIG, gm0[:, 0:1])):
                gate(v.tensor_tensor_scan(gg[:, a:z], ones8[:, a:z], ga[:, a:z], m0, ALU.mult, ALU.max))
            gate(v.tensor_scalar(gneg[:, :], gg[:, :], -1.0, None, ALU.mult))
            for n, (a, z) in enumerate(groups):
                gate(v.tensor_tensor(gm[:, n:n + 1], gg[:, z - 1:z], nb[:, z - 1:z], ALU.subtract))
            gate(v.tensor_tensor(gem[:, :], nb[:, :], gg[:, :], ALU.subtract))

            with dve.Fori(0, PAIRS) as i:
                b, u = in_pos(i)
                block_out(b.plus(0), u.plus(U_K))
                factored(u.plus(U_K), kf[:, 0:T])
                for e in range(2):
                    block_out(b.plus(1 + e), u.plus(U_V0 + e))
                    factored(u.plus(U_V0 + e), vf[:, e, :])
                block_out(b.plus(3), u.plus(U_Q))
                factored(u.plus(U_Q), qf[:, :], rstd_q)
                copied(dve, u.plus(U_Q))
                dve.wait_ge(pair_loaded, i * (7 * 16) + 7 * 16)
                v.tensor_scalar(n0b[:, :], ones[:, :], par[:, ds(i + C_N0)], None, ALU.mult)
                v.tensor_tensor(qw[:, :], qf[:, TP:T], wint[:, :], ALU.mult).then_inc(qw_ready, 1)
                dve.wait_ge(gT_full, i + 1)
                for g, dst in enumerate((acol, wcol)):
                    src = Z[:, g * 5 * H:(g + 1) * 5 * H].rearrange("p (t h) -> p t h", h=H)
                    v.tensor_copy(dst[:, 0:4, :], src[:, 0:4, ds(i * 2, 2)])
                    last = v.tensor_copy(dst[0:TS, 4:5, :], src[0:TS, 4:5, ds(i * 2, 2)])
                last.then_inc(cols_ready, 1)
                dve.wait_ge(cols_ready, i + 1)
                to = u.plus(U_KT)
                full(dve, to)
                for rows, t0, t1 in ((P, 0, 4), (TS, 4, 5)):
                    last = v.tensor_tensor(
                        kw[0:rows, t0:t1, :].rearrange("p t (e k) -> p t e k", e=2),
                        slot(to)[0:rows, t0 * P:t1 * P].rearrange("p (t e k) -> p t e k", e=2, k=DK),
                        wcol[0:rows, t0:t1, :].unsqueeze(3).broadcast_to([rows, t1 - t0, 2, DK]), ALU.mult)
                last.then_inc(out_free[to.slot], 1)

                def finish(e):
                    to = u.plus(U_SSQ[e])
                    full(dve, to)
                    dve.wait_ge(den_squared, i * 2 + (e + 1))
                    v.tensor_tensor(inv[:, :], slot(to)[:, 0:T], inv[:, :], ALU.add).then_inc(out_free[to.slot], 1)
                    dve.wait_ge(inv_ready, i * 2 + (e + 1))
                    v.tensor_tensor(hm[:, :], num[:, :], inv[:, :], ALU.mult).then_inc(hm_ready, 1)
                    dve.wait_ge(hm_ready, i * 4 + (2 * e + 1))
                    v.scalar_tensor_tensor(out=hm[:, :], in0=tg[:, e, :], scalar=1.0, in1=hm[:, :], op0=ALU.add,
                                           op1=ALU.mult).then_inc(hm_ready, 1)
                    dve.wait_ge(hm_ready, i * 4 + (2 * e + 2))
                    dve.wait_ge(h_high, i * 2 + (e + 1))
                    v.scalar_tensor_tensor(out=tile_of(hl, i * 2 + e), in0=hm[:, :], scalar=out_half[:, ds(i * 2 + e)],
                                           in1=fb(tile_of(hh, i * 2 + e)), op0=ALU.mult,
                                           op1=ALU.subtract).then_inc(h_split, 1)

                for e in range(2):
                    dve.wait_ge(s_full, i * 2 + (e + 1))
                    dve.wait_ge(dec_ready, i * 2 + (e + 1))
                    for j in range(4):
                        n = TP - P * j if j < 3 else P + TS
                        last = v.tensor_tensor(sdec[:, j, 0:n], Zb[:, j, 0:n], dec[:, j, 0:n], ALU.mult)
                    last.then_inc(sdec_ready, 1)
                    block_out(b.plus(4 + e), u.plus(U_O[e]))
                    factored(u.plus(U_O[e]), tg[:, e, :])
                    if e == 1:
                        finish(0)
                    copied(dve, u.plus(U_DEN[e]))
                    v.tensor_tensor(dn[:, :], dn[:, :], eb[:, e, :], ALU.max).then_inc(den_ready, 1)
                to = u.plus(U_STATE)
                full(dve, to)
                dve.wait_ge(state_stored, i * 32 + 16)
                decay = wint[:, TS - 1:TS]
                for e in range(2):
                    rows = slice(e * DK, (e + 1) * DK)
                    v.tensor_copy(cst[rows, 0, :], slot(to)[rows, e * DV:(e + 1) * DV])
                    v.scalar_tensor_tensor(out=cst[rows, 1, :], in0=c0s[rows, :], scalar=decay[rows, :],
                                           in1=slot(to)[rows, BANK + e * DV:BANK + (e + 1) * DV], op0=ALU.mult,
                                           op1=ALU.add)
                v.tensor_copy(nall[:, 0, ds(i)], slot(to)[:, 2 * DV:2 * DV + 1])
                v.scalar_tensor_tensor(out=nall[:, 1, ds(i)], in0=n0b[:, 0:1], scalar=decay,
                                       in1=slot(to)[:, BANK + 2 * DV:BANK + 2 * DV + 1], op0=ALU.mult,
                                       op1=ALU.add).then_inc(out_free[to.slot], 1)
                finish(1)

            def residual(phase, s, norm=None, gain=None, next_gain=None):
                u = U(phase, s)
                block_out(B(phase, s), u, next_gain)
                xs = two(tile_of(x, s.at(0)))
                v.tensor_tensor(xs, halves(u), xs, ALU.add).then_inc(out_free[u.slot], 1)
                if norm is not None and norm < 4:
                    norm_split(Pos(KT * norm + s.const, s.i, s.stride), s.at(0),
                               par[:, ds(s.at(gain))] if gain is not None else None)

            def ffn_tiles(layer, next_norm):
                done = 0
                for t, nt in enumerate(THIRDS):
                    up, down = ("up", layer, t), ("down", layer, t)

                    def tile(s):
                        f = Pos(layer * FT + done + s.const, s.i, s.stride)
                        tap = Pos(C_CONV + layer * CONV_ROWS + done + s.const, s.i, s.stride)
                        ua, uv = U(up, s, 2, 0), U(up, s, 2, 1)
                        block_out(B(up, s, 2, 0), ua)
                        dve.wait_ge(rows_taken, f.at(1))
                        split_at = TP - HALF
                        v.tensor_tensor(ext[:, 2:2 + HALF], slot(ua)[:, 0:HALF], rstd[:, 0:HALF], ALU.mult)
                        v.tensor_tensor(ext[:, 2 + HALF:2 + TP], slot(ua)[:, BANK:BANK + split_at], rstd[:, HALF:TP],
                                        ALU.mult)
                        v.tensor_tensor(ext[:, 4 + TP:4 + T], slot(ua)[:, BANK + split_at:BANK + HALF], rstd[:, TP:T],
                                        ALU.mult).then_inc(out_free[ua.slot], 1)
                        copied(dve, ua)
                        dve.wait_ge(prev_ready, f.at(1))
                        chain.link(v.tensor_scalar(acc[:, :], ext[:, 0:T + 2], par[:, ds(tap.at(0))], None, ALU.mult))
                        chain.link(v.scalar_tensor_tensor(out=acc[:, :], in0=ext[:, 1:T + 3],
                                                          scalar=par[:, ds(tap.at(FT))], in1=acc[:, :],
                                                          op0=ALU.mult, op1=ALU.add))
                        v.scalar_tensor_tensor(out=acc[:, :], in0=ext[:, 2:T + 4], scalar=par[:, ds(tap.at(2 * FT))],
                                               in1=acc[:, :], op0=ALU.mult, op1=ALU.add).then_inc(conv_ready, 1)
                        block_out(B(up, s, 2, 1), uv)
                        factored(uv, val[:, :])
                        copied(dve, uv)
                        dve.wait_ge(gelu_ready, f.at(1))
                        v.tensor_tensor(hid[:, :], gel[:, :], val[:, :], ALU.mult).then_inc(hid_ready, 1)
                        dve.wait_ge(hid_ready, f.at(1))
                        dve.wait_ge(h_high, f.at(1 + (H if layer == 0 else 2 * H)))
                        v.tensor_tensor(tile_of(hl, s.at(0)), hid[:, :], fb(tile_of(hh, s.at(0))), ALU.subtract).then_inc(h_split, 1)

                    counted(chain, dve, nt, tile, 2)
                    if t < 2:
                        stepwise(dve, KT, lambda s: residual(down, s))
                    elif layer == 0:
                        stepwise(dve, KT, lambda s: residual(down, s, next_norm, None,
                                                             C_KV if s.i is None else None), peel=1)
                    else:
                        stepwise(dve, KT, lambda s: residual(down, s, next_norm), peel=1)
                    done += nt

            stepwise(dve, KT, lambda s: residual("out", s, 1, C_FFN))
            norm_factor(1)
            v.memset(ext[:, 0:2], 0.0)
            ffn_tiles(0, 2)
            norm_factor(2, DH ** -0.5)

            v.memset(kfa[:, :, T:5 * P], 0.0)
            chain.link(v.memset(vta[TS:P, :, 4, :], 0.0))

            def att_step(s, c):
                if s is not None:
                    e = s.const % 2
                    block_out(B("kvq", s, 3, 0), att_use(s, S_K), C_MIX + KT)
                    factored(att_use(s, S_K), kfa[:, e, 0:T])
                if c is not None:
                    dve.wait_ge(z_log, c.at(1))
                    v.scalar_tensor_tensor(out=sp[:, :, :], in0=prob[:, :, :], scalar=0.0, in1=za[:, :, :], op0=ALU.max,
                                           op1=ALU.add).then_inc(sp_raw, 1)
                last_head = s is not None and s.i is None and s.const == H - 1
                if s is not None:
                    block_out(B("kvq", s, 3, 1), att_use(s, S_V), None if last_head else C_KV)
                    factored(att_use(s, S_V), vfa[:, :])
                if c is not None:
                    dve.wait_ge(log_full, c.at(1))
                    v.tensor_tensor(prob[:, :, :], prob[:, :, :], Zb[:, :, :], ALU.add).then_inc(log_ready, 1)
                if s is not None:
                    block_out(B("kvq", s, 3, 2), att_use(s, S_Q), None if last_head else C_KV)
                    factored(att_use(s, S_Q), qfa[:, e, :], rstd_q)
                if c is not None:
                    u = s_av(c)
                    full(dve, u)
                    dve.wait_ge(h_high, c.at(1 + H + FT))
                    v.tensor_tensor(tile_of(hl, c.at(0)), slot(u)[:, 0:T], fb(tile_of(hh, c.at(0))), ALU.subtract).then_inc(out_free[u.slot], 1)

            att_steps(dve, att_step)
            stepwise(dve, KT, lambda s: residual("o", s, 3, C_FFN + KT))
            norm_factor(3)
            ffn_tiles(1, 4)
            norm_factor(4)
            for m in range(KT):
                v.scalar_tensor_tensor(out=yT[:, m, :], in0=x[:, m, :], scalar=par[:, C_FIN + m:C_FIN + m + 1],
                                       in1=rstd[:, :], op0=ALU.mult, op1=ALU.mult).then_inc(y_ready, 1)

        @block.scalar
        def _(act):
            a = nc.scalar.activation
            chain = Chain(act, chain_act)
            act.sem_inc(prob_raw, 1)
            act.wait_ge(consts_ready, 1)

            def norm_high(m, gain, u):
                copied(act, u)
                apart(act)
                a(tile_of(xh, m), tile_of(x, m), ACT.Copy, scale=1.0 if gain is None else gain).then_inc(x_high, 1)

            def norm_square(n, s, m, u):
                copied(act, u)
                act.wait_ge(x_summed, Pos(9 * n + s.const + 1, s.i, s.stride).at(0))
                apart(act)
                a(sq[:, s.const % 2, :], tile_of(x, m), ACT.Square).then_inc(x_square, 1)

            def norm_first(n):
                act.wait_ge(ms_full, n + 1)
                chain.link(a(nr[:, :], Z[:, 0:T], ACT.Ln, bias=eps[:, 0:1]))
                a(nr[:, :], nr[:, :], ACT.Exp, scale=-0.5).then_inc(rstd_raw, 1)

            copied(act, Pos(0))
            for m in range(KT):
                norm_high(m, par[:, C_MIX + m:C_MIX + m + 1], Pos(1 + m))
                norm_square(0, Pos(m), m, Pos(1 + m))
            norm_first(0)
            act.wait_ge(gate_dve, 1)
            copied(act, Pos(1 + KT))
            chain.link(a(gth[:, :], gth[:, :], ACT.Tanh, bias=gbias[:, 0:1], scale=1.0 / CAP))
            a(nlf[:, :], gth[G_LF:G_LF + H, :], ACT.Exp, scale=-CAP).then_inc(gate_act, 1)
            act.wait_ge(gate_act, 1)
            a(nlf[:, :], nlf[:, :], ACT.Ln, bias=1.0).then_inc(gate_act, 1)
            act.wait_ge(gate_dve, 8)
            a(gwint[:, :], gneg[:, TP:T], ACT.Exp, bias=gm0[:, 0:1]).then_inc(gate_act, 1)
            for lo_, hi_ in ((0, TP), (TP, T)):
                a(gwin[:, lo_:hi_], ga[:, lo_:hi_], ACT.Exp, bias=gneg[:, hi_ - 1:hi_]).then_inc(gate_act, 1)
            act.wait_ge(gate_dve, 11)
            a(gem[:, :], gem[:, :], ACT.Exp).then_inc(gate_act, 1)

            act.sem_inc(state_stored, 16)
            states = [O[k].rearrange("l b h k v -> (l b h k) v") for k in ("p_c", "s_c")]
            with act.Fori(0, PAIRS) as i:
                b, u = in_pos(i)
                chain.enter(i, 2)

                def decays(e):
                    act.wait_ge(pair_loaded, i * (7 * 16) + 7 * 16)
                    act.wait_ge(cols_ready, i + 1)
                    act.wait_ge(sdec_ready, i * 2 + (e + 1))
                    for j in range(4):
                        a(dec[:, j, 0:TP - P * j], gb[:, e, j * P:TP], ACT.Exp, bias=acol[:, j, e:e + 1])
                    a(dec[:, 3, P:P + TS], gb[:, e, TP:T], ACT.Exp, bias=acol[:, 4, e:e + 1]).then_inc(dec_exp, 1)

                def tanh_gate(e):
                    copied(act, u.plus(U_O[e]))
                    a(tg[:, e, :], tg[:, e, :], ACT.Tanh, scale=0.5).then_inc(tanh_ready, 1)

                def num_den(e):
                    to = u.plus(U_NUM[e])
                    full(act, to)
                    a(nsq[:, :], slot(to)[:, 0:T], ACT.Square).then_inc(num_squared, 1)
                    a(num[:, :], slot(to)[:, 0:T], ACT.Copy).then_inc(out_free[to.slot], 1)
                    to = u.plus(U_DEN[e])
                    full(act, to)
                    a(dn[:, :], slot(to)[:, 0:T], ACT.Abs).then_inc(out_free[to.slot], 1)
                    act.wait_ge(den_ready, i * 2 + (e + 1))
                    a(inv[:, :], dn[:, :], ACT.Square, scale=EPS ** 0.5).then_inc(den_squared, 1)

                def inverse(e):
                    copied(act, u.plus(U_SSQ[e]))
                    chain.link(a(inv[:, :], inv[:, :], ACT.Ln))
                    a(inv[:, :], inv[:, :], ACT.Exp, scale=-0.5).then_inc(inv_ready, 1)

                def high(e):
                    act.wait_ge(hm_ready, i * 4 + (2 * e + 2))
                    apart(act)
                    a(tile_of(hh, i * 2 + e), hm[:, :], ACT.Copy, scale=out_half[:, ds(i * 2 + e)]).then_inc(h_high, 1)

                decays(0)
                for e in range(2):
                    to = u.plus(U_V0T + e)
                    full(act, to)
                    for rows, t0, t1 in ((P, 0, 4), (TS, 4, 5)):
                        last = a(vtok[0:rows, t0:t1, e * DV:(e + 1) * DV],
                                 slot(to)[0:rows, t0 * P:t1 * P].rearrange("p (t d) -> p t d", d=DV), ACT.Copy)
                    last.then_inc(out_free[to.slot], 1)
                decays(1)
                tanh_gate(0)
                num_den(0)
                tanh_gate(1)
                inverse(0)
                high(0)
                num_den(1)
                copied(act, u.plus(U_STATE))
                for n in range(2):
                    act.dma_start(states[n][ds(i * P, P), :], cst[:, n, :]).then_inc(state_stored, 16)
                inverse(1)
                high(1)
            chain.leave(PAIRS)

            def norm_steps(phase, n, gain):
                def step(s):
                    u, m = U(phase, s), s.at(0)
                    if n < 4:
                        norm_high(m, par[:, ds(s.at(gain))] if gain is not None else None, u)
                    norm_square(n, s, m, u)
                stepwise(act, KT, step)
                norm_first(n)

            def ffn_tiles(layer):
                done = 0
                for t, nt in enumerate(THIRDS):
                    def tile(s):
                        f = Pos(layer * FT + done + s.const, s.i, s.stride)
                        bias = par[:, ds(Pos(C_CONV + layer * CONV_ROWS + 3 * FT + done + s.const, s.i, s.stride).at(0))]
                        act.wait_ge(conv_ready, f.at(2))
                        apart(act)
                        a(gel[:, 0:TP], acc[:, 0:TP], ACT.Gelu_apprx_tanh, bias=bias)
                        a(gel[:, TP:T], acc[:, TP + 2:T + 2], ACT.Gelu_apprx_tanh, bias=bias).then_inc(gelu_ready, 1)
                        act.wait_ge(hid_ready, f.at(1))
                        apart(act)
                        a(tile_of(hh, s.at(0)), hid[:, :], ACT.Copy).then_inc(h_high, 1)

                    stepwise(act, nt, tile)
                    done += nt

            norm_steps("out", 1, C_FFN)
            ffn_tiles(0)
            norm_steps(("down", 0, 2), 2, None)

            def by_tokens(to, dst):
                full(act, to)
                for rows, t0, t1 in ((P, 0, 4), (TS, 4, 5)):
                    last = a(dst[0:rows, t0:t1, :], slot(to)[0:rows, t0 * P:t1 * P].rearrange("p (t d) -> p t d", d=P),
                             ACT.Copy)
                last.then_inc(out_free[to.slot], 1)

            p_kv = [O[k][0].rearrange("(t p) h d -> p t (h d)", p=P) for k in ("p_k", "p_v")]
            s_kv = [O[k][0].rearrange("t h d -> t (h d)") for k in ("s_k", "s_v")]

            def store(n, s, u, rows, stored):
                copied(act, u)
                head = ds(s.at(0, P), P)
                act.dma_start(p_kv[n][:, :, head], rows[:, 0:4, :]).then_inc(stored, 16)
                act.dma_start(s_kv[n][:, head], rows[0:TS, 4, :]).then_inc(stored, 16)

            act.sem_inc(k_stored, 16)
            for e in range(2):
                act.sem_inc(v_stored[e], 16)

            def att_step(s, c):
                if c is not None:
                    act.wait_ge(z_full, c.at(1))
                    a(prob[:, :, :], Zb[:, :, :], ACT.Copy).then_inc(z_kept, 1)
                    act.wait_ge(z_kept, c.at(1))
                    chain.link(a(za[:, :, :], prob[:, :, :], ACT.Abs))
                    chain.link(a(za[:, :, :], za[:, :, :], ACT.Exp, scale=-1.0))
                    a(za[:, :, :], za[:, :, :], ACT.Ln, bias=1.0).then_inc(z_log, 1)
                if s is not None:
                    e = s.const % 2
                    act.wait_ge(k_stored, s.at(0, 32) + 16)
                    by_tokens(att_use(s, S_KT), ktok)
                if c is not None:
                    act.wait_ge(log_ready, c.at(1))
                    a(prob[:, :, :], prob[:, :, :], ACT.Exp).then_inc(prob_raw, 1)
                if s is not None:
                    store(0, s, att_use(s, S_KT), ktok, k_stored)
                    act.wait_ge(v_stored[e], s.turn(0, 32) + 16)
                    by_tokens(att_use(s, S_VT), vta[:, e, :, :])
                if c is not None:
                    u = s_av(c)
                    full(act, u)
                    apart(act)
                    a(tile_of(hh, c.at(0)), slot(u)[:, 0:T], ACT.Copy).then_inc(h_high, 1)
                if s is not None:
                    store(1, s, att_use(s, S_VT), vta[:, e, :, :], v_stored[e])
                    to = s_ckT(s)
                    full(act, to)
                    a(ckT[:, e, :], slot(to)[:, 0:PAST], ACT.Copy).then_inc(out_free[to.slot], 1)

            att_step(Pos(0), None)
            with act.Fori(0, PAIRS - 1) as i:
                chain.enter(i, 4)
                att_step(Pos(1, i, 2), Pos(0, i, 2))
                att_step(Pos(2, i, 2), Pos(1, i, 2))
            chain.leave(PAIRS - 1)
            att_step(Pos(H - 1), Pos(H - 2))
            att_step(None, Pos(H - 1))

            norm_steps("o", 3, C_FFN + KT)
            ffn_tiles(1)
            norm_steps(("down", 1, 2), 4, None)
            for t in range(5):
                u = Pos(AT["end"][1] + t)
                w = P if t < 4 else TS
                full(act, u)
                if t >= 2:
                    act.wait_ge(y_stored[t % 2], 16 * (t // 2))
                a(ytok[0:w, t % 2, :], slot(u)[0:w, :], ACT.Copy).then_inc(out_free[u.slot], 1)
            u = Pos(AT["end"][1] + 5)
            full(act, u)
            for n in range(3):
                rows = 88 if n < 2 else 8
                last = a(tails[0:rows, n, :], slot(u)[0:rows, n * P:(n + 1) * P], ACT.Copy)
            last.then_inc(out_free[u.slot], 1)

        @block.gpsimd
        def _(pool):
            g = nc.gpsimd
            chain = Chain(pool, chain_pool)
            pool.sem_inc(x_summed, 1)
            pool.sem_inc(rows_taken, 1)
            for tile, value in ((ident, 0.0), (ones, 1.0), (mean_d, 1.0 / D), (mean_v, 1.0 / DV), (neg_tri, -1.0),
                                (neg_one, -1.0)):
                g.memset(tile[:, :], value)
            chain.link(g.memset(eps[:, :], EPS))
            chain.link(g.affine_select(out=ident[:, :], in_=ident[:, :], compare_op=ALU.not_equal, fill=1.0, base=0,
                                       pattern=[[-1, P]], channel_multiplier=1))
            g.affine_select(out=neg_tri[:, :], in_=neg_tri[:, :], compare_op=ALU.is_ge, fill=0.0, base=0,
                            pattern=[[-1, P]], channel_multiplier=1).then_inc(consts_ready, 1)
            g.memset(gbias[:, :], 0.0).then_inc(pads_ready, 1)
            g.memset(kf[:, T:5 * P], 0.0)
            g.memset(vtok[:, 4, :], 0.0)
            g.memset(acol[:, :, :], 0.0)
            chain.link(g.memset(wcol[:, :, :], 0.0))
            g.memset(vtok[:, :, 2 * DV:2 * DV + 1], 1.0).then_inc(pads_ready, 1)

            def sum_squares(n):
                if n:
                    pool.wait_ge(ms_full, n)
                g.memset(ssq[:, :], 0.0).then_inc(x_summed, 1)

                def step(s):
                    pool.wait_ge(x_summed, Pos(9 * n + 2 + s.const, s.i, s.stride).at(0))
                    pool.wait_ge(x_square, Pos(KT * n + 1 + s.const, s.i, s.stride).at(0))
                    g.tensor_tensor(ssq[:, :], ssq[:, :], sq[:, s.const % 2, :], ALU.add).then_inc(x_summed, 1)

                stepwise(pool, KT, step)

            def mask(tile, keep, sample_at, done):
                diagonal = tile[:, :, 0:P]
                apart(pool)
                g.affine_select(out=diagonal, in_=diagonal, compare_op=keep, fill=0.0, base=0,
                                pattern=[[0, 4], [1, P]], channel_multiplier=-1)
                new = tile[:, 3, sample_at:sample_at + TS]
                g.affine_select(out=new, in_=new, compare_op=keep, fill=0.0, base=0, pattern=[[1, TS]],
                                channel_multiplier=-1).then_inc(done, 1)

            sum_squares(0)
            pool.wait_ge(gate_act, 6)
            pool.dma_start(rows_d[0:H, :], gneg[:, :]).then_inc(rows_stored, 16)
            pool.dma_start(rows_d[H:2 * H, :], gem[:, :]).then_inc(rows_stored, 16)
            pool.dma_start(wint_d[:, :], gwint[:, :]).then_inc(rows_stored, 16)
            pool.dma_start(O["p_m"][0, 0].unsqueeze(1), gm[:, 0:1]).then_inc(tail_stored, 16)
            pool.dma_start(O["s_m"][0, 0].unsqueeze(1), gm[:, 1:2]).then_inc(tail_stored, 16)
            with pool.Fori(0, PAIRS) as i:
                for e in range(2):
                    pool.wait_ge(dec_exp, i * 2 + (e + 1))
                    mask(dec, ALU.is_ge, P, dec_ready)

            def ffn_rows(layer):
                done = 0
                for t, nt in enumerate(THIRDS):
                    up = ("up", layer, t)

                    def tile(s):
                        f = Pos(layer * FT + done + s.const, s.i, s.stride)
                        pool.wait_ge(conv_ready, f.at(1))
                        apart(pool)
                        prev = par[:, C_PREV + 2 * FT * layer:C_PREV + 2 * FT * (layer + 1)].rearrange(
                            "p (r t) -> p r t", r=2)
                        tile_no = ds(s.at(done))
                        g.tensor_copy(ext[:, 2 + TP:4 + TP].unsqueeze(2), prev[:, :, tile_no]).then_inc(prev_ready, 1)
                        copied(pool, U(up, s, 2, 0))
                        apart(pool)
                        for grp, at in ((0, TP), (1, T + 2)):
                            last = g.tensor_copy(conv_rows[:, layer, grp, :, tile_no], ext[:, at:at + 2].unsqueeze(2))
                        last.then_inc(rows_taken, 1)

                    stepwise(pool, nt, tile)
                    done += nt

            sum_squares(1)
            ffn_rows(0)
            sum_squares(2)

            def att_step(s, c):
                if c is not None:
                    pool.wait_ge(sp_raw, c.at(1))
                    mask(sp, ALU.is_gt, P + 4 * TS, sp_ready)
                    pool.wait_ge(prob_raw, c.at(2))
                    mask(prob, ALU.is_gt, P + 4 * TS, prob_ready)

            att_steps(pool, att_step)
            sum_squares(3)
            ffn_rows(1)
            sum_squares(4)
            for t in range(5):
                copied(pool, Pos(AT["end"][1] + t))
                if t < 4:
                    pool.dma_start(O["y_p"][0, t * P:(t + 1) * P, :], ytok[:, t % 2, :]).then_inc(y_stored[t % 2], 16)
                else:
                    pool.dma_start(O["y_s"][0, :, :], ytok[0:TS, 0, :]).then_inc(y_stored[0], 16)
            copied(pool, Pos(AT["end"][1] + 5))
            for l in range(2):
                for grp, name in enumerate(("p_conv", "s_conv")):
                    pool.dma_start(O[name][l, 0].rearrange("r (t p) -> (r t) p", p=P),
                                   tails[grp * 44:(grp + 1) * 44, l, :]).then_inc(tail_stored, 16)
            for grp, name in enumerate(("p_n", "s_n")):
                pool.dma_start(O[name].rearrange("l b (i e) k -> (l b i) (e k)", e=2),
                               tails[grp * PAIRS:(grp + 1) * PAIRS, 2, :]).then_inc(tail_stored, 16)
            pool.wait_ge(tail_stored, 8 * 16)
            pool.wait_ge(state_stored, 16 + 2 * 16 * PAIRS)
            pool.wait_ge(k_stored, 16 + 2 * 16 * H)
            for e in range(2):
                pool.wait_ge(v_stored[e], 16 + 2 * 16 * PAIRS)
            pool.wait_ge(y_stored[0], 3 * 16)
            pool.wait_ge(y_stored[1], 2 * 16)


_INS = ["x_prompt", "x_sample", "cache_k", "cache_v", "state_mlstm_c", "state_mlstm_n", "state_mlstm_m",
        "state_ffn_conv", "g_mix_norm", "w_mlstm_in", "b_mlstm_gates", "g_mlstm_out", "w_mlstm_out", "g_kv_norm", "w_kv",
        "w_sb_q", "w_sb_o", "g_ffn_norm", "w_ffn_up", "w_ffn_conv", "b_ffn_conv", "w_ffn_down", "g_final"]
_OUTS = [("y_p", (1, TP, D)), ("y_s", (1, TS, D)),
         ("p_c", (1, 1, H, DK, DV)), ("p_n", (1, 1, H, DK)), ("p_m", (1, 1, H)), ("p_conv", (2, 1, 2, FF)),
         ("p_k", (1, TP, H, DH)), ("p_v", (1, TP, H, DH)),
         ("s_c", (1, 1, H, DK, DV)), ("s_n", (1, 1, H, DK)), ("s_m", (1, 1, H)), ("s_conv", (2, 1, 2, FF)),
         ("s_k", (1, TS, H, DH)), ("s_v", (1, TS, H, DH))]


def kernel(**inputs):
    import numpy as _np
    import concourse.bacc as _bacc
    from concourse import mybir as _mybir
    from concourse.bass_utils import run_bass_kernel_spmd as _run

    nc = _bacc.Bacc("TRN2", target_bir_lowering=False, num_devices=1)
    arrays, ins, outs = {}, {}, {}
    for name in _INS:
        a = _np.ascontiguousarray(inputs[name])
        arrays[f"in_{name}"] = a
        ins[name] = nc.dram_tensor(f"in_{name}", a.shape, _mybir.dt.from_np(a.dtype), kind="ExternalInput").ap()
    for name, shape in _OUTS:
        outs[name] = nc.dram_tensor(f"out_{name}", shape, _mybir.dt.float32, kind="ExternalOutput").ap()
    trunk_kernel(nc, ins, outs)
    r = _run(nc, [arrays], core_ids=[0])
    return tuple(r.results[0][f"out_{name}"] for name, _ in _OUTS)
```

```python
import concourse.bass as bass
from concourse import mybir
from contextlib import ExitStack

P = 128
D = 1024
TP, TS = 512, 64
T = TP + TS
HALF = T // 2
BANK = 512
KT = D // P
H = 8
DK, DV = D // (2 * H), D // H
DH = D // H
PAST = 512
FF = 2816
FT = FF // P
THIRDS = (8, 8, 6)
EPS = 1e-6
CAP = 15.0
NEG_BIG = -1e30
PAIRS = H // 2
IN_BLOCKS, IN_USES = 6, 16
G_LI, G_LF, G_ROWS = 0, 32, 40

C_MIX, C_OUT, C_KV, C_FFN, C_FIN, C_N0 = 0, 16, 24, 32, 48, 56
C_CONV, CONV_ROWS = 60, 88
C_PREV = C_CONV + 2 * CONV_ROWS
C_ALL = C_PREV + 2 * 44

LN_EXP = "natural_log_exp_and_others"

ACT = mybir.ActivationFunctionType
ALU = mybir.AluOpType
F32 = mybir.dt.float32
F32R = mybir.dt.float32r


class Pos:

    def __init__(self, const, i=None, stride=0):
        self.const, self.i, self.stride = const, i, stride

    def at(self, k=0, times=1):
        n = (self.const + k) * times
        return n if self.i is None else self.i * (self.stride * times) + n

    def plus(self, k):
        return Pos(self.const + k, self.i, self.stride)

    @property
    def slot(self):
        return self.const % 2

    def turn(self, k=0, times=1):
        n = (self.const // 2 + k) * times
        return n if self.i is None else self.i * (self.stride // 2 * times) + n


class Chain:

    def __init__(self, eng, sem):
        self.eng, self.sem, self.n, self.i, self.k = eng, sem, 0, None, 0

    def link(self, ins):
        ins.then_inc(self.sem, 1)
        self.n += 1
        self.eng.wait_ge(self.sem, self.n if self.i is None else self.i * self.k + self.n)

    def enter(self, i, k):
        self.i, self.k, self.start = i, k, self.n

    def leave(self, turns):
        assert self.n - self.start == self.k, (self.n - self.start, self.k)
        self.i, self.n = None, self.start + self.k * turns


def plan():
    b, u = 0, 1 + KT + 1
    at = {"in": (b, u)}
    b, u = b + IN_BLOCKS * PAIRS, u + IN_USES * PAIRS
    at["out"] = (b, u)
    b, u = b + KT, u + KT
    for layer in range(2):
        for t, n in enumerate(THIRDS):
            at["up", layer, t] = (b, u)
            b, u = b + 2 * n, u + 2 * n
            at["down", layer, t] = (b, u)
            b, u = b + KT, u + KT
        if layer == 0:
            at["kvq"] = (b, u)
            b, u = b + 3 * H, u + 7 * H - 1
            at["o"] = (b, u)
            b, u = b + KT, u + KT
    at["end"] = (b, u)
    return at


AT = plan()
LAST_BLOCK = AT["end"][0]


def trunk_kernel(nc, A, O):
    ctx = ExitStack()
    with ctx:
        def sb(name, shape, dt=F32, scope=ctx):
            return scope.enter_context(nc.sbuf_tensor(name, shape, dt))

        def sem(name):
            return ctx.enter_context(nc.semaphore(name))

        def fb(x):
            return x.bitcast(F32)

        x = sb("x", [P, KT, T])
        xh, xl = sb("xh", [P, KT, T], F32R), sb("xl", [P, KT, T], F32R)
        hh, hl = sb("hh", [P, KT, T], F32R), sb("hl", [P, KT, T], F32R)
        wraw = sb("wraw", [P, 2, KT, P])
        whi, wlo = sb("whi", [P, 2, KT, P], F32R), sb("wlo", [P, 2, KT, P], F32R)
        ident, ones = sb("ident", [P, P]), sb("ones", [P, P])
        mean_d, mean_v = sb("mean_d", [P, P]), sb("mean_v", [P, P])
        neg_tri = sb("neg_tri", [P, P])
        neg_tri_r, neg_one_r = sb("neg_tri_r", [P, P], F32R), sb("neg_one_r", [P, P], F32R)
        eps = sb("eps", [P, 1])
        par = sb("par", [P, C_ALL])
        out_half = sb("out_half", [P, KT])
        rstd, rstd_q = sb("rstd", [P, T]), sb("rstd_q", [P, T])
        ssq, sq = sb("ssq", [P, T]), sb("sq", [P, 2, T])
        nr = sq[:, 0, :]
        conv_rows = sb("conv_rows", [P, 2, 2, 2, FT])
        tails = sb("tails", [88, 3, P])
        gm = sb("gm", [H, 2])
        nall = sb("nall", [P, 2, PAIRS])

        setup = ExitStack()
        xtok = sb("xtok", [P, 5, D], scope=setup)
        prow = sb("prow", [P, 4, P], scope=setup)
        graw = sb("graw", [P, KT, G_ROWS], scope=setup)
        ghi, glo = sb("ghi", [P, KT, G_ROWS], F32R, setup), sb("glo", [P, KT, G_ROWS], F32R, setup)
        setup.close()

        ml = ExitStack()
        ga, gwin = sb("ga", [H, T], scope=ml), sb("gwin", [H, T], scope=ml)
        gates = ExitStack()
        gth = sb("gth", [G_ROWS, T], scope=gates)
        nlf, ones8 = sb("nlf", [H, T], scope=gates), sb("ones8", [H, T], scope=gates)
        nb, gg = sb("nb", [H, T], scope=gates), sb("gg", [H, T], scope=gates)
        gneg, gem = sb("gneg", [H, T], scope=gates), sb("gem", [H, T], scope=gates)
        gates.close()
        dec, sdec = sb("dec", [P, 4, BANK], scope=ml), sb("sdec", [P, 4, BANK], scope=ml)
        num, nsq = sb("num", [P, 2, T], scope=ml), sb("nsq", [P, T], scope=ml)
        dn, inv = sb("dn", [P, T], scope=ml), sb("inv", [P, T], scope=ml)
        hm = sb("hm", [P, T], scope=ml)
        gwint, gbias = sb("gwint", [H, TS], scope=ml), sb("gbias", [G_ROWS, 1], scope=ml)
        gm0 = sb("gm0", [H, 1], scope=ml)
        kf, qf = sb("kf", [P, 5 * P], scope=ml), sb("qf", [P, T], scope=ml)
        vf = sb("vf", [P, 2, T], scope=ml)
        qw = sb("qw", [P, TS], scope=ml)
        vtok = sb("vtok", [P, 5, 2 * DV + 1], scope=ml)
        kw = sb("kw", [P, 5, P], scope=ml)
        acol, wcol = sb("acol", [P, 5, 2], scope=ml), sb("wcol", [P, 5, 2], scope=ml)
        gb, eb = sb("gb", [P, 2, T], scope=ml), sb("eb", [P, 2, T], scope=ml)
        wint = sb("wint", [P, TS], scope=ml)
        c0s, n0b = sb("c0s", [P, DV], scope=ml), sb("n0b", [P, P], scope=ml)
        tg = sb("tg", [P, 2, T], scope=ml)
        cst = sb("cst", [P, 2, DV], scope=ml)
        ml.close()

        late = ExitStack()
        ext = sb("ext", [P, T + 4], scope=late)
        ffn = ExitStack()
        acc, gel = sb("acc", [P, T + 2], scope=ffn), sb("gel", [P, T], scope=ffn)
        val, hid = sb("val", [P, T], scope=ffn), sb("hid", [P, T], scope=ffn)
        ffn.close()
        att = ExitStack()
        sp, prob = sb("sp", [P, 4, BANK], scope=att), sb("prob", [P, 4, BANK], scope=att)
        sph = sb("sph", [P, 4, BANK], F32R, att)
        low = ExitStack()
        za = sb("za", [P, 4, BANK], scope=low)
        low.close()
        spl = sb("spl", [P, 4, BANK], F32R, att)
        kfa, qfa, vfa = sb("kfa", [P, 5 * P], scope=att), sb("qfa", [P, T], scope=att), sb("vfa", [P, T], scope=att)
        ktok, vta = sb("ktok", [P, 5, P], scope=att), sb("vta", [P, 5, P], scope=att)
        ck, cv = sb("ck", [P, 4, P], scope=att), sb("cv", [P, 2, 4, P], scope=att)
        ckT = sb("ckT", [P, PAST], scope=att)
        att.close()
        yT = sb("yT", [P, KT, T], scope=late)
        ytok = sb("ytok", [P, 5, D], scope=late)
        factor = sb("factor", [P, 2, 5], scope=late)
        late.close()

        slots = [ctx.enter_context(nc.psum_tensor(f"slot{s}", [P, 2 * BANK], F32)) for s in range(2)]
        Z = ctx.enter_context(nc.psum_tensor("Z", [P, 4 * BANK], F32))
        Zb = Z[:, :].rearrange("p (b n) -> p b n", b=4)
        rows_d = nc.dram_tensor("gate_rows", (2 * H, T), F32).ap()
        wint_d = nc.dram_tensor("gate_winter", (H, TS), F32).ap()

        w_loaded = [sem("w_loaded0"), sem("w_loaded1")]
        w_gained, w_high = sem("w_gained"), sem("w_high")
        w_split = sem("w_split")
        out_full = sem("out_full")
        out_free = [sem("out_free0"), sem("out_free1")]
        chain_dve, chain_act, chain_pool = sem("chain_dve"), sem("chain_act"), sem("chain_pool")
        passed = sem("passed")
        consts_ready, pads_ready = sem("consts_ready"), sem("pads_ready")
        prow_loaded, x_loaded, g_loaded = sem("prow_loaded"), sem("x_loaded"), sem("g_loaded")
        gbias_loaded, x2_loaded = sem("gbias_loaded"), sem("x2_loaded")
        g_high, g_split = sem("g_high"), sem("g_split")
        x_high, x_split = sem("x_high"), sem("x_split")
        x_square, x_summed = sem("x_square"), sem("x_summed")
        ms_full, rstd_raw, rstd_ready = sem("ms_full"), sem("rstd_raw"), sem("rstd_ready")
        h_high, h_split = sem("h_high"), sem("h_split")
        gate_dve, gate_act = sem("gate_dve"), sem("gate_act")
        rows_stored, pair_loaded = sem("rows_stored"), sem("pair_loaded")
        gT_full, cols_ready, qw_ready = sem("gT_full"), sem("cols_ready"), sem("qw_ready")
        dec_exp, dec_ready = sem("dec_exp"), sem("dec_ready")
        s_full, sdec_ready = sem("s_full"), sem("sdec_ready")
        num_squared, den_ready, den_squared = sem("num_squared"), sem("den_ready"), sem("den_squared")
        inv_ready, tanh_ready, hm_ready = sem("inv_ready"), sem("tanh_ready"), sem("hm_ready")
        state_stored = sem("state_stored")
        prev_ready, conv_ready = sem("prev_ready"), sem("conv_ready")
        gelu_ready, hid_ready, rows_taken = sem("gelu_ready"), sem("hid_ready"), sem("rows_taken")
        ck_loaded = sem("ck_loaded")
        cv_loaded = [sem("cv_loaded0"), sem("cv_loaded1")]
        z_full, z_abs, z_log, z_kept = sem("z_full"), sem("z_abs"), sem("z_log"), sem("z_kept")
        sp_raw, sp_masked, sp_high, sp_split = sem("sp_raw"), sem("sp_masked"), sem("sp_high"), sem("sp_split")
        last_full, last_split = sem("last_full"), sem("last_split")
        negs_ready = sem("negs_ready")
        log_full, log_ready = sem("log_full"), sem("log_ready")
        prob_raw, prob_ready = sem("prob_raw"), sem("prob_ready")
        k_stored, v_stored = sem("k_stored"), sem("v_stored")
        y_ready, mean_full = sem("y_ready"), sem("mean_full")
        factor_raw, factor_ready = sem("factor_raw"), sem("factor_ready")
        y_stored, tail_stored = sem("y_stored"), sem("tail_stored")

        def by_rows(w):
            return w.rearrange("(k p) n -> p k n", p=P)

        w_in, w_out = by_rows(A["w_mlstm_in"][0]), by_rows(A["w_mlstm_out"][0])
        w_kv, w_q, w_o = by_rows(A["w_kv"]), by_rows(A["w_sb_q"][0]), by_rows(A["w_sb_o"][0])
        w_up = [by_rows(A["w_ffn_up"][l]) for l in range(2)]
        w_down = [by_rows(A["w_ffn_down"][l]) for l in range(2)]
        K_COL, V_COL = H * DK, 2 * H * DK
        O_COL = V_COL + H * DV
        G_COL = O_COL + D

        def ds(start, size=1):
            return slice(start, start + size) if isinstance(start, int) else bass.ds(start, size)

        def fb(ap):
            return ap.bitcast(F32)

        def tile_of(buf, m):
            return buf[:, ds(m), :].rearrange("p a n -> p (a n)")

        def slot(u):
            return slots[u.slot]

        def halves(u):
            return slot(u)[:, :].rearrange("p (b n) -> p b n", b=2)[:, :, 0:HALF]

        def two(ap):
            return ap.rearrange("p (b n) -> p b n", b=2)

        def apart(eng):
            eng.sem_inc(passed, 1)

        def full(eng, u):
            eng.wait_ge(out_full, u.at(1))

        def copied(eng, u):
            eng.wait_ge(out_free[u.slot], u.turn(2))

        def stepwise(eng, n, body, peel=0):
            turns = n // 2 - peel
            with eng.Fori(0, turns) as i:
                for e in range(2):
                    body(Pos(e, i, 2))
            for s in range(2 * turns, n):
                body(Pos(s))

        def counted(chain, eng, n, body, per_step, peel=0):
            turns = n // 2 - peel
            with eng.Fori(0, turns) as i:
                chain.enter(i, 2 * per_step)
                for e in range(2):
                    body(Pos(e, i, 2))
            chain.leave(turns)
            for s in range(2 * turns, n):
                body(Pos(s))

        def scaled(phase, which, s, per=1, k=0):
            return Pos(AT[phase][which] + s.const * per + k, s.i, s.stride * per)

        def B(phase, s, per=1, k=0):
            return scaled(phase, 0, s, per, k)

        def U(phase, s, per=1, k=0):
            return scaled(phase, 1, s, per, k)

        def in_pos(i):
            return Pos(AT["in"][0], i, IN_BLOCKS), Pos(AT["in"][1], i, IN_USES)

        (U_K, U_V0, U_V1, U_V0T, U_Q, U_KT, U_V1T, U_O0, U_NUM0, U_DEN0, U_O1, U_SSQ0, U_NUM1, U_DEN1, U_STATE,
         U_SSQ1) = range(IN_USES)
        U_O, U_NUM, U_DEN, U_SSQ = (U_O0, U_O1), (U_NUM0, U_NUM1), (U_DEN0, U_DEN1), (U_SSQ0, U_SSQ1)

        S_K, S_V, S_KT, S_Q, S_AV, S_VT, S_CKT = range(7)

        def att_use(s, which):
            start = 7 * s.const - 1 if s.const else (0 if which < S_AV else -1)
            return Pos(AT["kvq"][1] + start + which, s.i, 7 * s.stride)

        def att_steps(eng, body):
            body(Pos(0), None)
            with eng.Fori(0, PAIRS - 1) as i:
                body(Pos(1, i, 2), Pos(0, i, 2))
                body(Pos(2, i, 2), Pos(1, i, 2))
            body(Pos(H - 1), Pos(H - 2))
            body(None, Pos(H - 1))

        block = ctx.enter_context(nc.Block())

        @block.sync
        def _(dma):
            def load_block(b, src, nk=KT):
                dma.wait_ge(w_split, b.at(1))
                apart(dma)
                dma.dma_start(wraw[:, b.slot, 0:nk, :], src).then_inc(w_loaded[b.slot], 16)

            dma.dma_start(xtok[:, 0:4, 0:D // 2],
                          A["x_prompt"][0].rearrange("(t p) d -> p t d", p=P)[:, :, 0:D // 2]).then_inc(x_loaded, 16)
            dma.dma_start(xtok[0:TS, 4, :], A["x_sample"][0]).then_inc(x_loaded, 16)
            dma.dma_start(xtok[:, 0:4, D // 2:D],
                          A["x_prompt"][0].rearrange("(t p) d -> p t d", p=P)[:, :, D // 2:D]).then_inc(x2_loaded, 16)
            for at, src, n in ((0, G_COL, 2 * H), (2 * H, G_COL, 2 * H), (G_LF, G_COL + H, H)):
                dma.dma_start(graw[:, :, at:at + n], w_in[:, :, src:src + n]).then_inc(g_loaded, 16)

            with dma.Fori(0, PAIRS) as i:
                b, _ = in_pos(i)
                load_block(b.plus(0), w_in[:, :, ds(i * P + K_COL, P)])
                load_block(b.plus(1), w_in[:, :, ds(i * (2 * P) + V_COL, P)])
                load_block(b.plus(2), w_in[:, :, ds(i * (2 * P) + (V_COL + P), P)])
                load_block(b.plus(3), w_in[:, :, ds(i * P, P)])
                dma.wait_ge(h_split, i * 2 + 1)
                dma.wait_ge(rows_stored, 48)
                for e in range(2):
                    dma.dma_start(gb[:, e, :], rows_d[ds(i * 2 + e), :].broadcast_to([P, T])).then_inc(pair_loaded, 16)
                    dma.dma_start(eb[:, e, :], rows_d[ds(i * 2 + (e + H)), :].broadcast_to([P, T])).then_inc(pair_loaded, 16)
                    dma.dma_start(wint[e * DK:(e + 1) * DK, :],
                                  wint_d[ds(i * 2 + e), :].broadcast_to([DK, TS])).then_inc(pair_loaded, 16)
                dma.dma_start(c0s[:, :], A["state_mlstm_c"].rearrange("l b h k v -> (l b h k) v")[ds(i * P, P), :]
                              ).then_inc(pair_loaded, 16)
                load_block(b.plus(4), w_in[:, :, ds(i * (2 * P) + O_COL, P)])
                load_block(b.plus(5), w_in[:, :, ds(i * (2 * P) + (O_COL + P), P)])

            def load_square(phase, w):
                stepwise(dma, KT, lambda s: load_block(B(phase, s), w[:, :, ds(s.at(0, P), P)]))

            def load_ffn(layer):
                done = 0
                for t, n in enumerate(THIRDS):
                    up, down = ("up", layer, t), ("down", layer, t)

                    def load_up(s):
                        load_block(B(up, s, 2, 0), w_up[layer][:, :, ds(s.at(done, P), P)])
                        load_block(B(up, s, 2, 1), w_up[layer][:, :, ds(s.at(done + FT, P), P)])

                    stepwise(dma, n, load_up)
                    stepwise(dma, KT, lambda s: load_block(
                        B(down, s), w_down[layer][:, done:done + n, ds(s.at(0, P), P)], n))
                    done += n

            load_square("out", w_out)
            load_ffn(0)

            def load_head(s, c):
                if s is None:
                    return
                e = s.const % 2
                head = ds(s.at(0, P), P)
                cache = [A[name][0].rearrange("(t p) h d -> p t (h d)", p=P) for name in ("cache_k", "cache_v")]
                start = AT["kvq"][1] + 7 * s.const
                load_block(B("kvq", s, 3, 0), w_kv[:, :, head])
                load_block(B("kvq", s, 3, 1), w_kv[:, :, ds(s.at(KT, P), P)])
                dma.wait_ge(out_full, Pos(start - 3, s.i, 7 * s.stride).at(0))
                dma.dma_start(cv[:, e, :, :], cache[1][:, :, head]).then_inc(cv_loaded[e], 16)
                dma.wait_ge(out_full, Pos(start - 1, s.i, 7 * s.stride).at(0))
                dma.dma_start(ck[:, :, :], cache[0][:, :, head]).then_inc(ck_loaded, 16)
                load_block(B("kvq", s, 3, 2), w_q[:, :, head])

            att_steps(dma, load_head)
            load_square("o", w_o)
            load_ffn(1)
            for t in range(5):
                copied(dma, Pos(AT["end"][1] + 1 + t))
                if t < 4:
                    dma.dma_start(O["y_p"][0, t * P:(t + 1) * P, :], ytok[:, t, :]).then_inc(y_stored, 16)
                else:
                    dma.dma_start(O["y_s"][0, :, :], ytok[0:TS, t, :]).then_inc(y_stored, 16)
            dma.wait_ge(y_stored, 5 * 16)

        @block.tensor
        def _(pe):
            mm = nc.tensor.matmul

            def take(u):
                pe.wait_ge(out_free[u.slot], u.turn(1))

            def product(b, u, rh, rl, tiles=None, nk=KT, lh=whi, ll=wlo, rows=P, ks=None):
                ks = range(nk) if ks is None else ks
                if ks[0] == 0:
                    take(u)
                    if b is not None:
                        pe.wait_ge(w_split, b.at(3))
                for k in ks:
                    if tiles is not None:
                        tiles(k)
                    hi = lh[:, b.slot, k, :] if b is not None else lh[:, k, :]
                    lo = ll[:, b.slot, k, :] if b is not None else ll[:, k, :]
                    for half in range(2):
                        out = slot(u)[0:rows, half * BANK:half * BANK + HALF]
                        cols = slice(half * HALF, (half + 1) * HALF)
                        mm(out, hi, rh[:, k, cols], start=(k == 0), stop=False)
                        mm(out, hi, rl[:, k, cols], start=False, stop=False)
                        last = mm(out, lo, rh[:, k, cols], start=False, stop=(k == nk - 1))
                return last

            def weights_product(b, u, rh, rl, tiles=None, nk=KT):
                product(b, u, rh, rl, tiles, nk).then_inc(out_full, 1)

            def norm_stats(n):
                pe.wait_ge(x_summed, 9 * n + 10)
                mm(Z[:, 0:TP], mean_d[:, :], ssq[:, 0:TP], start=True, stop=True)
                mm(Z[:, TP:T], mean_d[:, :], ssq[:, TP:T], start=True, stop=True).then_inc(ms_full, 1)

            def x_tiles(n):
                return lambda k: pe.wait_ge(x_split, KT * n + k + 1)

            pe.wait_ge(consts_ready, 1)
            pe.wait_ge(prow_loaded, 11 * 16)
            u = Pos(0)
            take(u)
            at = 0
            for tile, n in enumerate((C_CONV, CONV_ROWS, CONV_ROWS, 88)):
                last = nc.tensor.transpose(slot(u)[:, at:at + n], prow[0:n, tile, :], ident[0:n, 0:n])
                at += n
            last.then_inc(out_full, 1)
            pe.wait_ge(x_loaded, 32)
            for m in range(KT):
                u = Pos(1 + m)
                if m == KT // 2:
                    pe.wait_ge(x2_loaded, 16)
                take(u)
                for t in range(5):
                    n = P if t < 4 else TS
                    last = nc.tensor.transpose(slot(u)[:, t * P:t * P + n], xtok[0:n, t, m * P:(m + 1) * P],
                                               ident[0:n, 0:n])
                last.then_inc(out_full, 1)
            pe.wait_ge(g_split, 1)
            product(None, Pos(1 + KT), xh, xl, x_tiles(0), lh=ghi, ll=glo, rows=G_ROWS).then_inc(out_full, 1)
            norm_stats(0)

            def by_tokens(to, src, n=5):
                take(to)
                for t in range(n):
                    w = P if t < 4 else TS
                    last = nc.tensor.transpose(slot(to)[0:w, t * P:(t + 1) * P], src[:, t * P:t * P + w], ident[:, :])
                last.then_inc(out_full, 1)

            with pe.Fori(0, PAIRS) as i:
                b, u = in_pos(i)
                for k, use in enumerate((U_K, U_V0, U_V1)):
                    weights_product(b.plus(k), u.plus(use), xh, xl)
                pe.wait_ge(sdec_ready, i * 2 + 1)
                pe.wait_ge(gate_act, 5)
                apart(pe)
                for g, src in enumerate((ga, gwin)):
                    for t in range(5):
                        n = P if t < 4 else TS
                        last = nc.tensor.transpose(Z[0:n, (g * 5 + t) * H:(g * 5 + t + 1) * H],
                                                   src[:, t * P:t * P + n], ident[0:H, 0:H])
                last.then_inc(gT_full, 1)
                copied(pe, u.plus(U_V0))
                by_tokens(u.plus(U_V0T), vf[:, 0, :])
                weights_product(b.plus(3), u.plus(U_Q), xh, xl)
                copied(pe, u.plus(U_K))
                by_tokens(u.plus(U_KT), kf)
                copied(pe, u.plus(U_V1))
                by_tokens(u.plus(U_V1T), vf[:, 1, :])
                for e in range(2):
                    rows = slice(e * DK, (e + 1) * DK)
                    pe.wait_ge(sdec_ready, i * 2 + (e + 1))
                    pe.wait_ge(cols_ready, i + 1)
                    pe.wait_ge(pads_ready, 2)
                    copied(pe, u.plus(U_Q))
                    for j in range(4):
                        mm(Zb[:, j, 0:TP - P * j], kf[rows, j * P:(j + 1) * P], qf[rows, j * P:TP],
                           start=True, stop=(j < 3))
                    mm(Zb[:, 3, P:P + TS], kf[rows, TP:TP + P], qf[rows, TP:T], start=False,
                       stop=True).then_inc(s_full, 1)
                    weights_product(b.plus(4 + e), u.plus(U_O[e]), xh, xl)
                    if e == 1:
                        to = u.plus(U_SSQ[0])
                        take(to)
                        pe.wait_ge(num_squared, i * 2 + 1)
                        mm(slot(to)[:, 0:TP], mean_v[:, :], nsq[:, 0:TP], start=True, stop=True)
                        mm(slot(to)[:, TP:T], mean_v[:, :], nsq[:, TP:T], start=True, stop=True).then_inc(out_full, 1)
                    pe.wait_ge(sdec_ready, i * 2 + (e + 2))
                    copied(pe, u.plus(U_V1T if e else U_V0T))
                    pe.wait_ge(qw_ready, i + 1)
                    for which in (U_NUM[e], U_DEN[e]):
                        to = u.plus(which)
                        take(to)
                        values = which == U_NUM[e]
                        for j in range(4):
                            mm(slot(to)[:, j * P:TP], vtok[:, j, e * DV:(e + 1) * DV] if values else ones[:, :],
                               sdec[:, j, 0:TP - P * j], start=(j == 0), stop=(j == 3))
                        mm(slot(to)[:, TP:T], vtok[:, 4, e * DV:(e + 1) * DV] if values else ones[:, :],
                           sdec[:, 3, P:P + TS], start=True, stop=False)
                        mm(slot(to)[:, TP:T], c0s[rows, :] if values else n0b[rows, :], qw[rows, :],
                           start=False, stop=True).then_inc(out_full, 1)
                to = u.plus(U_STATE)
                take(to)
                copied(pe, u.plus(U_KT))
                for j in range(4):
                    mm(slot(to)[:, 0:2 * DV + 1], kw[:, j, :], vtok[:, j, :], start=(j == 0), stop=(j == 3))
                mm(slot(to)[:, BANK:BANK + 2 * DV + 1], kw[0:TS, 4, :], vtok[0:TS, 4, :], start=True,
                   stop=True).then_inc(out_full, 1)
                to = u.plus(U_SSQ[1])
                take(to)
                pe.wait_ge(num_squared, i * 2 + 2)
                mm(slot(to)[:, 0:TP], mean_v[:, :], nsq[:, 0:TP], start=True, stop=True)
                mm(slot(to)[:, TP:T], mean_v[:, :], nsq[:, TP:T], start=True, stop=True).then_inc(out_full, 1)

            def square(phase, tiles, between=(None, None)):
                for m in range(2):
                    product(B(phase, Pos(m)), U(phase, Pos(m)), hh, hl, tiles if m == 0 else None, ks=range(KT - 1))
                    if between[m] is not None:
                        between[m]()
                for m in range(2):
                    product(B(phase, Pos(m)), U(phase, Pos(m)), hh, hl, tiles if m == 0 else None,
                            ks=range(KT - 1, KT)).then_inc(out_full, 1)
                with pe.Fori(0, KT // 2 - 1) as i:
                    for e in range(2):
                        s = Pos(2 + e, i, 2)
                        weights_product(B(phase, s), U(phase, s), hh, hl)

            def h_tiles(base):
                return lambda k: pe.wait_ge(h_split, 1 + base + k + 1)

            def ffn_products(layer, n, hbase):
                done = 0
                for t, nt in enumerate(THIRDS):
                    up, down = ("up", layer, t), ("down", layer, t)

                    def up_pair(s):
                        first = t == 0 and s.i is None and s.const == 0
                        weights_product(B(up, s, 2, 0), U(up, s, 2, 0), xh, xl, x_tiles(n) if first else None)
                        if first:
                            norm_stats(n)
                        weights_product(B(up, s, 2, 1), U(up, s, 2, 1), xh, xl)

                    first = 2 if t == 0 else 0
                    for f in range(first):
                        up_pair(Pos(f))
                    with pe.Fori(0, (nt - first) // 2) as i:
                        for e in range(2):
                            up_pair(Pos(first + e, i, 2))
                    stepwise(pe, KT, lambda s: weights_product(
                        B(down, s), U(down, s), hh, hl, h_tiles(hbase + done) if s.const == 0 else None, nt))
                    done += nt

            square("out", h_tiles(0))
            ffn_products(0, 1, H)

            def scores(s):
                if s.const:
                    pe.wait_ge(prob_raw, s.at(0))
                else:
                    pe.wait_ge(rstd_ready, 1)
                copied(pe, att_use(s, S_K))
                copied(pe, att_use(s, S_Q))
                copied(pe, att_use(s, S_CKT))
                for j in range(4):
                    mm(Zb[:, j, 0:TP - P * j], kfa[:, j * P:(j + 1) * P], qfa[:, j * P:TP],
                       start=True, stop=(j < 3))
                for j in range(4):
                    mm(Zb[:, 3, P + j * TS:P + (j + 1) * TS], ckT[:, j * P:(j + 1) * P], qfa[:, TP:T],
                       start=False, stop=False)
                mm(Zb[:, 3, P + 4 * TS:P + 5 * TS], kfa[:, TP:TP + P], qfa[:, TP:T], start=False,
                   stop=True).then_inc(z_full, 1)

            def keep_sums(c):
                pe.wait_ge(z_kept, c.at(1))
                pe.wait_ge(sp_split, c.at(1))
                for j in range(4):
                    for n, part in enumerate((sph, spl)):
                        for jp in range(j, 4):
                            mm(Zb[:, j, (jp - j) * P:TP - P * j], (neg_tri_r if jp == j else neg_one_r)[:, :],
                               part[:, jp, 0:TP - P * jp], start=(n == 0 and jp == j), stop=(j < 3 and n == 1 and jp == 3))
                target = Zb[:, 3, P:P + 5 * TS].rearrange("p (j n) -> p j n", j=5)
                for n, part in enumerate((sph, spl)):
                    late_keys = part[:, 3, P:P + 5 * TS].rearrange("p (j n) -> p j n", j=5)
                    mm(target, neg_tri_r[:, :], late_keys, start=False, stop=False)
                    for jp in range(1, 5):
                        last = mm(target[:, 0:jp, :], neg_one_r[:, :],
                                  late_keys[:, jp:jp + 1, :].broadcast_to([P, jp, TS]), start=False,
                                  stop=(n == 1 and jp == 4))
                last.then_inc(log_full, 1)

            def values(c, out, done):
                e = c.const % 2
                pe.wait_ge(prob_ready, c.at(1))
                copied(pe, att_use(c, S_VT))
                pe.wait_ge(cv_loaded[e], c.turn(1, 16))
                for j in range(4):
                    mm(out[:, j * P:TP], vta[:, j, :], prob[:, j, 0:TP - P * j], start=(j == 0), stop=(j == 3))
                for j in range(4):
                    mm(out[:, TP:T], cv[:, e, j, :], prob[:, 3, P + j * TS:P + (j + 1) * TS],
                       start=(j == 0), stop=False)
                mm(out[:, TP:T], vta[:, 4, :], prob[:, 3, P + 4 * TS:P + 5 * TS], start=False,
                   stop=True).then_inc(done, 1)

            def att_step(s, c):
                if s is None:
                    return
                weights_product(B("kvq", s, 3, 0), att_use(s, S_K), xh, xl, x_tiles(2) if c is None else None)
                if c is None:
                    norm_stats(2)
                weights_product(B("kvq", s, 3, 1), att_use(s, S_V), xh, xl)
                if c is not None:
                    keep_sums(c)
                copied(pe, att_use(s, S_K))
                by_tokens(att_use(s, S_KT), kfa)
                weights_product(B("kvq", s, 3, 2), att_use(s, S_Q), xh, xl)
                if c is not None:
                    take(att_use(s, S_AV))
                    values(c, slot(att_use(s, S_AV)), out_full)
                copied(pe, att_use(s, S_V))
                by_tokens(att_use(s, S_VT), vfa)
                to = att_use(s, S_CKT)
                take(to)
                pe.wait_ge(ck_loaded, s.at(1, 16))
                for t in range(4):
                    last = nc.tensor.transpose(slot(to)[:, t * P:(t + 1) * P], ck[:, t, :], ident[:, :])
                last.then_inc(out_full, 1)
                scores(s)

            pe.wait_ge(negs_ready, 2)
            att_steps(pe, att_step)
            last_head = Pos(H - 1)
            square("o", lambda k: pe.wait_ge(last_split, 1) if k == H - 1 else None,
                   (lambda: keep_sums(last_head), lambda: values(last_head, Z, last_full)))
            ffn_products(1, 3, H + FT)

            u = Pos(AT["end"][1])
            take(u)
            pe.wait_ge(rows_taken, 2 * FT + 1)
            for l in range(2):
                nc.tensor.transpose(slot(u)[0:88, l * P:(l + 1) * P],
                                    conv_rows[:, l, :, :, :].rearrange("p g r t -> p (g r t)"), ident[:, :])
            nc.tensor.transpose(slot(u)[0:8, 2 * P:3 * P], nall[:, :, :].rearrange("p g i -> p (g i)"),
                                ident[:, :]).then_inc(out_full, 1)
            pe.wait_ge(y_ready, KT)
            for t in range(5):
                w = P if t < 4 else TS
                u = Pos(AT["end"][1] + 1 + t)
                take(u)
                for m in range(KT):
                    last = nc.tensor.transpose(slot(u)[0:w, m * P:(m + 1) * P], yT[:, m, t * P:t * P + w], ident[:, :])
                last.then_inc(out_full, 1)
                if t == 0:
                    pe.wait_ge(x_summed, 9 * 4 + 10)
                    for tt in range(5):
                        wt = P if tt < 4 else TS
                        last = mm(Z[0:wt, tt:tt + 1], ssq[:, tt * P:tt * P + wt], mean_d[:, 0:1], start=True, stop=True)
                    last.then_inc(mean_full, 1)

        @block.vector
        def _(dve):
            v = nc.vector
            chain = Chain(dve, chain_dve)
            dve.sem_inc(w_split, 2)
            dve.sem_inc(sdec_ready, 1)
            dve.sem_inc(h_split, 1)
            dve.sem_inc(conv_ready, 1)
            for s in range(2):
                dve.sem_inc(out_free[s], 1)

            def split(b, gain=None):
                if b.i is None and b.const >= LAST_BLOCK:
                    return
                raw = wraw[:, b.slot, :, :]
                dve.wait_ge(w_loaded[b.slot], b.turn(1, 16))
                if gain is not None:
                    v.tensor_tensor(raw, raw, par[:, gain:gain + KT].unsqueeze(2).broadcast_to([P, KT, P]),
                                    ALU.mult).then_inc(w_gained, 1)
                    dve.wait_ge(w_gained, Pos(b.const - AT["kvq"][0], b.i, b.stride).at(1))
                v.tensor_copy(whi[:, b.slot, :, :], raw).then_inc(w_high, 1)
                dve.wait_ge(w_high, b.at(1))
                v.tensor_tensor(wlo[:, b.slot, :, :], raw, fb(whi[:, b.slot, :, :]), ALU.subtract).then_inc(w_split, 1)

            def block_out(b, u, gain=None):
                full(dve, u)
                split(b.plus(2), gain)

            def norm_split(ev, m, gain):
                dve.wait_ge(x_high, ev.at(1))
                lo, xm, hi = tile_of(xl, m), tile_of(x, m), fb(tile_of(xh, m))
                if gain is None:
                    ins = v.tensor_tensor(lo, xm, hi, ALU.subtract)
                else:
                    ins = v.scalar_tensor_tensor(out=lo, in0=xm, scalar=gain, in1=hi,
                                                 op0=ALU.mult, op1=ALU.subtract)
                ins.then_inc(x_split, 1)

            def norm_factor(n, query_scale=None):
                dve.wait_ge(rstd_raw, n + 1)
                chain.link(v.tensor_tensor(rstd_q[:, :], nr, nr, ALU.mult))
                chain.link(v.scalar_tensor_tensor(out=rstd_q[:, :], in0=Z[:, 0:T], scalar=EPS, in1=rstd_q[:, :],
                                                  op0=ALU.add, op1=ALU.mult))
                chain.link(v.tensor_scalar(rstd_q[:, :], rstd_q[:, :], -0.5, 1.5, ALU.mult, ALU.add))
                chain.link(v.tensor_tensor(rstd[:, :], nr, rstd_q[:, :], ALU.mult))
                if query_scale is not None:
                    chain.link(v.tensor_scalar(rstd_q[:, :], rstd[:, :], query_scale, None, ALU.mult))

            def factored(u, out, factor=rstd):
                v.tensor_tensor(two(out), halves(u), two(factor[:, :]), ALU.mult).then_inc(out_free[u.slot], 1)

            v.memset(Z[:, :], 0.0)
            split(Pos(0))
            split(Pos(1))
            full(dve, Pos(0))
            v.tensor_copy(par[:, :], slots[0][:, 0:C_ALL]).then_inc(out_free[0], 1)
            copied(dve, Pos(0))
            chain.link(v.tensor_scalar(out_half[:, :], par[:, C_OUT:C_OUT + KT], 0.5, None, ALU.mult))
            dve.wait_ge(consts_ready, 1)
            v.tensor_scalar(neg_one_r[:, :], ones[:, :], -1.0, None, ALU.mult).then_inc(negs_ready, 1)
            v.tensor_copy(neg_tri_r[:, :], neg_tri[:, :]).then_inc(negs_ready, 1)
            dve.wait_ge(g_loaded, 48)
            v.tensor_copy(ghi[:, :, :], graw[:, :, :]).then_inc(g_high, 1)
            dve.wait_ge(g_high, 1)
            v.tensor_tensor(glo[:, :, :], graw[:, :, :], fb(ghi[:, :, :]), ALU.subtract).then_inc(g_split, 1)
            for m in range(KT + 1):
                if m < KT:
                    u = Pos(1 + m)
                    full(dve, u)
                    v.tensor_copy(x[:, m, :], slot(u)[:, 0:T]).then_inc(out_free[u.slot], 1)
                if m:
                    norm_split(Pos(m - 1), m - 1, par[:, C_MIX + m - 1:C_MIX + m])
            norm_factor(0, DK ** -0.5)

            u = Pos(1 + KT)
            gstep = [0]

            def gate(ins):
                gstep[0] += 1
                ins.then_inc(gate_dve, 1)
                dve.wait_ge(gate_dve, gstep[0])

            full(dve, u)
            v.tensor_tensor(two(gth[:, :]), halves(u)[0:G_ROWS], two(rstd[0:G_ROWS, :]),
                            ALU.mult).then_inc(out_free[u.slot], 1)
            dve.wait_ge(gbias_loaded, 48)
            gate(v.tensor_scalar(gbias[:, :], gbias[:, :], 1.0 / CAP, None, ALU.mult))
            gate(v.memset(ones8[:, :], 1.0))
            dve.wait_ge(gate_act, 2)
            groups = ((0, TP), (TP, T))
            for a, z in groups:
                gate(v.tensor_tensor_scan(nb[:, a:z], ones8[:, a:z], nlf[:, a:z], 0.0, ALU.mult, ALU.add))
            gate(v.scalar_tensor_tensor(out=ga[:, :], in0=gth[G_LI:G_LI + H, :], scalar=CAP, in1=nb[:, :],
                                        op0=ALU.mult, op1=ALU.add))
            for (a, z), m0 in zip(groups, (NEG_BIG, gm0[:, 0:1])):
                gate(v.tensor_tensor_scan(gg[:, a:z], ones8[:, a:z], ga[:, a:z], m0, ALU.mult, ALU.max))
            gate(v.tensor_scalar(gneg[:, :], gg[:, :], -1.0, None, ALU.mult))
            for n, (a, z) in enumerate(groups):
                gate(v.tensor_tensor(gm[:, n:n + 1], gg[:, z - 1:z], nb[:, z - 1:z], ALU.subtract))
            gate(v.tensor_tensor(gem[:, :], nb[:, :], gg[:, :], ALU.subtract))

            with dve.Fori(0, PAIRS) as i:
                b, u = in_pos(i)
                block_out(b.plus(0), u.plus(U_K))
                factored(u.plus(U_K), kf[:, 0:T])
                for e in range(2):
                    block_out(b.plus(1 + e), u.plus(U_V0 + e))
                    factored(u.plus(U_V0 + e), vf[:, e, :])
                dve.wait_ge(gT_full, i + 1)
                for g, dst in enumerate((acol, wcol)):
                    src = Z[:, g * 5 * H:(g + 1) * 5 * H].rearrange("p (t h) -> p t h", h=H)
                    v.tensor_copy(dst[:, 0:4, :], src[:, 0:4, ds(i * 2, 2)])
                    last = v.tensor_copy(dst[0:TS, 4:5, :], src[0:TS, 4:5, ds(i * 2, 2)])
                last.then_inc(cols_ready, 1)
                dve.wait_ge(cols_ready, i + 1)
                dve.wait_ge(pair_loaded, i * (7 * 16) + 7 * 16)
                v.tensor_scalar(n0b[:, :], ones[:, :], par[:, ds(i + C_N0)], None, ALU.mult)
                block_out(b.plus(3), u.plus(U_Q))
                factored(u.plus(U_Q), qf[:, :], rstd_q)
                to = u.plus(U_KT)
                full(dve, to)
                for rows, t0, t1 in ((P, 0, 4), (TS, 4, 5)):
                    last = v.tensor_tensor(
                        kw[0:rows, t0:t1, :].rearrange("p t (e k) -> p t e k", e=2),
                        slot(to)[0:rows, t0 * P:t1 * P].rearrange("p (t e k) -> p t e k", e=2, k=DK),
                        wcol[0:rows, t0:t1, :].unsqueeze(3).broadcast_to([rows, t1 - t0, 2, DK]), ALU.mult)
                last.then_inc(out_free[to.slot], 1)
                copied(dve, u.plus(U_Q))
                v.tensor_tensor(qw[:, :], qf[:, TP:T], wint[:, :], ALU.mult).then_inc(qw_ready, 1)

                def mean_square(e):
                    to = u.plus(U_SSQ[e])
                    full(dve, to)
                    dve.wait_ge(den_squared, i * 2 + (e + 1))
                    v.tensor_tensor(inv[:, :], slot(to)[:, 0:T], inv[:, :], ALU.add).then_inc(out_free[to.slot], 1)

                def normalise(e):
                    dve.wait_ge(inv_ready, i * 2 + (e + 1))
                    v.tensor_tensor(hm[:, :], num[:, e, :], inv[:, :], ALU.mult).then_inc(hm_ready, 1)
                    dve.wait_ge(hm_ready, i * 4 + (2 * e + 1))
                    v.scalar_tensor_tensor(out=hm[:, :], in0=tg[:, e, :], scalar=1.0, in1=hm[:, :], op0=ALU.add,
                                           op1=ALU.mult).then_inc(hm_ready, 1)

                def low(e):
                    dve.wait_ge(hm_ready, i * 4 + (2 * e + 2))
                    dve.wait_ge(h_high, i * 2 + (e + 1))
                    v.scalar_tensor_tensor(out=tile_of(hl, i * 2 + e), in0=hm[:, :], scalar=out_half[:, ds(i * 2 + e)],
                                           in1=fb(tile_of(hh, i * 2 + e)), op0=ALU.mult,
                                           op1=ALU.subtract).then_inc(h_split, 1)

                for e in range(2):
                    dve.wait_ge(s_full, i * 2 + (e + 1))
                    dve.wait_ge(dec_ready, i * 2 + (e + 1))
                    for j in range(4):
                        n = TP - P * j if j < 3 else P + TS
                        last = v.tensor_tensor(sdec[:, j, 0:n], Zb[:, j, 0:n], dec[:, j, 0:n], ALU.mult)
                    last.then_inc(sdec_ready, 1)
                    block_out(b.plus(4 + e), u.plus(U_O[e]))
                    factored(u.plus(U_O[e]), tg[:, e, :])
                    if e == 1:
                        mean_square(0)
                        normalise(0)
                    copied(dve, u.plus(U_DEN[e]))
                    v.tensor_tensor(dn[:, :], dn[:, :], eb[:, e, :], ALU.max).then_inc(den_ready, 1)
                low(0)
                to = u.plus(U_STATE)
                full(dve, to)
                dve.wait_ge(state_stored, i * 32 + 16)
                decay = wint[:, TS - 1:TS]
                for e in range(2):
                    rows = slice(e * DK, (e + 1) * DK)
                    v.tensor_copy(cst[rows, 0, :], slot(to)[rows, e * DV:(e + 1) * DV])
                    v.scalar_tensor_tensor(out=cst[rows, 1, :], in0=c0s[rows, :], scalar=decay[rows, :],
                                           in1=slot(to)[rows, BANK + e * DV:BANK + (e + 1) * DV], op0=ALU.mult,
                                           op1=ALU.add)
                v.tensor_copy(nall[:, 0, ds(i)], slot(to)[:, 2 * DV:2 * DV + 1])
                v.scalar_tensor_tensor(out=nall[:, 1, ds(i)], in0=n0b[:, 0:1], scalar=decay,
                                       in1=slot(to)[:, BANK + 2 * DV:BANK + 2 * DV + 1], op0=ALU.mult,
                                       op1=ALU.add).then_inc(out_free[to.slot], 1)
                mean_square(1)
                normalise(1)
                low(1)

            def residual(phase, s, norm=None, gain=None, next_gain=None):
                u = U(phase, s)
                block_out(B(phase, s), u, next_gain)
                xs = two(tile_of(x, s.at(0)))
                v.tensor_tensor(xs, halves(u), xs, ALU.add).then_inc(out_free[u.slot], 1)
                if norm is not None and norm < 4:
                    norm_split(Pos(KT * norm + s.const, s.i, s.stride), s.at(0),
                               par[:, ds(s.at(gain))] if gain is not None else None)

            def ffn_tiles(layer, next_norm):
                done = 0
                for t, nt in enumerate(THIRDS):
                    up, down = ("up", layer, t), ("down", layer, t)

                    def tile(s):
                        f = Pos(layer * FT + done + s.const, s.i, s.stride)
                        tap = Pos(C_CONV + layer * CONV_ROWS + done + s.const, s.i, s.stride)
                        ua, uv = U(up, s, 2, 0), U(up, s, 2, 1)
                        block_out(B(up, s, 2, 0), ua)
                        dve.wait_ge(rows_taken, f.at(1))
                        split_at = TP - HALF
                        v.tensor_tensor(ext[:, 2:2 + HALF], slot(ua)[:, 0:HALF], rstd[:, 0:HALF], ALU.mult)
                        v.tensor_tensor(ext[:, 2 + HALF:2 + TP], slot(ua)[:, BANK:BANK + split_at], rstd[:, HALF:TP],
                                        ALU.mult)
                        v.tensor_tensor(ext[:, 4 + TP:4 + T], slot(ua)[:, BANK + split_at:BANK + HALF], rstd[:, TP:T],
                                        ALU.mult).then_inc(out_free[ua.slot], 1)
                        copied(dve, ua)
                        dve.wait_ge(prev_ready, f.at(1))
                        chain.link(v.tensor_scalar(acc[:, :], ext[:, 0:T + 2], par[:, ds(tap.at(0))], None, ALU.mult))
                        chain.link(v.scalar_tensor_tensor(out=acc[:, :], in0=ext[:, 1:T + 3],
                                                          scalar=par[:, ds(tap.at(FT))], in1=acc[:, :],
                                                          op0=ALU.mult, op1=ALU.add))
                        v.scalar_tensor_tensor(out=acc[:, :], in0=ext[:, 2:T + 4], scalar=par[:, ds(tap.at(2 * FT))],
                                               in1=acc[:, :], op0=ALU.mult, op1=ALU.add).then_inc(conv_ready, 1)
                        block_out(B(up, s, 2, 1), uv)
                        factored(uv, val[:, :])
                        copied(dve, uv)
                        dve.wait_ge(gelu_ready, f.at(1))
                        v.tensor_tensor(hid[:, :], gel[:, :], val[:, :], ALU.mult).then_inc(hid_ready, 1)
                        dve.wait_ge(hid_ready, f.at(1))
                        dve.wait_ge(h_high, f.at(1 + (H if layer == 0 else 2 * H)))
                        v.tensor_tensor(tile_of(hl, s.at(0)), hid[:, :], fb(tile_of(hh, s.at(0))), ALU.subtract).then_inc(h_split, 1)

                    counted(chain, dve, nt, tile, 2)
                    if t < 2:
                        stepwise(dve, KT, lambda s: residual(down, s))
                    elif layer == 0:
                        stepwise(dve, KT, lambda s: residual(down, s, next_norm, None,
                                                             C_KV if s.i is None else None), peel=1)
                    else:
                        stepwise(dve, KT, lambda s: residual(down, s, next_norm), peel=1)
                    done += nt

            stepwise(dve, KT, lambda s: residual("out", s, 1, C_FFN))
            norm_factor(1)
            v.memset(ext[:, 0:2], 0.0)
            ffn_tiles(0, 2)
            norm_factor(2, DH ** -0.5)

            v.memset(kfa[:, T:5 * P], 0.0)
            v.memset(vta[TS:P, 4, :], 0.0).then_inc(rstd_ready, 1)

            def att_step(s, c):
                last_head = s is not None and s.i is None and s.const == H - 1
                if c is not None:
                    dve.wait_ge(z_kept, c.at(1))
                    dve.wait_ge(z_log, c.at(1))
                    v.scalar_tensor_tensor(out=sp[:, :, :], in0=prob[:, :, :], scalar=0.0, in1=za[:, :, :], op0=ALU.max,
                                           op1=ALU.add).then_inc(sp_raw, 1)
                if s is not None:
                    block_out(B("kvq", s, 3, 0), att_use(s, S_K), C_MIX + KT)
                    factored(att_use(s, S_K), kfa[:, 0:T])
                if c is not None:
                    dve.wait_ge(sp_masked, c.at(1))
                    v.tensor_copy(sph[:, :, :], sp[:, :, :]).then_inc(sp_high, 1)
                    dve.wait_ge(sp_high, c.at(1))
                    v.tensor_tensor(spl[:, :, :], sp[:, :, :], fb(sph[:, :, :]), ALU.subtract).then_inc(sp_split, 1)
                if s is not None:
                    block_out(B("kvq", s, 3, 1), att_use(s, S_V), None if last_head else C_KV)
                    factored(att_use(s, S_V), vfa[:, :])
                if c is not None:
                    dve.wait_ge(log_full, c.at(1))
                    v.tensor_tensor(prob[:, :, :], prob[:, :, :], Zb[:, :, :], ALU.add).then_inc(log_ready, 1)
                if s is not None:
                    block_out(B("kvq", s, 3, 2), att_use(s, S_Q), None if last_head else C_KV)
                    factored(att_use(s, S_Q), qfa[:, :], rstd_q)
                if c is not None:
                    dve.wait_ge(h_high, c.at(1 + H + FT))
                    lo, hi = tile_of(hl, c.at(0)), fb(tile_of(hh, c.at(0)))
                    if s is None:
                        v.tensor_tensor(lo, Z[:, 0:T], hi, ALU.subtract).then_inc(last_split, 1)
                    else:
                        u = att_use(s, S_AV)
                        v.tensor_tensor(lo, slot(u)[:, 0:T], hi, ALU.subtract).then_inc(out_free[u.slot], 1)
                if s is not None:
                    dve.wait_ge(z_abs, s.at(1))
                    v.tensor_copy(prob[:, :, :], Zb[:, :, :]).then_inc(z_kept, 1)

            att_steps(dve, att_step)
            stepwise(dve, KT, lambda s: residual("o", s, 3, C_FFN + KT))
            norm_factor(3)
            ffn_tiles(1, 4)
            dve.wait_ge(factor_raw, 1)
            mean, raw, out = Z[:, 0:5], factor[:, 0, :], factor[:, 1, :]
            chain.link(v.tensor_tensor(out, raw, raw, ALU.mult))
            chain.link(v.scalar_tensor_tensor(out=out, in0=mean, scalar=EPS, in1=out, op0=ALU.add, op1=ALU.mult))
            chain.link(v.tensor_scalar(out, out, -0.5, 1.5, ALU.mult, ALU.add))
            v.tensor_tensor(out, raw, out, ALU.mult).then_inc(factor_ready, 1)
            dve.wait_ge(factor_ready, 1)
            for t in (1, 3):
                u = Pos(AT["end"][1] + 1 + t)
                full(dve, u)
                v.tensor_scalar(ytok[:, t, :], slot(u)[:, :], out[:, t:t + 1], None, ALU.mult).then_inc(out_free[u.slot], 1)

        @block.scalar
        def _(act):
            a = nc.scalar.activation
            chain = Chain(act, chain_act)

            for at, name, dims, n in ((C_MIX, "g_mix_norm", "l (t p) -> (l t) p", 16),
                                      (C_OUT, "g_mlstm_out", "l (t p) -> (l t) p", 8),
                                      (C_KV, "g_kv_norm", "(t p) -> t p", 8),
                                      (C_FFN, "g_ffn_norm", "l (t p) -> (l t) p", 16),
                                      (C_FIN, "g_final", "(t p) -> t p", 8)):
                act.dma_start(prow[at:at + n, 0, :], A[name].rearrange(dims, p=P)).then_inc(prow_loaded, 16)
            act.dma_start(prow[C_N0:C_N0 + PAIRS, 0, :],
                          A["state_mlstm_n"].rearrange("l b (i e) k -> (l b i) (e k)", e=2)).then_inc(prow_loaded, 16)
            for l in range(2):
                act.dma_start(prow[0:3 * FT, 1 + l, :],
                              A["w_ffn_conv"][l].rearrange("i (t p) -> (i t) p", p=P)).then_inc(prow_loaded, 16)
                act.dma_start(prow[3 * FT:4 * FT, 1 + l, :],
                              A["b_ffn_conv"][l].rearrange("(t p) -> t p", p=P)).then_inc(prow_loaded, 16)
            act.dma_start(prow[0:4 * FT, 3, :],
                          A["state_ffn_conv"].rearrange("l b r (t p) -> (l b r t) p", p=P)).then_inc(prow_loaded, 16)
            act.wait_ge(pads_ready, 1)
            for at, src in ((G_LI, 0), (G_LF, H)):
                act.dma_start(gbias[at:at + H, :],
                              A["b_mlstm_gates"][0, src:src + H].unsqueeze(1)).then_inc(gbias_loaded, 16)
            act.dma_start(gm0[:, :], A["state_mlstm_m"][0, 0].unsqueeze(1)).then_inc(gbias_loaded, 16)
            act.wait_ge(consts_ready, 1)

            def norm_high(m, gain, u):
                copied(act, u)
                apart(act)
                a(tile_of(xh, m), tile_of(x, m), ACT.Copy, scale=1.0 if gain is None else gain).then_inc(x_high, 1)

            def norm_square(n, s, m, u):
                copied(act, u)
                act.wait_ge(x_summed, Pos(9 * n + s.const + 1, s.i, s.stride).at(0))
                apart(act)
                a(sq[:, s.const % 2, :], tile_of(x, m), ACT.Square).then_inc(x_square, 1)

            def norm_first(n):
                act.wait_ge(ms_full, n + 1)
                act.preload_act_table_set(LN_EXP)
                chain.link(a(nr, Z[:, 0:T], ACT.Ln, bias=eps[:, 0:1]))
                a(nr, nr, ACT.Exp, scale=-0.5).then_inc(rstd_raw, 1)

            copied(act, Pos(0))
            for m in range(KT):
                norm_high(m, par[:, C_MIX + m:C_MIX + m + 1], Pos(1 + m))
                norm_square(0, Pos(m), m, Pos(1 + m))
            norm_first(0)
            act.wait_ge(gate_dve, 1)
            copied(act, Pos(1 + KT))
            chain.link(a(gth[:, :], gth[:, :], ACT.Tanh, bias=gbias[:, 0:1], scale=1.0 / CAP))
            act.preload_act_table_set(LN_EXP)
            a(nlf[:, :], gth[G_LF:G_LF + H, :], ACT.Exp, scale=-CAP).then_inc(gate_act, 1)
            act.wait_ge(gate_act, 1)
            a(nlf[:, :], nlf[:, :], ACT.Ln, bias=1.0).then_inc(gate_act, 1)
            act.wait_ge(gate_dve, 8)
            a(gwint[:, :], gneg[:, TP:T], ACT.Exp, bias=gm0[:, 0:1]).then_inc(gate_act, 1)
            for lo_, hi_ in ((0, TP), (TP, T)):
                a(gwin[:, lo_:hi_], ga[:, lo_:hi_], ACT.Exp, bias=gneg[:, hi_ - 1:hi_]).then_inc(gate_act, 1)
            act.wait_ge(gate_dve, 11)
            a(gem[:, :], gem[:, :], ACT.Exp).then_inc(gate_act, 1)

            act.sem_inc(state_stored, 16)
            states = [O[k].rearrange("l b h k v -> (l b h k) v") for k in ("p_c", "s_c")]
            with act.Fori(0, PAIRS) as i:
                b, u = in_pos(i)
                chain.enter(i, 2)

                def decays(e):
                    act.wait_ge(pair_loaded, i * (7 * 16) + 7 * 16)
                    act.wait_ge(cols_ready, i + 1)
                    act.wait_ge(sdec_ready, i * 2 + (e + 1))
                    for j in range(4):
                        a(dec[:, j, 0:TP - P * j], gb[:, e, j * P:TP], ACT.Exp, bias=acol[:, j, e:e + 1])
                    a(dec[:, 3, P:P + TS], gb[:, e, TP:T], ACT.Exp, bias=acol[:, 4, e:e + 1]).then_inc(dec_exp, 1)

                def tanh_gate(e):
                    copied(act, u.plus(U_O[e]))
                    a(tg[:, e, :], tg[:, e, :], ACT.Tanh, scale=0.5).then_inc(tanh_ready, 1)

                def num_den(e):
                    to = u.plus(U_NUM[e])
                    full(act, to)
                    a(nsq[:, :], slot(to)[:, 0:T], ACT.Square).then_inc(num_squared, 1)
                    a(num[:, e, :], slot(to)[:, 0:T], ACT.Copy).then_inc(out_free[to.slot], 1)
                    to = u.plus(U_DEN[e])
                    full(act, to)
                    a(dn[:, :], slot(to)[:, 0:T], ACT.Abs).then_inc(out_free[to.slot], 1)

                def den_square(e):
                    act.wait_ge(den_ready, i * 2 + (e + 1))
                    a(inv[:, :], dn[:, :], ACT.Square, scale=EPS ** 0.5).then_inc(den_squared, 1)

                def inverse(e):
                    copied(act, u.plus(U_SSQ[e]))
                    apart(act)
                    if e == 0:
                        act.preload_act_table_set(LN_EXP)
                    chain.link(a(inv[:, :], inv[:, :], ACT.Ln))
                    a(inv[:, :], inv[:, :], ACT.Exp, scale=-0.5).then_inc(inv_ready, 1)

                def high(e):
                    act.wait_ge(hm_ready, i * 4 + (2 * e + 2))
                    apart(act)
                    a(tile_of(hh, i * 2 + e), hm[:, :], ACT.Copy, scale=out_half[:, ds(i * 2 + e)]).then_inc(h_high, 1)

                def values_by_tokens(e):
                    to = u.plus(U_V1T if e else U_V0T)
                    full(act, to)
                    for rows, t0, t1 in ((P, 0, 4), (TS, 4, 5)):
                        last = a(vtok[0:rows, t0:t1, e * DV:(e + 1) * DV],
                                 slot(to)[0:rows, t0 * P:t1 * P].rearrange("p (t d) -> p t d", d=DV), ACT.Copy)
                    last.then_inc(out_free[to.slot], 1)

                values_by_tokens(0)
                decays(0)
                values_by_tokens(1)
                decays(1)
                tanh_gate(0)
                num_den(0)
                den_square(0)
                tanh_gate(1)
                inverse(0)
                num_den(1)
                high(0)
                den_square(1)
                copied(act, u.plus(U_STATE))
                for n in range(2):
                    act.dma_start(states[n][ds(i * P, P), :], cst[:, n, :]).then_inc(state_stored, 16)
                inverse(1)
                high(1)
            chain.leave(PAIRS)

            def norm_steps(phase, n, gain):
                def step(s):
                    u, m = U(phase, s), s.at(0)
                    if n < 4:
                        norm_high(m, par[:, ds(s.at(gain))] if gain is not None else None, u)
                    norm_square(n, s, m, u)
                    if n == 4:
                        a(tile_of(yT, m), tile_of(x, m), ACT.Copy, scale=par[:, ds(s.at(gain))]).then_inc(y_ready, 1)
                stepwise(act, KT, step)
                if n < 4:
                    norm_first(n)

            def ffn_tiles(layer):
                done = 0
                for t, nt in enumerate(THIRDS):
                    def tile(s):
                        f = Pos(layer * FT + done + s.const, s.i, s.stride)
                        bias = par[:, ds(Pos(C_CONV + layer * CONV_ROWS + 3 * FT + done + s.const, s.i, s.stride).at(0))]
                        act.wait_ge(conv_ready, f.at(2))
                        apart(act)
                        a(gel[:, 0:TP], acc[:, 0:TP], ACT.Gelu_apprx_tanh, bias=bias)
                        a(gel[:, TP:T], acc[:, TP + 2:T + 2], ACT.Gelu_apprx_tanh, bias=bias).then_inc(gelu_ready, 1)
                        act.wait_ge(hid_ready, f.at(1))
                        apart(act)
                        a(tile_of(hh, s.at(0)), hid[:, :], ACT.Copy).then_inc(h_high, 1)

                    stepwise(act, nt, tile)
                    done += nt

            norm_steps("out", 1, C_FFN)
            ffn_tiles(0)
            norm_steps(("down", 0, 2), 2, None)

            def by_tokens(to, dst):
                full(act, to)
                for rows, t0, t1 in ((P, 0, 4), (TS, 4, 5)):
                    last = a(dst[0:rows, t0:t1, :], slot(to)[0:rows, t0 * P:t1 * P].rearrange("p (t d) -> p t d", d=P),
                             ACT.Copy)
                last.then_inc(out_free[to.slot], 1)

            p_kv = [O[k][0].rearrange("(t p) h d -> p t (h d)", p=P) for k in ("p_k", "p_v")]
            s_kv = [O[k][0].rearrange("t h d -> t (h d)") for k in ("s_k", "s_v")]

            def store(n, s, u, rows, stored):
                copied(act, u)
                head = ds(s.at(0, P), P)
                act.dma_start(p_kv[n][:, :, head], rows[:, 0:4, :]).then_inc(stored, 16)
                act.dma_start(s_kv[n][:, head], rows[0:TS, 4, :]).then_inc(stored, 16)

            act.sem_inc(k_stored, 16)
            act.sem_inc(v_stored, 16)
            act.preload_act_table_set(LN_EXP)

            def att_step(s, c):
                if s is not None:
                    act.wait_ge(k_stored, s.at(0, 32) + 16)
                    by_tokens(att_use(s, S_KT), ktok)
                if c is not None:
                    act.wait_ge(log_ready, c.at(1))
                    a(prob[:, :, :], prob[:, :, :], ACT.Exp).then_inc(prob_raw, 1)
                if s is not None:
                    store(0, s, att_use(s, S_KT), ktok, k_stored)
                if c is not None:
                    if s is None:
                        act.wait_ge(last_full, 1)
                    else:
                        full(act, att_use(s, S_AV))
                    apart(act)
                    out = Z if s is None else slot(att_use(s, S_AV))
                    a(tile_of(hh, c.at(0)), out[:, 0:T], ACT.Copy).then_inc(h_high, 1)
                if s is not None:
                    act.wait_ge(v_stored, s.at(0, 32) + 16)
                    by_tokens(att_use(s, S_VT), vta)
                    to = att_use(s, S_CKT)
                    full(act, to)
                    a(ckT[:, :], slot(to)[:, 0:PAST], ACT.Copy).then_inc(out_free[to.slot], 1)
                    store(1, s, att_use(s, S_VT), vta, v_stored)
                    act.wait_ge(z_full, s.at(1))
                    a(za[:, :, :], Zb[:, :, :], ACT.Abs).then_inc(z_abs, 1)
                    act.wait_ge(z_abs, s.at(1))
                    chain.link(a(za[:, :, :], za[:, :, :], ACT.Exp, scale=-1.0))
                    a(za[:, :, :], za[:, :, :], ACT.Ln, bias=1.0).then_inc(z_log, 1)

            att_step(Pos(0), None)
            with act.Fori(0, PAIRS - 1) as i:
                chain.enter(i, 2)
                att_step(Pos(1, i, 2), Pos(0, i, 2))
                att_step(Pos(2, i, 2), Pos(1, i, 2))
            chain.leave(PAIRS - 1)
            att_step(Pos(H - 1), Pos(H - 2))
            att_step(None, Pos(H - 1))

            norm_steps("o", 3, C_FFN + KT)
            ffn_tiles(1)
            norm_steps(("down", 1, 2), 4, C_FIN)
            u = Pos(AT["end"][1])
            full(act, u)
            for n in range(3):
                rows = 88 if n < 2 else 8
                last = a(tails[0:rows, n, :], slot(u)[0:rows, n * P:(n + 1) * P], ACT.Copy)
            last.then_inc(out_free[u.slot], 1)
            act.wait_ge(mean_full, 1)
            act.preload_act_table_set(LN_EXP)
            chain.link(a(factor[:, 0, :], Z[:, 0:5], ACT.Ln, bias=eps[:, 0:1]))
            a(factor[:, 0, :], factor[:, 0, :], ACT.Exp, scale=-0.5).then_inc(factor_raw, 1)
            act.wait_ge(factor_ready, 1)
            for t in (0, 2, 4):
                u = Pos(AT["end"][1] + 1 + t)
                w = P if t < 4 else TS
                full(act, u)
                a(ytok[0:w, t, :], slot(u)[0:w, :], ACT.Copy, scale=factor[0:w, 1, t:t + 1]).then_inc(out_free[u.slot], 1)

        @block.gpsimd
        def _(pool):
            g = nc.gpsimd
            chain = Chain(pool, chain_pool)
            pool.sem_inc(x_summed, 1)
            pool.sem_inc(rows_taken, 1)
            for tile, value in ((ident, 0.0), (ones, 1.0), (mean_d, 1.0 / D), (mean_v, 1.0 / DV), (neg_tri, -1.0)):
                g.memset(tile[:, :], value)
            chain.link(g.memset(eps[:, :], EPS))
            chain.link(g.affine_select(out=ident[:, :], in_=ident[:, :], compare_op=ALU.not_equal, fill=1.0, base=0,
                                       pattern=[[-1, P]], channel_multiplier=1))
            g.affine_select(out=neg_tri[:, :], in_=neg_tri[:, :], compare_op=ALU.is_ge, fill=0.0, base=0,
                            pattern=[[-1, P]], channel_multiplier=1).then_inc(consts_ready, 1)
            g.memset(gbias[:, :], 0.0).then_inc(pads_ready, 1)
            g.memset(kf[:, T:5 * P], 0.0)
            g.memset(vtok[:, 4, :], 0.0)
            g.memset(acol[:, :, :], 0.0)
            chain.link(g.memset(wcol[:, :, :], 0.0))
            g.memset(vtok[:, :, 2 * DV:2 * DV + 1], 1.0).then_inc(pads_ready, 1)

            def sum_squares(n):
                if n:
                    pool.wait_ge(ms_full, n)
                g.memset(ssq[:, :], 0.0).then_inc(x_summed, 1)

                def step(s):
                    pool.wait_ge(x_summed, Pos(9 * n + 2 + s.const, s.i, s.stride).at(0))
                    pool.wait_ge(x_square, Pos(KT * n + 1 + s.const, s.i, s.stride).at(0))
                    g.tensor_tensor(ssq[:, :], ssq[:, :], sq[:, s.const % 2, :], ALU.add).then_inc(x_summed, 1)

                stepwise(pool, KT, step)

            def mask(tile, keep, sample_at, done):
                diagonal = tile[:, :, 0:P]
                apart(pool)
                g.affine_select(out=diagonal, in_=diagonal, compare_op=keep, fill=0.0, base=0,
                                pattern=[[0, 4], [1, P]], channel_multiplier=-1)
                new = tile[:, 3, sample_at:sample_at + TS]
                g.affine_select(out=new, in_=new, compare_op=keep, fill=0.0, base=0, pattern=[[1, TS]],
                                channel_multiplier=-1).then_inc(done, 1)

            sum_squares(0)
            pool.wait_ge(gate_act, 6)
            pool.dma_start(rows_d[0:H, :], gneg[:, :]).then_inc(rows_stored, 16)
            pool.dma_start(rows_d[H:2 * H, :], gem[:, :]).then_inc(rows_stored, 16)
            pool.dma_start(wint_d[:, :], gwint[:, :]).then_inc(rows_stored, 16)
            pool.dma_start(O["p_m"][0, 0].unsqueeze(1), gm[:, 0:1]).then_inc(tail_stored, 16)
            pool.dma_start(O["s_m"][0, 0].unsqueeze(1), gm[:, 1:2]).then_inc(tail_stored, 16)
            with pool.Fori(0, PAIRS) as i:
                for e in range(2):
                    pool.wait_ge(dec_exp, i * 2 + (e + 1))
                    mask(dec, ALU.is_ge, P, dec_ready)

            def ffn_rows(layer):
                done = 0
                for t, nt in enumerate(THIRDS):
                    up = ("up", layer, t)

                    def tile(s):
                        f = Pos(layer * FT + done + s.const, s.i, s.stride)
                        pool.wait_ge(conv_ready, f.at(1))
                        apart(pool)
                        prev = par[:, C_PREV + 2 * FT * layer:C_PREV + 2 * FT * (layer + 1)].rearrange(
                            "p (r t) -> p r t", r=2)
                        tile_no = ds(s.at(done))
                        g.tensor_copy(ext[:, 2 + TP:4 + TP].unsqueeze(2), prev[:, :, tile_no]).then_inc(prev_ready, 1)
                        copied(pool, U(up, s, 2, 0))
                        apart(pool)
                        for grp, at in ((0, TP), (1, T + 2)):
                            last = g.tensor_copy(conv_rows[:, layer, grp, :, tile_no], ext[:, at:at + 2].unsqueeze(2))
                        last.then_inc(rows_taken, 1)

                    stepwise(pool, nt, tile)
                    done += nt

            sum_squares(1)
            ffn_rows(0)
            sum_squares(2)

            def att_step(s, c):
                if c is not None:
                    pool.wait_ge(sp_raw, c.at(1))
                    mask(sp, ALU.is_gt, P + 4 * TS, sp_masked)
                    pool.wait_ge(prob_raw, c.at(1))
                    mask(prob, ALU.is_gt, P + 4 * TS, prob_ready)

            att_steps(pool, att_step)
            sum_squares(3)
            ffn_rows(1)
            sum_squares(4)
            copied(pool, Pos(AT["end"][1]))
            for l in range(2):
                for grp, name in enumerate(("p_conv", "s_conv")):
                    pool.dma_start(O[name][l, 0].rearrange("r (t p) -> (r t) p", p=P),
                                   tails[grp * 44:(grp + 1) * 44, l, :]).then_inc(tail_stored, 16)
            for grp, name in enumerate(("p_n", "s_n")):
                pool.dma_start(O[name].rearrange("l b (i e) k -> (l b i) (e k)", e=2),
                               tails[grp * PAIRS:(grp + 1) * PAIRS, 2, :]).then_inc(tail_stored, 16)
            pool.wait_ge(tail_stored, 8 * 16)
            pool.wait_ge(state_stored, 16 + 2 * 16 * PAIRS)
            pool.wait_ge(k_stored, 16 + 2 * 16 * H)
            pool.wait_ge(v_stored, 16 + 2 * 16 * H)


_INS = ["x_prompt", "x_sample", "cache_k", "cache_v", "state_mlstm_c", "state_mlstm_n", "state_mlstm_m",
        "state_ffn_conv", "g_mix_norm", "w_mlstm_in", "b_mlstm_gates", "g_mlstm_out", "w_mlstm_out", "g_kv_norm", "w_kv",
        "w_sb_q", "w_sb_o", "g_ffn_norm", "w_ffn_up", "w_ffn_conv", "b_ffn_conv", "w_ffn_down", "g_final"]
_OUTS = [("y_p", (1, TP, D)), ("y_s", (1, TS, D)),
         ("p_c", (1, 1, H, DK, DV)), ("p_n", (1, 1, H, DK)), ("p_m", (1, 1, H)), ("p_conv", (2, 1, 2, FF)),
         ("p_k", (1, TP, H, DH)), ("p_v", (1, TP, H, DH)),
         ("s_c", (1, 1, H, DK, DV)), ("s_n", (1, 1, H, DK)), ("s_m", (1, 1, H)), ("s_conv", (2, 1, 2, FF)),
         ("s_k", (1, TS, H, DH)), ("s_v", (1, TS, H, DH))]


def kernel(**inputs):
    import numpy as _np
    import concourse.bacc as _bacc
    from concourse import mybir as _mybir
    from concourse.bass_utils import run_bass_kernel_spmd as _run

    nc = _bacc.Bacc("TRN2", target_bir_lowering=False, num_devices=1)
    arrays, ins, outs = {}, {}, {}
    for name in _INS:
        a = _np.ascontiguousarray(inputs[name])
        arrays[f"in_{name}"] = a
        ins[name] = nc.dram_tensor(f"in_{name}", a.shape, _mybir.dt.from_np(a.dtype), kind="ExternalInput").ap()
    for name, shape in _OUTS:
        outs[name] = nc.dram_tensor(f"out_{name}", shape, _mybir.dt.float32, kind="ExternalOutput").ap()
    trunk_kernel(nc, ins, outs)
    r = _run(nc, [arrays], core_ids=[0])
    return tuple(r.results[0][f"out_{name}"] for name, _ in _OUTS)
```

```python
import concourse.bass as bass
from concourse import mybir
from contextlib import ExitStack

P = 128
D = 1024
TP, TS = 512, 64
T = TP + TS
HALF = T // 2
BANK = 512
KT = D // P
H = 8
DK, DV = D // (2 * H), D // H
DH = D // H
PAST = 512
FF = 2816
FT = FF // P
THIRDS = (8, 8, 6)
EPS = 1e-6
CAP = 15.0
NEG_BIG = -1e30
PAIRS = H // 2
IN_BLOCKS, IN_USES = 6, 16
G_LI, G_LF, G_ROWS = 0, 32, 40

C_MIX, C_OUT, C_KV, C_FFN, C_FIN, C_N0 = 0, 16, 24, 32, 48, 56
C_CONV, CONV_ROWS = 60, 88
C_PREV = C_CONV + 2 * CONV_ROWS
C_ALL = C_PREV + 2 * 44

LN_EXP = "natural_log_exp_and_others"

ACT = mybir.ActivationFunctionType
ALU = mybir.AluOpType
F32 = mybir.dt.float32
F32R = mybir.dt.float32r


PAR_USE, CONV_USE, GATES_USE = 2, KT + 1, KT + 2


class Pos:

    def __init__(self, const, i=None, stride=0):
        self.const, self.i, self.stride = const, i, stride

    def at(self, k=0, times=1):
        n = (self.const + k) * times
        return n if self.i is None else self.i * (self.stride * times) + n

    def plus(self, k):
        return Pos(self.const + k, self.i, self.stride)

    @property
    def slot(self):
        return self.const % 2

    def turn(self, k=0, times=1):
        n = (self.const // 2 + k) * times
        return n if self.i is None else self.i * (self.stride // 2 * times) + n


class Chain:

    def __init__(self, eng, sem):
        self.eng, self.sem, self.n, self.i, self.k = eng, sem, 0, None, 0

    def link(self, ins):
        ins.then_inc(self.sem, 1)
        self.n += 1
        self.eng.wait_ge(self.sem, self.n if self.i is None else self.i * self.k + self.n)

    def enter(self, i, k):
        self.i, self.k, self.start = i, k, self.n

    def leave(self, turns):
        assert self.n - self.start == self.k, (self.n - self.start, self.k)
        self.i, self.n = None, self.start + self.k * turns


def plan():
    b, u = 0, GATES_USE + 1
    at = {"in": (b, u)}
    b, u = b + IN_BLOCKS * PAIRS, u + IN_USES * PAIRS
    at["out"] = (b, u)
    b, u = b + KT, u + KT
    for layer in range(2):
        for t, n in enumerate(THIRDS):
            at["up", layer, t] = (b, u)
            b, u = b + 2 * n, u + 2 * n
            at["down", layer, t] = (b, u)
            b, u = b + KT, u + KT
        if layer == 0:
            at["kvq"] = (b, u)
            b, u = b + 3 * H, u + 7 * H - 1
            at["o"] = (b, u)
            b, u = b + KT, u + KT
    at["end"] = (b, u)
    return at


AT = plan()
LAST_BLOCK = AT["end"][0]


def trunk_kernel(nc, A, O):
    ctx = ExitStack()
    with ctx:
        def sb(name, shape, dt=F32, scope=ctx):
            return scope.enter_context(nc.sbuf_tensor(name, shape, dt))

        def sem(name):
            return ctx.enter_context(nc.semaphore(name))

        def fb(x):
            return x.bitcast(F32)

        x = sb("x", [P, KT, T])
        xh, xl = sb("xh", [P, KT, T], F32R), sb("xl", [P, KT, T], F32R)
        hh, hl = sb("hh", [P, KT, T], F32R), sb("hl", [P, KT, T], F32R)
        wraw = sb("wraw", [P, 2, KT, P])
        whi, wlo = sb("whi", [P, 2, KT, P], F32R), sb("wlo", [P, 2, KT, P], F32R)
        ident, ones = sb("ident", [P, P]), sb("ones", [P, P])
        mean_d, mean_v = sb("mean_d", [P, P]), sb("mean_v", [P, P])
        neg_tri = sb("neg_tri", [P, P])
        neg_tri_r, neg_one_r = sb("neg_tri_r", [P, P], F32R), sb("neg_one_r", [P, P], F32R)
        eps = sb("eps", [P, 1])
        par = sb("par", [P, C_ALL])
        out_half = sb("out_half", [P, KT])
        rstd, rstd_q = sb("rstd", [P, T]), sb("rstd_q", [P, T])
        ssq, sq = sb("ssq", [P, T]), sb("sq", [P, 2, T])
        nr = sq[:, 0, :]
        conv_rows = sb("conv_rows", [P, 2, 2, 2, FT])
        tails = sb("tails", [88, 3, P])
        gm = sb("gm", [H, 2])
        nall = sb("nall", [P, 2, PAIRS])

        setup = ExitStack()
        xtok = sb("xtok", [P, 5, D], scope=setup)
        prow = sb("prow", [P, 4, P], scope=setup)
        graw = sb("graw", [P, KT, G_ROWS], scope=setup)
        ghi, glo = sb("ghi", [P, KT, G_ROWS], F32R, setup), sb("glo", [P, KT, G_ROWS], F32R, setup)
        setup.close()

        ml = ExitStack()
        ga, gwin = sb("ga", [H, T], scope=ml), sb("gwin", [H, T], scope=ml)
        gates = ExitStack()
        gth = sb("gth", [G_ROWS, T], scope=gates)
        nlf, ones8 = sb("nlf", [H, T], scope=gates), sb("ones8", [H, T], scope=gates)
        nb, gg = sb("nb", [H, T], scope=gates), sb("gg", [H, T], scope=gates)
        gneg, gem = sb("gneg", [H, T], scope=gates), sb("gem", [H, T], scope=gates)
        gates.close()
        dec, sdec = sb("dec", [P, 4, BANK], scope=ml), sb("sdec", [P, 4, BANK], scope=ml)
        num, nsq = sb("num", [P, 2, T], scope=ml), sb("nsq", [P, T], scope=ml)
        dn, inv = sb("dn", [P, T], scope=ml), sb("inv", [P, T], scope=ml)
        hm = sb("hm", [P, T], scope=ml)
        gwint, gbias = sb("gwint", [H, TS], scope=ml), sb("gbias", [G_ROWS, 1], scope=ml)
        gm0 = sb("gm0", [H, 1], scope=ml)
        kf, qf = sb("kf", [P, 5 * P], scope=ml), sb("qf", [P, T], scope=ml)
        vf = sb("vf", [P, 2, T], scope=ml)
        qw, dsum = sb("qw", [P, TS], scope=ml), sb("dsum", [P, TP], scope=ml)
        vtok = sb("vtok", [P, 5, 2 * DV + 1], scope=ml)
        kw = sb("kw", [P, 5, P], scope=ml)
        acol, wcol = sb("acol", [P, 5, 2], scope=ml), sb("wcol", [P, 5, 2], scope=ml)
        gb, eb = sb("gb", [P, 2, T], scope=ml), sb("eb", [P, 2, T], scope=ml)
        wint = sb("wint", [P, TS], scope=ml)
        c0s, n0b = sb("c0s", [P, DV], scope=ml), sb("n0b", [P, P], scope=ml)
        tg = sb("tg", [P, 2, T], scope=ml)
        cst = sb("cst", [P, 2, DV], scope=ml)
        ml.close()

        late = ExitStack()
        ext = sb("ext", [P, T + 4], scope=late)
        ffn = ExitStack()
        acc, gel = sb("acc", [P, T + 2], scope=ffn), sb("gel", [P, T], scope=ffn)
        val, hid = sb("val", [P, T], scope=ffn), sb("hid", [P, T], scope=ffn)
        ffn.close()
        att = ExitStack()
        sp, prob = sb("sp", [P, 4, BANK], scope=att), sb("prob", [P, 4, BANK], scope=att)
        sph = sb("sph", [P, 4, BANK], F32R, att)
        low = ExitStack()
        za = sb("za", [P, 4, BANK], scope=low)
        low.close()
        spl = sb("spl", [P, 4, BANK], F32R, att)
        kfa, qfa, vfa = sb("kfa", [P, 5 * P], scope=att), sb("qfa", [P, T], scope=att), sb("vfa", [P, T], scope=att)
        ktok, vta = sb("ktok", [P, 5, P], scope=att), sb("vta", [P, 5, P], scope=att)
        ck, cv = sb("ck", [P, 4, P], scope=att), sb("cv", [P, 2, 4, P], scope=att)
        ckT = sb("ckT", [P, PAST], scope=att)
        att.close()
        yT = sb("yT", [P, KT, T], scope=late)
        ytok = sb("ytok", [P, 5, D], scope=late)
        factor = sb("factor", [P, 2, 5], scope=late)
        late.close()

        slots = [ctx.enter_context(nc.psum_tensor(f"slot{s}", [P, 2 * BANK], F32)) for s in range(2)]
        Z = ctx.enter_context(nc.psum_tensor("Z", [P, 4 * BANK], F32))
        Zb = Z[:, :].rearrange("p (b n) -> p b n", b=4)
        rows_d = nc.dram_tensor("gate_rows", (2 * H, T), F32).ap()
        wint_d = nc.dram_tensor("gate_winter", (H, TS), F32).ap()

        w_loaded = [sem("w_loaded0"), sem("w_loaded1")]
        w_gained, w_high = sem("w_gained"), sem("w_high")
        w_split = sem("w_split")
        out_full = sem("out_full")
        out_free = [sem("out_free0"), sem("out_free1")]
        chain_dve, chain_act, chain_pool = sem("chain_dve"), sem("chain_act"), sem("chain_pool")
        passed = sem("passed")
        consts_ready, pads_ready = sem("consts_ready"), sem("pads_ready")
        prow_loaded, conv_loaded = sem("prow_loaded"), sem("conv_loaded")
        x_loaded, g_loaded = sem("x_loaded"), sem("g_loaded")
        gbias_loaded, x2_loaded = sem("gbias_loaded"), sem("x2_loaded")
        g_high, g_split = sem("g_high"), sem("g_split")
        x_high, x_split = sem("x_high"), sem("x_split")
        x_square, x_summed = sem("x_square"), sem("x_summed")
        ms_full, rstd_raw, rstd_ready = sem("ms_full"), sem("rstd_raw"), sem("rstd_ready")
        h_high, h_split = sem("h_high"), sem("h_split")
        gate_dve, gate_act = sem("gate_dve"), sem("gate_act")
        rows_stored, pair_loaded = sem("rows_stored"), sem("pair_loaded")
        gT_full, cols_ready, qw_ready = sem("gT_full"), sem("cols_ready"), sem("qw_ready")
        dec_exp, dec_ready = sem("dec_exp"), sem("dec_ready")
        s_full, sdec_ready = sem("s_full"), sem("sdec_ready")
        den_summed = sem("den_summed")
        num_squared, den_ready, den_squared = sem("num_squared"), sem("den_ready"), sem("den_squared")
        inv_ready, tanh_ready, hm_ready = sem("inv_ready"), sem("tanh_ready"), sem("hm_ready")
        state_stored = sem("state_stored")
        prev_ready, conv_ready = sem("prev_ready"), sem("conv_ready")
        gelu_ready, hid_ready, rows_taken = sem("gelu_ready"), sem("hid_ready"), sem("rows_taken")
        ck_loaded = sem("ck_loaded")
        cv_loaded = [sem("cv_loaded0"), sem("cv_loaded1")]
        z_full, z_abs, z_log, z_kept = sem("z_full"), sem("z_abs"), sem("z_log"), sem("z_kept")
        sp_raw, sp_masked, sp_high, sp_split = sem("sp_raw"), sem("sp_masked"), sem("sp_high"), sem("sp_split")
        last_full, last_split = sem("last_full"), sem("last_split")
        negs_ready = sem("negs_ready")
        log_full, log_ready = sem("log_full"), sem("log_ready")
        prob_raw, prob_ready = sem("prob_raw"), sem("prob_ready")
        k_stored, v_stored = sem("k_stored"), sem("v_stored")
        y_ready, y_full = sem("y_ready"), sem("y_full")
        y_copied = [sem("y_copied0"), sem("y_copied1")]
        factor_raw, factor_ready = sem("factor_raw"), sem("factor_ready")
        y_stored, tail_stored = sem("y_stored"), sem("tail_stored")

        def by_rows(w):
            return w.rearrange("(k p) n -> p k n", p=P)

        w_in, w_out = by_rows(A["w_mlstm_in"][0]), by_rows(A["w_mlstm_out"][0])
        w_kv, w_q, w_o = by_rows(A["w_kv"]), by_rows(A["w_sb_q"][0]), by_rows(A["w_sb_o"][0])
        w_up = [by_rows(A["w_ffn_up"][l]) for l in range(2)]
        w_down = [by_rows(A["w_ffn_down"][l]) for l in range(2)]
        K_COL, V_COL = H * DK, 2 * H * DK
        O_COL = V_COL + H * DV
        G_COL = O_COL + D

        def ds(start, size=1):
            return slice(start, start + size) if isinstance(start, int) else bass.ds(start, size)

        def fb(ap):
            return ap.bitcast(F32)

        def tile_of(buf, m):
            return buf[:, ds(m), :].rearrange("p a n -> p (a n)")

        def slot(u):
            return slots[u.slot]

        def halves(u):
            return slot(u)[:, :].rearrange("p (b n) -> p b n", b=2)[:, :, 0:HALF]

        def two(ap):
            return ap.rearrange("p (b n) -> p b n", b=2)

        def apart(eng):
            eng.sem_inc(passed, 1)

        def full(eng, u):
            eng.wait_ge(out_full, u.at(1))

        def copied(eng, u):
            eng.wait_ge(out_free[u.slot], u.turn(2))

        def stepwise(eng, n, body, peel=0):
            turns = n // 2 - peel
            with eng.Fori(0, turns) as i:
                for e in range(2):
                    body(Pos(e, i, 2))
            for s in range(2 * turns, n):
                body(Pos(s))

        def x_use(m):
            return Pos(m if m < PAR_USE else m + 1)

        def scaled(phase, which, s, per=1, k=0):
            return Pos(AT[phase][which] + s.const * per + k, s.i, s.stride * per)

        def B(phase, s, per=1, k=0):
            return scaled(phase, 0, s, per, k)

        def U(phase, s, per=1, k=0):
            return scaled(phase, 1, s, per, k)

        def in_pos(i):
            return Pos(AT["in"][0], i, IN_BLOCKS), Pos(AT["in"][1], i, IN_USES)

        (U_K, U_V0, U_V1, U_V0T, U_Q, U_KT, U_V1T, U_O0, U_NUM0, U_DEN0, U_O1, U_SSQ0, U_NUM1, U_DEN1, U_STATE,
         U_SSQ1) = range(IN_USES)
        U_O, U_NUM, U_DEN, U_SSQ = (U_O0, U_O1), (U_NUM0, U_NUM1), (U_DEN0, U_DEN1), (U_SSQ0, U_SSQ1)

        S_K, S_VT, S_CKT, S_Q, S_KT, S_AV, S_V = range(7)
        FIRST_STEP = (S_K, S_Q, S_CKT, S_KT, S_V)

        def att_use(s, which):
            at = 7 * s.const - 2 + which if s.const else FIRST_STEP.index(which)
            return Pos(AT["kvq"][1] + at, s.i, 7 * s.stride)

        LAST_VT = att_use(Pos(H), 0)

        def att_steps(eng, body):
            body(Pos(0), None)
            with eng.Fori(0, PAIRS - 1) as i:
                body(Pos(1, i, 2), Pos(0, i, 2))
                body(Pos(2, i, 2), Pos(1, i, 2))
            body(Pos(H - 1), Pos(H - 2))
            body(None, Pos(H - 1))

        block = ctx.enter_context(nc.Block())

        @block.sync
        def _(dma):
            def load_block(b, src, nk=KT):
                dma.wait_ge(w_split, b.at(1))
                apart(dma)
                dma.dma_start(wraw[:, b.slot, 0:nk, :], src).then_inc(w_loaded[b.slot], 16)

            dma.dma_start(xtok[:, 0:4, 0:D // 2],
                          A["x_prompt"][0].rearrange("(t p) d -> p t d", p=P)[:, :, 0:D // 2]).then_inc(x_loaded, 16)
            dma.dma_start(xtok[0:TS, 4, :], A["x_sample"][0]).then_inc(x_loaded, 16)
            dma.dma_start(xtok[:, 0:4, D // 2:D],
                          A["x_prompt"][0].rearrange("(t p) d -> p t d", p=P)[:, :, D // 2:D]).then_inc(x2_loaded, 16)
            for at, src, n in ((0, G_COL, 2 * H), (2 * H, G_COL, 2 * H), (G_LF, G_COL + H, H)):
                dma.dma_start(graw[:, :, at:at + n], w_in[:, :, src:src + n]).then_inc(g_loaded, 16)

            with dma.Fori(0, PAIRS) as i:
                b, _ = in_pos(i)
                load_block(b.plus(0), w_in[:, :, ds(i * P + K_COL, P)])
                load_block(b.plus(1), w_in[:, :, ds(i * (2 * P) + V_COL, P)])
                load_block(b.plus(2), w_in[:, :, ds(i * (2 * P) + (V_COL + P), P)])
                load_block(b.plus(3), w_in[:, :, ds(i * P, P)])
                load_block(b.plus(4), w_in[:, :, ds(i * (2 * P) + O_COL, P)])
                dma.wait_ge(h_split, i * 2 + 1)
                dma.wait_ge(rows_stored, 48)
                for e in range(2):
                    dma.dma_start(gb[:, e, :], rows_d[ds(i * 2 + e), :].broadcast_to([P, T])).then_inc(pair_loaded, 16)
                    dma.dma_start(eb[:, e, :], rows_d[ds(i * 2 + (e + H)), :].broadcast_to([P, T])).then_inc(pair_loaded, 16)
                    dma.dma_start(wint[e * DK:(e + 1) * DK, :],
                                  wint_d[ds(i * 2 + e), :].broadcast_to([DK, TS])).then_inc(pair_loaded, 16)
                dma.dma_start(c0s[:, :], A["state_mlstm_c"].rearrange("l b h k v -> (l b h k) v")[ds(i * P, P), :]
                              ).then_inc(pair_loaded, 16)
                load_block(b.plus(5), w_in[:, :, ds(i * (2 * P) + (O_COL + P), P)])

            def load_square(phase, w):
                stepwise(dma, KT, lambda s: load_block(B(phase, s), w[:, :, ds(s.at(0, P), P)]))

            def load_ffn(layer):
                done = 0
                for t, n in enumerate(THIRDS):
                    up, down = ("up", layer, t), ("down", layer, t)

                    def load_up(s):
                        load_block(B(up, s, 2, 0), w_up[layer][:, :, ds(s.at(done, P), P)])
                        load_block(B(up, s, 2, 1), w_up[layer][:, :, ds(s.at(done + FT, P), P)])

                    stepwise(dma, n, load_up)
                    stepwise(dma, KT, lambda s: load_block(
                        B(down, s), w_down[layer][:, done:done + n, ds(s.at(0, P), P)], n))
                    done += n

            load_square("out", w_out)
            load_ffn(0)

            def load_head(s, c):
                if s is None:
                    return
                e = s.const % 2
                head = ds(s.at(0, P), P)
                cache = [A[name][0].rearrange("(t p) h d -> p t (h d)", p=P) for name in ("cache_k", "cache_v")]
                uses = AT["kvq"][1] + 7 * s.const
                load_block(B("kvq", s, 3, 0), w_kv[:, :, head])
                load_block(B("kvq", s, 3, 1), w_q[:, :, head])
                dma.wait_ge(out_full, Pos(uses - 4, s.i, 7 * s.stride).at(0))
                dma.dma_start(ck[:, :, :], cache[0][:, :, head]).then_inc(ck_loaded, 16)
                dma.wait_ge(out_full, Pos(uses - 3, s.i, 7 * s.stride).at(0))
                dma.dma_start(cv[:, e, :, :], cache[1][:, :, head]).then_inc(cv_loaded[e], 16)
                load_block(B("kvq", s, 3, 2), w_kv[:, :, ds(s.at(KT, P), P)])

            att_steps(dma, load_head)
            load_square("o", w_o)
            load_ffn(1)
            for t in range(5):
                if t < 2:
                    dma.wait_ge(y_copied[t], 1)
                else:
                    copied(dma, Pos(AT["end"][1] + t))
                if t < 4:
                    dma.dma_start(O["y_p"][0, t * P:(t + 1) * P, :], ytok[:, t, :]).then_inc(y_stored, 16)
                else:
                    dma.dma_start(O["y_s"][0, :, :], ytok[0:TS, t, :]).then_inc(y_stored, 16)
            dma.wait_ge(y_stored, 5 * 16)

        @block.tensor
        def _(pe):
            mm = nc.tensor.matmul

            def take(u):
                pe.wait_ge(out_free[u.slot], u.turn(1))

            def product(b, u, rh, rl, tiles=None, nk=KT, lh=whi, ll=wlo, rows=P, ks=None):
                ks = range(nk) if ks is None else ks
                if ks[0] == 0:
                    take(u)
                    if b is not None:
                        pe.wait_ge(w_split, b.at(3))
                for k in ks:
                    if tiles is not None:
                        tiles(k)
                    hi = lh[:, b.slot, k, :] if b is not None else lh[:, k, :]
                    lo = ll[:, b.slot, k, :] if b is not None else ll[:, k, :]
                    for half in range(2):
                        out = slot(u)[0:rows, half * BANK:half * BANK + HALF]
                        cols = slice(half * HALF, (half + 1) * HALF)
                        mm(out, hi, rh[:, k, cols], start=(k == 0), stop=False)
                        mm(out, hi, rl[:, k, cols], start=False, stop=False)
                        last = mm(out, lo, rh[:, k, cols], start=False, stop=(k == nk - 1))
                return last

            def weights_product(b, u, rh, rl, tiles=None, nk=KT):
                product(b, u, rh, rl, tiles, nk).then_inc(out_full, 1)

            def norm_stats(n):
                pe.wait_ge(x_summed, 9 * n + 10)
                mm(Z[:, 0:TP], mean_d[:, :], ssq[:, 0:TP], start=True, stop=True)
                mm(Z[:, TP:T], mean_d[:, :], ssq[:, TP:T], start=True, stop=True).then_inc(ms_full, 1)

            def x_tiles(n):
                return lambda k: pe.wait_ge(x_split, KT * n + k + 1)

            def x_tiles_and_stats(n):
                def tiles(k):
                    x_tiles(n)(k)
                    if k == KT - 1:
                        norm_stats(n)
                return tiles

            pe.wait_ge(consts_ready, 1)
            def parameters(use, tiles, first):
                take(Pos(use))
                at = 0
                for tile, n in enumerate(tiles):
                    last = nc.tensor.transpose(slot(Pos(use))[:, at:at + n], prow[0:n, first + tile, :], ident[0:n, 0:n])
                    at += n
                last.then_inc(out_full, 1)

            pe.wait_ge(x_loaded, 32)
            for m in range(KT):
                u = x_use(m)
                if m == PAR_USE:
                    pe.wait_ge(prow_loaded, 6 * 16)
                    parameters(PAR_USE, (C_CONV,), 0)
                if m == KT // 2:
                    pe.wait_ge(x2_loaded, 16)
                take(u)
                for t in range(5):
                    n = P if t < 4 else TS
                    last = nc.tensor.transpose(slot(u)[:, t * P:t * P + n], xtok[0:n, t, m * P:(m + 1) * P],
                                               ident[0:n, 0:n])
                last.then_inc(out_full, 1)
            pe.wait_ge(conv_loaded, 5 * 16)
            parameters(CONV_USE, (CONV_ROWS, CONV_ROWS, 88), 1)
            pe.wait_ge(g_split, 1)
            product(None, Pos(GATES_USE), xh, xl, x_tiles(0), lh=ghi, ll=glo, rows=G_ROWS).then_inc(out_full, 1)
            norm_stats(0)

            def by_tokens(to, src, n=5):
                take(to)
                for t in range(n):
                    w = P if t < 4 else TS
                    last = nc.tensor.transpose(slot(to)[0:w, t * P:(t + 1) * P], src[:, t * P:t * P + w], ident[:, :])
                last.then_inc(out_full, 1)

            with pe.Fori(0, PAIRS) as i:
                b, u = in_pos(i)
                for k, use in enumerate((U_K, U_V0, U_V1)):
                    weights_product(b.plus(k), u.plus(use), xh, xl)
                copied(pe, u.plus(U_V0))
                by_tokens(u.plus(U_V0T), vf[:, 0, :])
                weights_product(b.plus(3), u.plus(U_Q), xh, xl)
                copied(pe, u.plus(U_K))
                by_tokens(u.plus(U_KT), kf)
                pe.wait_ge(sdec_ready, i * 2 + 1)
                pe.wait_ge(gate_act, 5)
                apart(pe)
                for g, src in enumerate((ga, gwin)):
                    for t in range(5):
                        n = P if t < 4 else TS
                        last = nc.tensor.transpose(Z[0:n, (g * 5 + t) * H:(g * 5 + t + 1) * H],
                                                   src[:, t * P:t * P + n], ident[0:H, 0:H])
                last.then_inc(gT_full, 1)
                copied(pe, u.plus(U_V1))
                by_tokens(u.plus(U_V1T), vf[:, 1, :])
                for e in range(2):
                    rows = slice(e * DK, (e + 1) * DK)
                    pe.wait_ge(sdec_ready, i * 2 + (e + 1))
                    pe.wait_ge(cols_ready, i + 1)
                    pe.wait_ge(pads_ready, 2)
                    copied(pe, u.plus(U_Q))
                    for j in range(4):
                        mm(Zb[:, j, 0:TP - P * j], kf[rows, j * P:(j + 1) * P], qf[rows, j * P:TP],
                           start=True, stop=(j < 3))
                    mm(Zb[:, 3, P:P + TS], kf[rows, TP:TP + P], qf[rows, TP:T], start=False,
                       stop=True).then_inc(s_full, 1)
                    weights_product(b.plus(4 + e), u.plus(U_O[e]), xh, xl)
                    if e == 1:
                        to = u.plus(U_SSQ[0])
                        take(to)
                        pe.wait_ge(num_squared, i * 2 + 1)
                        mm(slot(to)[:, 0:TP], mean_v[:, :], nsq[:, 0:TP], start=True, stop=True)
                        mm(slot(to)[:, TP:T], mean_v[:, :], nsq[:, TP:T], start=True, stop=True).then_inc(out_full, 1)
                    pe.wait_ge(sdec_ready, i * 2 + (e + 2))
                    if e == 0:
                        copied(pe, u.plus(U_V0T))
                    pe.wait_ge(qw_ready, i + 1)
                    to = u.plus(U_NUM[e])
                    take(to)
                    for j in range(4):
                        mm(slot(to)[:, j * P:TP], vtok[:, j, e * DV:(e + 1) * DV], sdec[:, j, 0:TP - P * j],
                           start=(j == 0), stop=(j == 3))
                    mm(slot(to)[:, TP:T], vtok[:, 4, e * DV:(e + 1) * DV], sdec[:, 3, P:P + TS], start=True, stop=False)
                    mm(slot(to)[:, TP:T], c0s[rows, :], qw[rows, :], start=False, stop=True).then_inc(out_full, 1)
                    to = u.plus(U_DEN[e])
                    take(to)
                    pe.wait_ge(den_summed, i * 2 + (e + 1))
                    mm(slot(to)[:, 0:TP], ones[:, :], dsum[:, :], start=True, stop=True)
                    mm(slot(to)[:, TP:T], ones[:, :], sdec[:, 3, P:P + TS], start=True, stop=False)
                    mm(slot(to)[:, TP:T], n0b[rows, :], qw[rows, :], start=False, stop=True).then_inc(out_full, 1)
                to = u.plus(U_STATE)
                take(to)
                copied(pe, u.plus(U_KT))
                for j in range(4):
                    mm(slot(to)[:, 0:2 * DV + 1], kw[:, j, :], vtok[:, j, :], start=(j == 0), stop=(j == 3))
                mm(slot(to)[:, BANK:BANK + 2 * DV + 1], kw[0:TS, 4, :], vtok[0:TS, 4, :], start=True,
                   stop=True).then_inc(out_full, 1)
                to = u.plus(U_SSQ[1])
                take(to)
                pe.wait_ge(num_squared, i * 2 + 2)
                mm(slot(to)[:, 0:TP], mean_v[:, :], nsq[:, 0:TP], start=True, stop=True)
                mm(slot(to)[:, TP:T], mean_v[:, :], nsq[:, TP:T], start=True, stop=True).then_inc(out_full, 1)

            def square(phase, tiles, between=None, before_last=None):
                def part(m, first, end):
                    return product(B(phase, Pos(m)), U(phase, Pos(m)), hh, hl, None if m else tiles,
                                   ks=range(first, end))

                part(0, 0, KT - 1)
                if between is not None:
                    between()
                part(1, 0, KT // 2)
                if before_last is not None:
                    before_last()
                part(0, KT - 1, KT).then_inc(out_full, 1)
                part(1, KT // 2, KT).then_inc(out_full, 1)
                with pe.Fori(0, KT // 2 - 1) as i:
                    for e in range(2):
                        s = Pos(2 + e, i, 2)
                        weights_product(B(phase, s), U(phase, s), hh, hl)

            def h_tiles(base):
                return lambda k: pe.wait_ge(h_split, 1 + base + k + 1)

            def ffn_products(layer, n, hbase):
                done = 0
                for t, nt in enumerate(THIRDS):
                    up, down = ("up", layer, t), ("down", layer, t)

                    def up_pair(s):
                        first = t == 0 and s.i is None and s.const == 0
                        weights_product(B(up, s, 2, 0), U(up, s, 2, 0), xh, xl, x_tiles_and_stats(n) if first else None)
                        weights_product(B(up, s, 2, 1), U(up, s, 2, 1), xh, xl)

                    first = 2 if t == 0 else 0
                    for f in range(first):
                        up_pair(Pos(f))
                    with pe.Fori(0, (nt - first) // 2) as i:
                        for e in range(2):
                            up_pair(Pos(first + e, i, 2))
                    stepwise(pe, KT, lambda s: weights_product(
                        B(down, s), U(down, s), hh, hl, h_tiles(hbase + done) if s.const == 0 else None, nt))
                    done += nt

            square("out", h_tiles(0))
            ffn_products(0, 1, H)

            def scores(s):
                if s.const:
                    pe.wait_ge(log_ready, s.at(0))
                else:
                    pe.wait_ge(rstd_ready, 1)
                    copied(pe, att_use(s, S_CKT))
                copied(pe, att_use(s, S_Q))
                for j in range(4):
                    mm(Zb[:, j, 0:TP - P * j], kfa[:, j * P:(j + 1) * P], qfa[:, j * P:TP],
                       start=True, stop=(j < 3))
                for j in range(4):
                    mm(Zb[:, 3, P + j * TS:P + (j + 1) * TS], ckT[:, j * P:(j + 1) * P], qfa[:, TP:T],
                       start=False, stop=False)
                mm(Zb[:, 3, P + 4 * TS:P + 5 * TS], kfa[:, TP:TP + P], qfa[:, TP:T], start=False,
                   stop=True).then_inc(z_full, 1)

            def keep_sums(c):
                pe.wait_ge(z_kept, c.at(1))
                pe.wait_ge(sp_split, c.at(1))
                for j in range(4):
                    for n, part in enumerate((sph, spl)):
                        for jp in range(j, 4):
                            mm(Zb[:, j, (jp - j) * P:TP - P * j], (neg_tri_r if jp == j else neg_one_r)[:, :],
                               part[:, jp, 0:TP - P * jp], start=(n == 0 and jp == j), stop=(j < 3 and n == 1 and jp == 3))
                target = Zb[:, 3, P:P + 5 * TS].rearrange("p (j n) -> p j n", j=5)
                for n, part in enumerate((sph, spl)):
                    late_keys = part[:, 3, P:P + 5 * TS].rearrange("p (j n) -> p j n", j=5)
                    mm(target, neg_tri_r[:, :], late_keys, start=False, stop=False)
                    for jp in range(1, 5):
                        last = mm(target[:, 0:jp, :], neg_one_r[:, :],
                                  late_keys[:, jp:jp + 1, :].broadcast_to([P, jp, TS]), start=False,
                                  stop=(n == 1 and jp == 4))
                last.then_inc(log_full, 1)

            def values(c, out, done):
                e = c.const % 2
                pe.wait_ge(prob_ready, c.at(1))
                pe.wait_ge(cv_loaded[e], c.turn(1, 16))
                for j in range(4):
                    mm(out[:, j * P:TP], vta[:, j, :], prob[:, j, 0:TP - P * j], start=(j == 0), stop=(j == 3))
                for j in range(4):
                    mm(out[:, TP:T], cv[:, e, j, :], prob[:, 3, P + j * TS:P + (j + 1) * TS],
                       start=(j == 0), stop=False)
                mm(out[:, TP:T], vta[:, 4, :], prob[:, 3, P + 4 * TS:P + 5 * TS], start=False,
                   stop=True).then_inc(done, 1)

            def att_step(s, c):
                if s is None:
                    copied(pe, att_use(last_head, S_V))
                    by_tokens(LAST_VT, vfa)
                    return
                weights_product(B("kvq", s, 3, 0), att_use(s, S_K), xh, xl, x_tiles_and_stats(2) if c is None else None)
                if c is not None:
                    by_tokens(att_use(s, S_VT), vfa)
                    keep_sums(c)
                else:
                    weights_product(B("kvq", s, 3, 1), att_use(s, S_Q), xh, xl)
                to = att_use(s, S_CKT)
                take(to)
                pe.wait_ge(ck_loaded, s.at(1, 16))
                for t in range(4):
                    last = nc.tensor.transpose(slot(to)[:, t * P:(t + 1) * P], ck[:, t, :], ident[:, :])
                last.then_inc(out_full, 1)
                if c is not None:
                    weights_product(B("kvq", s, 3, 1), att_use(s, S_Q), xh, xl)
                by_tokens(att_use(s, S_KT), kfa)
                scores(s)
                if c is not None:
                    take(att_use(s, S_AV))
                    values(c, slot(att_use(s, S_AV)), out_full)
                weights_product(B("kvq", s, 3, 2), att_use(s, S_V), xh, xl)

            last_head = Pos(H - 1)
            pe.wait_ge(negs_ready, 2)
            att_steps(pe, att_step)

            def heads(k):
                if k == H - 2:
                    copied(pe, att_use(last_head, S_AV))
                if k == H - 1:
                    pe.wait_ge(last_split, 1)

            square("o", heads,
                   between=lambda: keep_sums(last_head), before_last=lambda: values(last_head, Z, last_full))
            ffn_products(1, 3, H + FT)

            u = Pos(AT["end"][1])
            take(u)
            pe.wait_ge(rows_taken, 2 * FT + 1)
            for l in range(2):
                nc.tensor.transpose(slot(u)[0:88, l * P:(l + 1) * P],
                                    conv_rows[:, l, :, :, :].rearrange("p g r t -> p (g r t)"), ident[:, :])
            nc.tensor.transpose(slot(u)[0:8, 2 * P:3 * P], nall[:, :, :].rearrange("p g i -> p (g i)"),
                                ident[:, :]).then_inc(out_full, 1)
            def result(t, out):
                w = P if t < 4 else TS
                for m in range(KT):
                    last = nc.tensor.transpose(out[0:w, m * P:(m + 1) * P], yT[:, m, t * P:t * P + w], ident[:, :])
                return last

            pe.wait_ge(y_ready, KT)
            result(0, Z[:, 0:D]).then_inc(y_full, 1)
            u = Pos(AT["end"][1] + 1)
            take(u)
            pe.wait_ge(x_summed, 9 * 4 + 10)
            mm(slot(u)[:, 4:5], ssq[:, 0:P], mean_d[:, 0:1], start=True, stop=True)
            for t in range(5):
                w = P if t < 4 else TS
                last = mm(slot(u)[0:w, t:t + 1], ssq[:, t * P:t * P + w], mean_d[:, 0:1], start=True, stop=True)
            last.then_inc(out_full, 1)
            result(1, Z[:, D:2 * D]).then_inc(y_full, 1)
            for t in range(2, 5):
                u = Pos(AT["end"][1] + t)
                take(u)
                result(t, slot(u)).then_inc(out_full, 1)

        @block.vector
        def _(dve):
            v = nc.vector
            chain = Chain(dve, chain_dve)
            dve.sem_inc(w_split, 2)
            dve.sem_inc(sdec_ready, 1)
            dve.sem_inc(h_split, 1)
            dve.sem_inc(conv_ready, 1)
            for s in range(2):
                dve.sem_inc(out_free[s], 1)

            def split(b, gain=None):
                if b.i is None and b.const >= LAST_BLOCK:
                    return
                raw = wraw[:, b.slot, :, :]
                dve.wait_ge(w_loaded[b.slot], b.turn(1, 16))
                if gain is not None:
                    v.tensor_tensor(raw, raw, par[:, gain:gain + KT].unsqueeze(2).broadcast_to([P, KT, P]),
                                    ALU.mult).then_inc(w_gained, 1)
                    dve.wait_ge(w_gained, Pos(b.const - AT["kvq"][0], b.i, b.stride).at(1))
                v.tensor_copy(whi[:, b.slot, :, :], raw).then_inc(w_high, 1)
                dve.wait_ge(w_high, b.at(1))
                v.tensor_tensor(wlo[:, b.slot, :, :], raw, fb(whi[:, b.slot, :, :]), ALU.subtract).then_inc(w_split, 1)

            def replace(b, gain=None):
                split(b.plus(2), gain)

            def norm_split(ev, m, gain):
                dve.wait_ge(x_high, ev.at(1))
                lo, xm, hi = tile_of(xl, m), tile_of(x, m), fb(tile_of(xh, m))
                if gain is None:
                    ins = v.tensor_tensor(lo, xm, hi, ALU.subtract)
                else:
                    ins = v.scalar_tensor_tensor(out=lo, in0=xm, scalar=gain, in1=hi,
                                                 op0=ALU.mult, op1=ALU.subtract)
                ins.then_inc(x_split, 1)

            def norm_factor(n):
                dve.wait_ge(rstd_raw, n + 1)
                chain.link(v.tensor_tensor(rstd_q[:, :], nr, nr, ALU.mult))
                chain.link(v.scalar_tensor_tensor(out=rstd_q[:, :], in0=Z[:, 0:T], scalar=EPS, in1=rstd_q[:, :],
                                                  op0=ALU.add, op1=ALU.mult))
                chain.link(v.tensor_scalar(rstd_q[:, :], rstd_q[:, :], -0.5, 1.5, ALU.mult, ALU.add))
                chain.link(v.tensor_tensor(rstd[:, :], nr, rstd_q[:, :], ALU.mult))

            def query_factor(scale):
                chain.link(v.tensor_scalar(rstd_q[:, :], rstd[:, :], scale, None, ALU.mult))

            def factored(u, out, factor=rstd):
                full(dve, u)
                v.tensor_tensor(two(out), halves(u), two(factor[:, :]), ALU.mult).then_inc(out_free[u.slot], 1)

            v.memset(Z[:, :], 0.0)
            for m in range(KT + 1):
                if m == PAR_USE:
                    full(dve, Pos(PAR_USE))
                    v.tensor_copy(par[:, 0:C_CONV], slots[0][:, 0:C_CONV]).then_inc(out_free[0], 1)
                    copied(dve, Pos(PAR_USE))
                    chain.link(v.tensor_scalar(out_half[:, :], par[:, C_OUT:C_OUT + KT], 0.5, None, ALU.mult))
                if m == PAR_USE:
                    dve.wait_ge(consts_ready, 1)
                    v.tensor_scalar(neg_one_r[:, :], ones[:, :], -1.0, None, ALU.mult).then_inc(negs_ready, 1)
                    v.tensor_copy(neg_tri_r[:, :], neg_tri[:, :]).then_inc(negs_ready, 1)
                    dve.wait_ge(g_loaded, 48)
                    v.tensor_copy(ghi[:, :, :], graw[:, :, :]).then_inc(g_high, 1)
                    dve.wait_ge(g_high, 1)
                    v.tensor_tensor(glo[:, :, :], graw[:, :, :], fb(ghi[:, :, :]), ALU.subtract).then_inc(g_split, 1)
                if m < KT:
                    u = x_use(m)
                    full(dve, u)
                    v.tensor_copy(x[:, m, :], slot(u)[:, 0:T]).then_inc(out_free[u.slot], 1)
                if m >= PAR_USE:
                    done = m - PAR_USE
                    norm_split(Pos(done), done, par[:, C_MIX + done:C_MIX + done + 1])
            norm_split(Pos(KT - 1), KT - 1, par[:, C_MIX + KT - 1:C_MIX + KT])
            u = Pos(CONV_USE)
            full(dve, u)
            v.tensor_copy(par[:, C_CONV:C_ALL], slot(u)[:, 0:C_ALL - C_CONV]).then_inc(out_free[u.slot], 1)
            split(Pos(0))
            split(Pos(1))
            norm_factor(0)

            u = Pos(GATES_USE)
            gstep = [0]

            def gate(ins):
                gstep[0] += 1
                ins.then_inc(gate_dve, 1)
                dve.wait_ge(gate_dve, gstep[0])

            dve.wait_ge(gbias_loaded, 48)
            gate(v.tensor_scalar(gbias[:, :], gbias[:, :], 1.0 / CAP, None, ALU.mult))
            gate(v.memset(ones8[:, :], 1.0))
            full(dve, u)
            v.tensor_tensor(two(gth[:, :]), halves(u)[0:G_ROWS], two(rstd[0:G_ROWS, :]),
                            ALU.mult).then_inc(out_free[u.slot], 1)
            query_factor(DK ** -0.5)

            def pair_in(b, u, which):
                use = u.plus((U_K, U_V0, U_V1)[which])
                factored(use, vf[:, which - 1, :] if which else kf[:, 0:T])
                replace(b.plus(which))

            pair_in(*in_pos(0), 0)
            dve.wait_ge(gate_act, 2)
            groups = ((0, TP), (TP, T))
            for a, z in groups:
                gate(v.tensor_tensor_scan(nb[:, a:z], ones8[:, a:z], nlf[:, a:z], 0.0, ALU.mult, ALU.add))
            gate(v.scalar_tensor_tensor(out=ga[:, :], in0=gth[G_LI:G_LI + H, :], scalar=CAP, in1=nb[:, :],
                                        op0=ALU.mult, op1=ALU.add))
            for (a, z), m0 in zip(groups, (NEG_BIG, gm0[:, 0:1])):
                gate(v.tensor_tensor_scan(gg[:, a:z], ones8[:, a:z], ga[:, a:z], m0, ALU.mult, ALU.max))
            gate(v.tensor_scalar(gneg[:, :], gg[:, :], -1.0, None, ALU.mult))
            gate(v.tensor_tensor(gem[:, :], nb[:, :], gg[:, :], ALU.subtract))
            for n, (a, z) in enumerate(groups):
                gate(v.tensor_tensor(gm[:, n:n + 1], gg[:, z - 1:z], nb[:, z - 1:z], ALU.subtract))
            pair_in(*in_pos(0), 1)
            pair_in(*in_pos(0), 2)

            def pair_rest(i):
                b, u = in_pos(i)
                v.tensor_scalar(n0b[:, :], ones[:, :], par[:, ds(i + C_N0)], None, ALU.mult)
                factored(u.plus(U_Q), qf[:, :], rstd_q)
                dve.wait_ge(gT_full, i + 1)
                for g, dst in enumerate((acol, wcol)):
                    src = Z[:, g * 5 * H:(g + 1) * 5 * H].rearrange("p (t h) -> p t h", h=H)
                    v.tensor_copy(dst[:, 0:4, :], src[:, 0:4, ds(i * 2, 2)])
                    last = v.tensor_copy(dst[0:TS, 4:5, :], src[0:TS, 4:5, ds(i * 2, 2)])
                last.then_inc(cols_ready, 1)
                to = u.plus(U_KT)
                full(dve, to)
                dve.wait_ge(cols_ready, i + 1)
                for rows, t0, t1 in ((P, 0, 4), (TS, 4, 5)):
                    last = v.tensor_tensor(
                        kw[0:rows, t0:t1, :].rearrange("p t (e k) -> p t e k", e=2),
                        slot(to)[0:rows, t0 * P:t1 * P].rearrange("p (t e k) -> p t e k", e=2, k=DK),
                        wcol[0:rows, t0:t1, :].unsqueeze(3).broadcast_to([rows, t1 - t0, 2, DK]), ALU.mult)
                last.then_inc(out_free[to.slot], 1)
                replace(b.plus(3))
                dve.wait_ge(pair_loaded, i * (7 * 16) + 7 * 16)
                copied(dve, u.plus(U_Q))
                v.tensor_tensor(qw[:, :], qf[:, TP:T], wint[:, :], ALU.mult).then_inc(qw_ready, 1)

                def mean_square(e):
                    to = u.plus(U_SSQ[e])
                    full(dve, to)
                    dve.wait_ge(den_squared, i * 2 + (e + 1))
                    v.tensor_tensor(inv[:, :], slot(to)[:, 0:T], inv[:, :], ALU.add).then_inc(out_free[to.slot], 1)

                def normalise(e):
                    dve.wait_ge(inv_ready, i * 2 + (e + 1))
                    v.tensor_tensor(hm[:, :], num[:, e, :], inv[:, :], ALU.mult).then_inc(hm_ready, 1)
                    dve.wait_ge(hm_ready, i * 4 + (2 * e + 1))
                    v.scalar_tensor_tensor(out=hm[:, :], in0=tg[:, e, :], scalar=1.0, in1=hm[:, :], op0=ALU.add,
                                           op1=ALU.mult).then_inc(hm_ready, 1)

                def low(e):
                    dve.wait_ge(hm_ready, i * 4 + (2 * e + 2))
                    dve.wait_ge(h_high, i * 2 + (e + 1))
                    v.scalar_tensor_tensor(out=tile_of(hl, i * 2 + e), in0=hm[:, :], scalar=out_half[:, ds(i * 2 + e)],
                                           in1=fb(tile_of(hh, i * 2 + e)), op0=ALU.mult,
                                           op1=ALU.subtract).then_inc(h_split, 1)

                for e in range(2):
                    dve.wait_ge(s_full, i * 2 + (e + 1))
                    dve.wait_ge(dec_ready, i * 2 + (e + 1))
                    for j in range(4):
                        n = TP - P * j if j < 3 else P + TS
                        last = v.tensor_tensor(sdec[:, j, 0:n], Zb[:, j, 0:n], dec[:, j, 0:n], ALU.mult)
                    last.then_inc(sdec_ready, 1)
                    dve.wait_ge(sdec_ready, i * 2 + (e + 2))
                    v.tensor_copy(dsum[:, 0:P], sdec[:, 0, 0:P])
                    chain.link(v.tensor_tensor(dsum[:, P:TP], sdec[:, 0, P:TP], sdec[:, 1, 0:TP - P], ALU.add))
                    chain.link(v.tensor_tensor(dsum[:, 2 * P:TP], dsum[:, 2 * P:TP], sdec[:, 2, 0:TP - 2 * P], ALU.add))
                    v.tensor_tensor(dsum[:, 3 * P:TP], dsum[:, 3 * P:TP], sdec[:, 3, 0:P],
                                    ALU.add).then_inc(den_summed, 1)
                    factored(u.plus(U_O[e]), tg[:, e, :])
                    replace(b.plus(4 + e))
                    if e == 1:
                        mean_square(0)
                    copied(dve, u.plus(U_DEN[e]))
                    v.tensor_tensor(dn[:, :], dn[:, :], eb[:, e, :], ALU.max).then_inc(den_ready, 1)
                to = u.plus(U_STATE)
                full(dve, to)
                dve.wait_ge(state_stored, i * 32 + 16)
                decay = wint[:, TS - 1:TS]
                for e in range(2):
                    rows = slice(e * DK, (e + 1) * DK)
                    v.tensor_copy(cst[rows, 0, :], slot(to)[rows, e * DV:(e + 1) * DV])
                    v.scalar_tensor_tensor(out=cst[rows, 1, :], in0=c0s[rows, :], scalar=decay[rows, :],
                                           in1=slot(to)[rows, BANK + e * DV:BANK + (e + 1) * DV], op0=ALU.mult,
                                           op1=ALU.add)
                v.tensor_copy(nall[:, 0, ds(i)], slot(to)[:, 2 * DV:2 * DV + 1])
                v.scalar_tensor_tensor(out=nall[:, 1, ds(i)], in0=n0b[:, 0:1], scalar=decay,
                                       in1=slot(to)[:, BANK + 2 * DV:BANK + 2 * DV + 1], op0=ALU.mult,
                                       op1=ALU.add).then_inc(out_free[to.slot], 1)
                normalise(0)
                low(0)
                mean_square(1)
                normalise(1)
                low(1)

            with dve.Fori(0, PAIRS - 1) as i:
                chain.enter(i, 4)
                pair_rest(i)
                b, u = in_pos(i)
                for which in range(3):
                    pair_in(b.plus(IN_BLOCKS), u.plus(IN_USES), which)
            chain.leave(PAIRS - 1)
            pair_rest(PAIRS - 1)

            def residual(phase, s, norm=None, gain=None, next_gain=None):
                u = U(phase, s)
                full(dve, u)
                xs = two(tile_of(x, s.at(0)))
                v.tensor_tensor(xs, halves(u), xs, ALU.add).then_inc(out_free[u.slot], 1)
                replace(B(phase, s), next_gain)
                if norm is not None and norm < 4:
                    norm_split(Pos(KT * norm + s.const, s.i, s.stride), s.at(0),
                               par[:, ds(s.at(gain))] if gain is not None else None)

            def ffn_tiles(layer, norm):
                done = 0
                for t, nt in enumerate(THIRDS):
                    first = 2 if t == 0 else 0
                    up, down = ("up", layer, t), ("down", layer, t)

                    def tile(s):
                        f = Pos(layer * FT + done + s.const, s.i, s.stride)
                        tap = Pos(C_CONV + layer * CONV_ROWS + done + s.const, s.i, s.stride)
                        ua, uv = U(up, s, 2, 0), U(up, s, 2, 1)
                        full(dve, ua)
                        starts = first and s.i is None and s.const == 0
                        if starts:
                            replace(B(up, s, 2, 0))
                            norm_factor(norm)
                        dve.wait_ge(rows_taken, f.at(1))
                        split_at = TP - HALF
                        v.tensor_tensor(ext[:, 2:2 + HALF], slot(ua)[:, 0:HALF], rstd[:, 0:HALF], ALU.mult)
                        v.tensor_tensor(ext[:, 2 + HALF:2 + TP], slot(ua)[:, BANK:BANK + split_at], rstd[:, HALF:TP],
                                        ALU.mult)
                        v.tensor_tensor(ext[:, 4 + TP:4 + T], slot(ua)[:, BANK + split_at:BANK + HALF], rstd[:, TP:T],
                                        ALU.mult).then_inc(out_free[ua.slot], 1)
                        if not starts:
                            replace(B(up, s, 2, 0))
                        copied(dve, ua)
                        dve.wait_ge(prev_ready, f.at(1))
                        chain.link(v.tensor_scalar(acc[:, :], ext[:, 0:T + 2], par[:, ds(tap.at(0))], None, ALU.mult))
                        chain.link(v.scalar_tensor_tensor(out=acc[:, :], in0=ext[:, 1:T + 3],
                                                          scalar=par[:, ds(tap.at(FT))], in1=acc[:, :],
                                                          op0=ALU.mult, op1=ALU.add))
                        v.scalar_tensor_tensor(out=acc[:, :], in0=ext[:, 2:T + 4], scalar=par[:, ds(tap.at(2 * FT))],
                                               in1=acc[:, :], op0=ALU.mult, op1=ALU.add).then_inc(conv_ready, 1)
                        factored(uv, val[:, :])
                        if starts:
                            replace(B(up, s, 2, 1))
                        copied(dve, uv)
                        dve.wait_ge(gelu_ready, f.at(1))
                        v.tensor_tensor(hid[:, :], gel[:, :], val[:, :], ALU.mult).then_inc(hid_ready, 1)
                        if not starts:
                            replace(B(up, s, 2, 1))
                        dve.wait_ge(hid_ready, f.at(1))
                        dve.wait_ge(h_high, f.at(1 + (H if layer == 0 else 2 * H)))
                        v.tensor_tensor(tile_of(hl, s.at(0)), hid[:, :], fb(tile_of(hh, s.at(0))), ALU.subtract).then_inc(h_split, 1)

                    for f in range(first):
                        tile(Pos(f))
                    with dve.Fori(0, (nt - first) // 2) as i:
                        chain.enter(i, 4)
                        for e in range(2):
                            tile(Pos(first + e, i, 2))
                    chain.leave((nt - first) // 2)
                    if t < 2:
                        stepwise(dve, KT, lambda s: residual(down, s))
                    else:
                        first_gain = {KT - 2: C_KV, KT - 1: C_MIX + KT}
                        stepwise(dve, KT, lambda s: residual(down, s, norm + 1, None, first_gain[s.const] if layer == 0
                                                             and s.i is None else None), peel=1)
                    done += nt

            stepwise(dve, KT, lambda s: residual("out", s, 1, C_FFN))
            v.memset(ext[:, 0:2], 0.0)
            ffn_tiles(0, 1)

            v.memset(kfa[:, T:5 * P], 0.0)
            v.memset(vta[TS:P, 4, :], 0.0).then_inc(rstd_ready, 1)

            def att_step(s, c):
                if s is not None:
                    last = s.i is None and s.const == H - 1
                    if c is None:
                        full(dve, att_use(s, S_K))
                        replace(B("kvq", s, 3, 0), C_KV)
                        norm_factor(2)
                    factored(att_use(s, S_K), kfa[:, 0:T])
                    if c is None:
                        query_factor(DH ** -0.5)
                    else:
                        replace(B("kvq", s, 3, 0), C_KV)
                if c is not None:
                    dve.wait_ge(log_full, c.at(1))
                    v.tensor_tensor(prob[:, :, :], prob[:, :, :], Zb[:, :, :], ALU.add).then_inc(log_ready, 1)
                if s is not None:
                    factored(att_use(s, S_Q), qfa[:, :], rstd_q)
                    replace(B("kvq", s, 3, 1), None if last else C_KV)
                    dve.wait_ge(z_abs, s.at(1))
                    if c is not None:
                        full(dve, att_use(s, S_AV))
                    v.tensor_copy(prob[:, :, :], Zb[:, :, :]).then_inc(z_kept, 1)
                if c is not None:
                    dve.wait_ge(h_high, c.at(1 + H + FT))
                    lo, hi = tile_of(hl, c.at(0)), fb(tile_of(hh, c.at(0)))
                    if s is None:
                        v.tensor_tensor(lo, Z[:, 0:T], hi, ALU.subtract).then_inc(last_split, 1)
                    else:
                        u = att_use(s, S_AV)
                        v.tensor_tensor(lo, slot(u)[:, 0:T], hi, ALU.subtract).then_inc(out_free[u.slot], 1)
                if s is not None:
                    dve.wait_ge(z_kept, s.at(1))
                    dve.wait_ge(z_log, s.at(1))
                    v.scalar_tensor_tensor(out=sp[:, :, :], in0=prob[:, :, :], scalar=0.0, in1=za[:, :, :], op0=ALU.max,
                                           op1=ALU.add).then_inc(sp_raw, 1)
                    factored(att_use(s, S_V), vfa[:, :])
                    dve.wait_ge(sp_masked, s.at(1))
                    v.tensor_copy(sph[:, :, :], sp[:, :, :]).then_inc(sp_high, 1)
                    dve.wait_ge(sp_high, s.at(1))
                    v.tensor_tensor(spl[:, :, :], sp[:, :, :], fb(sph[:, :, :]), ALU.subtract).then_inc(sp_split, 1)
                    replace(B("kvq", s, 3, 2), None if last else C_MIX + KT)

            att_steps(dve, att_step)
            stepwise(dve, KT, lambda s: residual("o", s, 3, C_FFN + KT))
            ffn_tiles(1, 3)
            dve.wait_ge(factor_raw, 1)
            mean_use = Pos(AT["end"][1] + 1)
            mean, raw, out = slot(mean_use)[:, 0:5], factor[:, 0, :], factor[:, 1, :]
            chain.link(v.tensor_tensor(out, raw, raw, ALU.mult))
            v.scalar_tensor_tensor(out=out, in0=mean, scalar=EPS, in1=out, op0=ALU.add,
                                   op1=ALU.mult).then_inc(out_free[mean_use.slot], 1)
            copied(dve, mean_use)
            chain.link(v.tensor_scalar(out, out, -0.5, 1.5, ALU.mult, ALU.add))
            v.tensor_tensor(out, raw, out, ALU.mult).then_inc(factor_ready, 1)
            dve.wait_ge(factor_ready, 1)
            dve.wait_ge(y_full, 2)
            v.tensor_scalar(ytok[:, 1, :], Z[:, D:2 * D], out[:, 1:2], None, ALU.mult).then_inc(y_copied[1], 1)
            u = Pos(AT["end"][1] + 3)
            full(dve, u)
            v.tensor_scalar(ytok[:, 3, :], slot(u)[:, :], out[:, 3:4], None, ALU.mult).then_inc(out_free[u.slot], 1)

        @block.scalar
        def _(act):
            a = nc.scalar.activation
            chain = Chain(act, chain_act)

            act.preload_act_table_set(LN_EXP)
            for at, name, dims, n in ((C_MIX, "g_mix_norm", "l (t p) -> (l t) p", 16),
                                      (C_OUT, "g_mlstm_out", "l (t p) -> (l t) p", 8),
                                      (C_KV, "g_kv_norm", "(t p) -> t p", 8),
                                      (C_FFN, "g_ffn_norm", "l (t p) -> (l t) p", 16),
                                      (C_FIN, "g_final", "(t p) -> t p", 8)):
                act.dma_start(prow[at:at + n, 0, :], A[name].rearrange(dims, p=P)).then_inc(prow_loaded, 16)
            act.dma_start(prow[C_N0:C_N0 + PAIRS, 0, :],
                          A["state_mlstm_n"].rearrange("l b (i e) k -> (l b i) (e k)", e=2)).then_inc(prow_loaded, 16)
            for l in range(2):
                act.dma_start(prow[0:3 * FT, 1 + l, :],
                              A["w_ffn_conv"][l].rearrange("i (t p) -> (i t) p", p=P)).then_inc(conv_loaded, 16)
                act.dma_start(prow[3 * FT:4 * FT, 1 + l, :],
                              A["b_ffn_conv"][l].rearrange("(t p) -> t p", p=P)).then_inc(conv_loaded, 16)
            act.dma_start(prow[0:4 * FT, 3, :],
                          A["state_ffn_conv"].rearrange("l b r (t p) -> (l b r t) p", p=P)).then_inc(conv_loaded, 16)
            act.wait_ge(pads_ready, 1)
            for at, src in ((G_LI, 0), (G_LF, H)):
                act.dma_start(gbias[at:at + H, :],
                              A["b_mlstm_gates"][0, src:src + H].unsqueeze(1)).then_inc(gbias_loaded, 16)
            act.dma_start(gm0[:, :], A["state_mlstm_m"][0, 0].unsqueeze(1)).then_inc(gbias_loaded, 16)
            act.wait_ge(consts_ready, 1)

            def norm_high(m, gain, u):
                copied(act, u)
                apart(act)
                a(tile_of(xh, m), tile_of(x, m), ACT.Copy, scale=1.0 if gain is None else gain).then_inc(x_high, 1)

            def norm_square(n, s, m, u):
                copied(act, u)
                act.wait_ge(x_summed, Pos(9 * n + s.const + 1, s.i, s.stride).at(0))
                apart(act)
                a(sq[:, s.const % 2, :], tile_of(x, m), ACT.Square).then_inc(x_square, 1)

            def norm_first(n):
                act.preload_act_table_set(LN_EXP)
                act.wait_ge(ms_full, n + 1)
                chain.link(a(nr, Z[:, 0:T], ACT.Ln, bias=eps[:, 0:1]))
                a(nr, nr, ACT.Exp, scale=-0.5).then_inc(rstd_raw, 1)

            for m in range(KT):
                norm_square(0, Pos(m), m, x_use(m))
                if m == PAR_USE - 1:
                    copied(act, Pos(PAR_USE))
                    norm_high(0, par[:, C_MIX:C_MIX + 1], x_use(0))
                if m >= PAR_USE - 1:
                    norm_high(m, par[:, C_MIX + m:C_MIX + m + 1], x_use(m))
            norm_first(0)
            act.wait_ge(gate_dve, 1)
            copied(act, Pos(GATES_USE))
            chain.link(a(gth[:, :], gth[:, :], ACT.Tanh, bias=gbias[:, 0:1], scale=1.0 / CAP))
            act.preload_act_table_set(LN_EXP)
            a(nlf[:, :], gth[G_LF:G_LF + H, :], ACT.Exp, scale=-CAP).then_inc(gate_act, 1)
            act.wait_ge(gate_act, 1)
            a(nlf[:, :], nlf[:, :], ACT.Ln, bias=1.0).then_inc(gate_act, 1)
            act.wait_ge(gate_dve, 8)
            a(gwint[:, :], gneg[:, TP:T], ACT.Exp, bias=gm0[:, 0:1]).then_inc(gate_act, 1)
            for lo_, hi_ in ((0, TP), (TP, T)):
                a(gwin[:, lo_:hi_], ga[:, lo_:hi_], ACT.Exp, bias=gneg[:, hi_ - 1:hi_]).then_inc(gate_act, 1)
            act.wait_ge(gate_dve, 9)
            a(gem[:, :], gem[:, :], ACT.Exp).then_inc(gate_act, 1)

            act.sem_inc(state_stored, 16)
            states = [O[k].rearrange("l b h k v -> (l b h k) v") for k in ("p_c", "s_c")]
            with act.Fori(0, PAIRS) as i:
                b, u = in_pos(i)
                chain.enter(i, 2)

                def decays(e):
                    act.wait_ge(pair_loaded, i * (7 * 16) + 7 * 16)
                    act.wait_ge(cols_ready, i + 1)
                    act.wait_ge(sdec_ready, i * 2 + (e + 1))
                    for j in range(4):
                        a(dec[:, j, 0:TP - P * j], gb[:, e, j * P:TP], ACT.Exp, bias=acol[:, j, e:e + 1])
                    a(dec[:, 3, P:P + TS], gb[:, e, TP:T], ACT.Exp, bias=acol[:, 4, e:e + 1]).then_inc(dec_exp, 1)

                def tanh_gate(e):
                    copied(act, u.plus(U_O[e]))
                    a(tg[:, e, :], tg[:, e, :], ACT.Tanh, scale=0.5).then_inc(tanh_ready, 1)

                def numerator(e):
                    to = u.plus(U_NUM[e])
                    full(act, to)
                    a(nsq[:, :], slot(to)[:, 0:T], ACT.Square).then_inc(num_squared, 1)
                    a(num[:, e, :], slot(to)[:, 0:T], ACT.Copy).then_inc(out_free[to.slot], 1)

                def denominator(e):
                    to = u.plus(U_DEN[e])
                    full(act, to)
                    a(dn[:, :], slot(to)[:, 0:T], ACT.Abs).then_inc(out_free[to.slot], 1)

                def den_square(e):
                    act.wait_ge(den_ready, i * 2 + (e + 1))
                    a(inv[:, :], dn[:, :], ACT.Square, scale=EPS ** 0.5).then_inc(den_squared, 1)

                def inverse(e):
                    copied(act, u.plus(U_SSQ[e]))
                    apart(act)
                    if e == 0:
                        act.preload_act_table_set(LN_EXP)
                    chain.link(a(inv[:, :], inv[:, :], ACT.Ln))
                    a(inv[:, :], inv[:, :], ACT.Exp, scale=-0.5).then_inc(inv_ready, 1)

                def high(e):
                    act.wait_ge(hm_ready, i * 4 + (2 * e + 2))
                    apart(act)
                    a(tile_of(hh, i * 2 + e), hm[:, :], ACT.Copy, scale=out_half[:, ds(i * 2 + e)]).then_inc(h_high, 1)

                def values_by_tokens(e):
                    to = u.plus(U_V1T if e else U_V0T)
                    full(act, to)
                    for rows, t0, t1 in ((P, 0, 4), (TS, 4, 5)):
                        last = a(vtok[0:rows, t0:t1, e * DV:(e + 1) * DV],
                                 slot(to)[0:rows, t0 * P:t1 * P].rearrange("p (t d) -> p t d", d=DV), ACT.Copy)
                    last.then_inc(out_free[to.slot], 1)

                values_by_tokens(0)
                values_by_tokens(1)
                decays(0)
                decays(1)
                tanh_gate(0)
                numerator(0)
                denominator(0)
                den_square(0)
                tanh_gate(1)
                numerator(1)
                denominator(1)
                inverse(0)
                high(0)
                den_square(1)
                copied(act, u.plus(U_STATE))
                for n in range(2):
                    act.dma_start(states[n][ds(i * P, P), :], cst[:, n, :]).then_inc(state_stored, 16)
                inverse(1)
                high(1)
            chain.leave(PAIRS)

            def norm_steps(phase, n, gain):
                def step(s):
                    u, m = U(phase, s), s.at(0)
                    if n < 4:
                        norm_high(m, par[:, ds(s.at(gain))] if gain is not None else None, u)
                    norm_square(n, s, m, u)
                    if n == 4:
                        a(tile_of(yT, m), tile_of(x, m), ACT.Copy, scale=par[:, ds(s.at(gain))]).then_inc(y_ready, 1)
                stepwise(act, KT, step)
                if n < 4:
                    norm_first(n)

            def ffn_tiles(layer):
                done = 0
                for t, nt in enumerate(THIRDS):
                    def tile(s):
                        f = Pos(layer * FT + done + s.const, s.i, s.stride)
                        bias = par[:, ds(Pos(C_CONV + layer * CONV_ROWS + 3 * FT + done + s.const, s.i, s.stride).at(0))]
                        act.wait_ge(conv_ready, f.at(2))
                        apart(act)
                        a(gel[:, 0:TP], acc[:, 0:TP], ACT.Gelu_apprx_tanh, bias=bias)
                        a(gel[:, TP:T], acc[:, TP + 2:T + 2], ACT.Gelu_apprx_tanh, bias=bias).then_inc(gelu_ready, 1)
                        act.wait_ge(hid_ready, f.at(1))
                        apart(act)
                        a(tile_of(hh, s.at(0)), hid[:, :], ACT.Copy).then_inc(h_high, 1)

                    stepwise(act, nt, tile)
                    done += nt

            norm_steps("out", 1, C_FFN)
            ffn_tiles(0)
            norm_steps(("down", 0, 2), 2, None)

            def by_tokens(to, dst):
                full(act, to)
                for rows, t0, t1 in ((P, 0, 4), (TS, 4, 5)):
                    last = a(dst[0:rows, t0:t1, :], slot(to)[0:rows, t0 * P:t1 * P].rearrange("p (t d) -> p t d", d=P),
                             ACT.Copy)
                last.then_inc(out_free[to.slot], 1)

            p_kv = [O[k][0].rearrange("(t p) h d -> p t (h d)", p=P) for k in ("p_k", "p_v")]
            s_kv = [O[k][0].rearrange("t h d -> t (h d)") for k in ("s_k", "s_v")]

            def store(n, s, u, rows, stored):
                copied(act, u)
                head = ds(s.at(0, P), P)
                act.dma_start(p_kv[n][:, :, head], rows[:, 0:4, :]).then_inc(stored, 16)
                act.dma_start(s_kv[n][:, head], rows[0:TS, 4, :]).then_inc(stored, 16)

            act.sem_inc(k_stored, 16)
            act.sem_inc(v_stored, 16)
            act.preload_act_table_set(LN_EXP)

            def att_step(s, c):
                if c is not None:
                    to = LAST_VT if s is None else att_use(s, S_VT)
                    act.wait_ge(v_stored, c.at(0, 32) + 16)
                    by_tokens(to, vta)
                    store(1, c, to, vta, v_stored)
                if s is not None:
                    to = att_use(s, S_CKT)
                    full(act, to)
                    a(ckT[:, :], slot(to)[:, 0:PAST], ACT.Copy).then_inc(out_free[to.slot], 1)
                if c is not None:
                    act.wait_ge(log_ready, c.at(1))
                    a(prob[:, :, :], prob[:, :, :], ACT.Exp).then_inc(prob_raw, 1)
                if s is not None:
                    act.wait_ge(k_stored, s.at(0, 32) + 16)
                    by_tokens(att_use(s, S_KT), ktok)
                    store(0, s, att_use(s, S_KT), ktok, k_stored)
                    act.wait_ge(z_full, s.at(1))
                    a(za[:, :, :], Zb[:, :, :], ACT.Abs).then_inc(z_abs, 1)
                    act.wait_ge(z_abs, s.at(1))
                    chain.link(a(za[:, :, :], za[:, :, :], ACT.Exp, scale=-1.0))
                if c is not None:
                    if s is None:
                        act.wait_ge(last_full, 1)
                    else:
                        full(act, att_use(s, S_AV))
                    apart(act)
                    out = Z if s is None else slot(att_use(s, S_AV))
                    a(tile_of(hh, c.at(0)), out[:, 0:T], ACT.Copy).then_inc(h_high, 1)
                if s is not None:
                    a(za[:, :, :], za[:, :, :], ACT.Ln, bias=1.0).then_inc(z_log, 1)

            att_step(Pos(0), None)
            with act.Fori(0, PAIRS - 1) as i:
                chain.enter(i, 2)
                att_step(Pos(1, i, 2), Pos(0, i, 2))
                att_step(Pos(2, i, 2), Pos(1, i, 2))
            chain.leave(PAIRS - 1)
            att_step(Pos(H - 1), Pos(H - 2))
            att_step(None, Pos(H - 1))

            norm_steps("o", 3, C_FFN + KT)
            ffn_tiles(1)
            norm_steps(("down", 1, 2), 4, C_FIN)
            u = Pos(AT["end"][1])
            full(act, u)
            for n in range(3):
                rows = 88 if n < 2 else 8
                last = a(tails[0:rows, n, :], slot(u)[0:rows, n * P:(n + 1) * P], ACT.Copy)
            last.then_inc(out_free[u.slot], 1)
            act.preload_act_table_set(LN_EXP)
            u = Pos(AT["end"][1] + 1)
            full(act, u)
            chain.link(a(factor[:, 0, :], slot(u)[:, 0:5], ACT.Ln, bias=eps[:, 0:1]))
            a(factor[:, 0, :], factor[:, 0, :], ACT.Exp, scale=-0.5).then_inc(factor_raw, 1)
            act.wait_ge(factor_ready, 1)
            act.wait_ge(y_full, 1)
            a(ytok[:, 0, :], Z[:, 0:D], ACT.Copy, scale=factor[:, 1, 0:1]).then_inc(y_copied[0], 1)
            for t in (2, 4):
                u = Pos(AT["end"][1] + t)
                w = P if t < 4 else TS
                full(act, u)
                a(ytok[0:w, t, :], slot(u)[0:w, :], ACT.Copy, scale=factor[0:w, 1, t:t + 1]).then_inc(out_free[u.slot], 1)

        @block.gpsimd
        def _(pool):
            g = nc.gpsimd
            chain = Chain(pool, chain_pool)
            pool.sem_inc(x_summed, 1)
            pool.sem_inc(rows_taken, 1)
            for tile, value in ((ident, 0.0), (ones, 1.0), (mean_d, 1.0 / D), (mean_v, 1.0 / DV), (neg_tri, -1.0)):
                g.memset(tile[:, :], value)
            chain.link(g.memset(eps[:, :], EPS))
            chain.link(g.affine_select(out=ident[:, :], in_=ident[:, :], compare_op=ALU.not_equal, fill=1.0, base=0,
                                       pattern=[[-1, P]], channel_multiplier=1))
            g.affine_select(out=neg_tri[:, :], in_=neg_tri[:, :], compare_op=ALU.is_ge, fill=0.0, base=0,
                            pattern=[[-1, P]], channel_multiplier=1).then_inc(consts_ready, 1)
            g.memset(gbias[:, :], 0.0).then_inc(pads_ready, 1)
            g.memset(kf[:, T:5 * P], 0.0)
            g.memset(vtok[:, 4, :], 0.0)
            g.memset(acol[:, :, :], 0.0)
            chain.link(g.memset(wcol[:, :, :], 0.0))
            g.memset(vtok[:, :, 2 * DV:2 * DV + 1], 1.0).then_inc(pads_ready, 1)

            def sum_squares(n):
                if n:
                    pool.wait_ge(ms_full, n)
                g.memset(ssq[:, :], 0.0).then_inc(x_summed, 1)

                def step(s):
                    pool.wait_ge(x_summed, Pos(9 * n + 2 + s.const, s.i, s.stride).at(0))
                    pool.wait_ge(x_square, Pos(KT * n + 1 + s.const, s.i, s.stride).at(0))
                    g.tensor_tensor(ssq[:, :], ssq[:, :], sq[:, s.const % 2, :], ALU.add).then_inc(x_summed, 1)

                stepwise(pool, KT, step)

            def mask(tile, keep, sample_at, done):
                diagonal = tile[:, :, 0:P]
                apart(pool)
                g.affine_select(out=diagonal, in_=diagonal, compare_op=keep, fill=0.0, base=0,
                                pattern=[[0, 4], [1, P]], channel_multiplier=-1)
                new = tile[:, 3, sample_at:sample_at + TS]
                g.affine_select(out=new, in_=new, compare_op=keep, fill=0.0, base=0, pattern=[[1, TS]],
                                channel_multiplier=-1).then_inc(done, 1)

            sum_squares(0)
            pool.wait_ge(gate_act, 6)
            pool.dma_start(rows_d[0:H, :], gneg[:, :]).then_inc(rows_stored, 16)
            pool.dma_start(rows_d[H:2 * H, :], gem[:, :]).then_inc(rows_stored, 16)
            pool.dma_start(wint_d[:, :], gwint[:, :]).then_inc(rows_stored, 16)
            pool.wait_ge(gate_dve, 11)
            pool.dma_start(O["p_m"][0, 0].unsqueeze(1), gm[:, 0:1]).then_inc(tail_stored, 16)
            pool.dma_start(O["s_m"][0, 0].unsqueeze(1), gm[:, 1:2]).then_inc(tail_stored, 16)
            with pool.Fori(0, PAIRS) as i:
                for e in range(2):
                    pool.wait_ge(dec_exp, i * 2 + (e + 1))
                    mask(dec, ALU.is_ge, P, dec_ready)

            def ffn_rows(layer):
                done = 0
                for t, nt in enumerate(THIRDS):
                    up = ("up", layer, t)

                    def tile(s):
                        f = Pos(layer * FT + done + s.const, s.i, s.stride)
                        pool.wait_ge(conv_ready, f.at(1))
                        apart(pool)
                        prev = par[:, C_PREV + 2 * FT * layer:C_PREV + 2 * FT * (layer + 1)].rearrange(
                            "p (r t) -> p r t", r=2)
                        tile_no = ds(s.at(done))
                        g.tensor_copy(ext[:, 2 + TP:4 + TP].unsqueeze(2), prev[:, :, tile_no]).then_inc(prev_ready, 1)
                        copied(pool, U(up, s, 2, 0))
                        apart(pool)
                        for grp, at in ((0, TP), (1, T + 2)):
                            last = g.tensor_copy(conv_rows[:, layer, grp, :, tile_no], ext[:, at:at + 2].unsqueeze(2))
                        last.then_inc(rows_taken, 1)

                    stepwise(pool, nt, tile)
                    done += nt

            sum_squares(1)
            ffn_rows(0)
            sum_squares(2)

            def att_step(s, c):
                if c is not None:
                    pool.wait_ge(prob_raw, c.at(1))
                    mask(prob, ALU.is_gt, P + 4 * TS, prob_ready)
                if s is not None:
                    pool.wait_ge(sp_raw, s.at(1))
                    mask(sp, ALU.is_gt, P + 4 * TS, sp_masked)

            att_steps(pool, att_step)
            sum_squares(3)
            ffn_rows(1)
            sum_squares(4)
            copied(pool, Pos(AT["end"][1]))
            for l in range(2):
                for grp, name in enumerate(("p_conv", "s_conv")):
                    pool.dma_start(O[name][l, 0].rearrange("r (t p) -> (r t) p", p=P),
                                   tails[grp * 44:(grp + 1) * 44, l, :]).then_inc(tail_stored, 16)
            for grp, name in enumerate(("p_n", "s_n")):
                pool.dma_start(O[name].rearrange("l b (i e) k -> (l b i) (e k)", e=2),
                               tails[grp * PAIRS:(grp + 1) * PAIRS, 2, :]).then_inc(tail_stored, 16)
            pool.wait_ge(tail_stored, 8 * 16)
            pool.wait_ge(state_stored, 16 + 2 * 16 * PAIRS)
            pool.wait_ge(k_stored, 16 + 2 * 16 * H)
            pool.wait_ge(v_stored, 16 + 2 * 16 * H)


_INS = ["x_prompt", "x_sample", "cache_k", "cache_v", "state_mlstm_c", "state_mlstm_n", "state_mlstm_m",
        "state_ffn_conv", "g_mix_norm", "w_mlstm_in", "b_mlstm_gates", "g_mlstm_out", "w_mlstm_out", "g_kv_norm", "w_kv",
        "w_sb_q", "w_sb_o", "g_ffn_norm", "w_ffn_up", "w_ffn_conv", "b_ffn_conv", "w_ffn_down", "g_final"]
_OUTS = [("y_p", (1, TP, D)), ("y_s", (1, TS, D)),
         ("p_c", (1, 1, H, DK, DV)), ("p_n", (1, 1, H, DK)), ("p_m", (1, 1, H)), ("p_conv", (2, 1, 2, FF)),
         ("p_k", (1, TP, H, DH)), ("p_v", (1, TP, H, DH)),
         ("s_c", (1, 1, H, DK, DV)), ("s_n", (1, 1, H, DK)), ("s_m", (1, 1, H)), ("s_conv", (2, 1, 2, FF)),
         ("s_k", (1, TS, H, DH)), ("s_v", (1, TS, H, DH))]


def kernel(**inputs):
    import numpy as _np
    import concourse.bacc as _bacc
    from concourse import mybir as _mybir
    from concourse.bass_utils import run_bass_kernel_spmd as _run

    nc = _bacc.Bacc("TRN2", target_bir_lowering=False, num_devices=1)
    arrays, ins, outs = {}, {}, {}
    for name in _INS:
        a = _np.ascontiguousarray(inputs[name])
        arrays[f"in_{name}"] = a
        ins[name] = nc.dram_tensor(f"in_{name}", a.shape, _mybir.dt.from_np(a.dtype), kind="ExternalInput").ap()
    for name, shape in _OUTS:
        outs[name] = nc.dram_tensor(f"out_{name}", shape, _mybir.dt.float32, kind="ExternalOutput").ap()
    trunk_kernel(nc, ins, outs)
    r = _run(nc, [arrays], core_ids=[0])
    return tuple(r.results[0][f"out_{name}"] for name, _ in _OUTS)
```
